# Optimizing a Trainium2 kernel written in Bass

```python
import jax
import jax.numpy as jnp
from jax import lax
import numpy as np

D_MODEL = 1024
BATCH = 1
SEQ = 256
DEPTH = 2
DEC_BATCH = 8
DEC_SEQ = 4
PAST_LEN = 1024
PAGE_SIZE = 128

HEAD_DIM = 64
ROT_DIM = HEAD_DIM // 4
ROPE_THETA = 500000.0
NORM_EPS = 1e-6
SCALE = HEAD_DIM ** -0.5
NEG_INF = -1e30
TINY = 1e-30
FORCE = 1e9

DIL_PATTERNS = ((128, 1), (512, 4), (2048, 16))
N_DIL = len(DIL_PATTERNS)
A_HEADS = 8
A_KV = 2
A_REP = A_HEADS // A_KV
A_WIDTH = A_HEADS * HEAD_DIM
A_QBLOCK = 128

B_WIDTH = D_MODEL // 2
CONV_W = 3

C_HEADS = 8
C_KV = 2
C_REP = C_HEADS // C_KV
C_WIDTH = C_HEADS * HEAD_DIM
CMP_LEN = 32
CMP_STRIDE = 16
CMP_HIDDEN = 2 * HEAD_DIM
SLC_BLOCK = 64
SLC_TOP = 16
WIN_C = 512
BAND = 128
C_QBLOCK = 64
N_NSA_ROWS = 4
N_BRANCH = 3

IN_SPLITS = (
    ('q_a', N_DIL * A_HEADS * HEAD_DIM),
    ('k_a', N_DIL * A_KV * HEAD_DIM),
    ('v_a', N_DIL * A_KV * HEAD_DIM),
    ('z_a', A_WIDTH),
    ('h_b', B_WIDTH),
    ('b_b', B_WIDTH),
    ('c_b', B_WIDTH),
    ('z_b', B_WIDTH),
    ('q_c', C_WIDTH),
    ('kv_c', 6 * C_KV * HEAD_DIM),
    ('g_c', 3 * C_HEADS),
    ('z_c', C_WIDTH),
    ('g_merge', N_BRANCH * D_MODEL),
)
IN_NAMES = tuple(n for n, _ in IN_SPLITS)
IN_OFFSETS = tuple(int(v) for v in np.cumsum([w for _, w in IN_SPLITS])[:-1])
N_IN = sum(w for _, w in IN_SPLITS)

kernel_name = 'hybrid_dilated_conv_nsa_decoder_step'

def rms_norm(x, g):
    xf = x.astype(jnp.float32)
    y = xf * lax.rsqrt(jnp.mean(xf * xf, axis=-1, keepdims=True) + NORM_EPS)
    return (y * g.astype(jnp.float32)).astype(x.dtype)

def rope(x, pos):
    half = ROT_DIM // 2
    inv = ROPE_THETA ** (-(2.0 / ROT_DIM) * jnp.arange(half, dtype=jnp.float32))
    ang = pos.astype(jnp.float32)[:, None] * inv[None, :]
    cos = jnp.cos(ang)[:, None, :]
    sin = jnp.sin(ang)[:, None, :]
    xf = x.astype(jnp.float32)
    x1 = xf[..., :half]
    x2 = xf[..., half:ROT_DIM]
    out = jnp.concatenate([x1 * cos - x2 * sin, x2 * cos + x1 * sin, xf[..., ROT_DIM:]], axis=-1)
    return out.astype(x.dtype)

def masked_softmax(s, valid, axis):
    s = jnp.where(valid, s, NEG_INF)
    m = jnp.max(s, axis=axis, keepdims=True)
    e = jnp.where(valid, jnp.exp(s - m), 0.0)
    den = jnp.maximum(jnp.sum(e, axis=axis, keepdims=True), TINY)
    return e / den, jnp.squeeze(m + jnp.log(den), axis=axis)

def project_layer(x, pos, norm_g, w_in):
    b, t, _ = x.shape
    h = rms_norm(x, norm_g) @ w_in
    pr = dict(zip(IN_NAMES, jnp.split(h, IN_OFFSETS, axis=-1)))
    q_a = rope(pr['q_a'].reshape(b, t, N_DIL * A_HEADS, HEAD_DIM), pos)
    k_a = rope(pr['k_a'].reshape(b, t, N_DIL * A_KV, HEAD_DIM), pos)
    q_c = rope(pr['q_c'].reshape(b, t, C_HEADS, HEAD_DIM), pos)
    kv_c = pr['kv_c'].reshape(b, t, 6, C_KV, HEAD_DIM)
    return dict(
        q_a=q_a.reshape(b, t, N_DIL, A_KV, A_REP, HEAD_DIM),
        k_a=k_a.reshape(b, t, N_DIL, A_KV, HEAD_DIM),
        v_a=pr['v_a'].reshape(b, t, N_DIL, A_KV, HEAD_DIM),
        u_b=pr['c_b'] * pr['h_b'],
        b_b=pr['b_b'],
        q_c=q_c.reshape(b, t, C_KV, C_REP, HEAD_DIM),
        k_cmp=kv_c[:, :, 0], v_cmp=kv_c[:, :, 1],
        k_slc=rope(kv_c[:, :, 2], pos), v_slc=kv_c[:, :, 3],
        k_win=rope(kv_c[:, :, 4], pos), v_win=kv_c[:, :, 5],
        g_c=pr['g_c'], z_a=pr['z_a'], z_b=pr['z_b'], z_c=pr['z_c'], g_merge=pr['g_merge'])

def dilated_attend(q, k_ext, v_ext, q_idx, dil, n_keys):
    idx = q_idx[:, None] - dil * jnp.arange(n_keys)[None, :]
    valid = idx >= 0
    idx = jnp.maximum(idx, 0)
    kg = k_ext[:, idx]
    vg = v_ext[:, idx]
    s = jnp.einsum('bqgrd,bqngd->bqgrn', q, kg).astype(jnp.float32) * SCALE
    p, lse = masked_softmax(s, valid[None, :, None, None, :], -1)
    o = jnp.einsum('bqgrn,bqngd->bqgrd', p.astype(vg.dtype), vg)
    return o, lse

def combine_dilated(q_a, ks, vs, q_idxs):
    outs, lses = [], []
    for gi, (win, dil) in enumerate(DIL_PATTERNS):
        o, lse = dilated_attend(q_a[:, :, gi], ks[gi], vs[gi], q_idxs[gi], dil, win // dil + 1)
        outs.append(o.astype(jnp.float32))
        lses.append(lse)
    w = jax.nn.softmax(jnp.stack(lses), axis=0)[..., None]
    return jnp.sum(w * jnp.stack(outs), axis=0).astype(q_a.dtype)

def dilated_prompt(q_a, k_a, v_a):
    b, s = q_a.shape[:2]
    nb = s // A_QBLOCK
    qb = q_a.reshape((b, nb, A_QBLOCK) + q_a.shape[2:]).swapaxes(0, 1)
    ks = [k_a[:, :, gi] for gi in range(N_DIL)]
    vs = [v_a[:, :, gi] for gi in range(N_DIL)]

    def block(args):
        q_blk, start = args
        q_idx = start + jnp.arange(A_QBLOCK)
        return combine_dilated(q_blk, ks, vs, [q_idx] * N_DIL)

    o = lax.map(block, (qb, jnp.arange(nb) * A_QBLOCK))
    return o.swapaxes(0, 1).reshape(b, s, A_WIDTH)

def short_conv(u_ext, w):
    return lax.conv_general_dilated(u_ext, w[:, None, :], window_strides=(1,), padding='VALID',
                                    dimension_numbers=('NWC', 'WIO', 'NWC'),
                                    feature_group_count=u_ext.shape[-1])

def compress(k_raw, v_raw, pe_k, pe_v, wk1, wk2, wv1, wv2):
    b, t, g, hd = k_raw.shape
    n_cmp = (t - CMP_LEN) // CMP_STRIDE + 1
    idx = CMP_STRIDE * jnp.arange(n_cmp)[:, None] + jnp.arange(CMP_LEN)[None, :]

    def phi(rows, pe, w1, w2):
        blk = rows[:, idx] + pe[None, None, :, None, :]
        flat = jnp.moveaxis(blk, 3, 2).reshape(b, n_cmp, g, CMP_LEN * hd)
        return jax.nn.silu(flat @ w1) @ w2

    end = CMP_STRIDE * jnp.arange(n_cmp) + CMP_LEN - 1
    kc = rope(phi(k_raw, pe_k, wk1, wk2), end)
    vc = phi(v_raw, pe_v, wv1, wv2)
    return kc, vc, end

def overlap_matrix(n_cmp, n_slc):
    cs = CMP_STRIDE * np.arange(n_cmp)[:, None]
    ss = SLC_BLOCK * np.arange(n_slc)[None, :]
    ov = np.clip(np.minimum(cs + CMP_LEN, ss + SLC_BLOCK) - np.maximum(cs, ss), 0, None)
    return jnp.asarray((ov / CMP_STRIDE).astype(np.float32))

def to_select_blocks(rows):
    b, t, g, hd = rows.shape
    n = -(-t // SLC_BLOCK)
    rows = jnp.pad(rows, ((0, 0), (0, n * SLC_BLOCK - t), (0, 0), (0, 0)))
    return rows.reshape(b, n, SLC_BLOCK, g, hd).transpose(0, 3, 1, 2, 4)

def nsa_core(q, q_pos, kc, vc, c_end, ks_blk, vs_blk, ov):
    b, _, g = q.shape[:3]
    s = jnp.einsum('bqgrd,bngd->bqgrn', q, kc).astype(jnp.float32) * SCALE
    valid_c = (c_end[None, :] <= q_pos[:, None])[None, :, None, None, :]
    p_cmp, _ = masked_softmax(s, valid_c, -1)
    o_cmp = jnp.einsum('bqgrn,bngd->bqgrd', p_cmp.astype(vc.dtype), vc)
    imp = jnp.einsum('bqgrn,nm->bqgm', p_cmp, ov)
    n_slc = ks_blk.shape[2]
    blk = jnp.arange(n_slc)[None, :]
    future = (blk * SLC_BLOCK > q_pos[:, None])[None, :, None, :]
    forced = ((blk == (q_pos // SLC_BLOCK)[:, None]) | (blk == 0))[None, :, None, :]
    imp = jnp.where(forced, FORCE, jnp.where(future, -FORCE, imp))
    _, sel = lax.top_k(imp, min(SLC_TOP, n_slc))
    bi = jnp.arange(b)[:, None, None, None]
    gi = jnp.arange(g)[None, None, :, None]
    kg = ks_blk[bi, gi, sel]
    vg = vs_blk[bi, gi, sel]
    kpos = sel[..., None] * SLC_BLOCK + jnp.arange(SLC_BLOCK)
    valid_s = (kpos <= q_pos[None, :, None, None, None])[:, :, :, None]
    s = jnp.einsum('bqgrd,bqgnkd->bqgrnk', q, kg).astype(jnp.float32) * SCALE
    p_slc, _ = masked_softmax(s, valid_s, (-2, -1))
    o_slc = jnp.einsum('bqgrnk,bqgnkd->bqgrd', p_slc.astype(vg.dtype), vg)
    return o_cmp, o_slc

def window_prompt(q, k, v):
    b, s_len, g, r, hd = q.shape
    nb = s_len // BAND
    nw = WIN_C // BAND + 1
    kp = jnp.pad(k, ((0, 0), (WIN_C, 0), (0, 0), (0, 0))).reshape(b, nb + nw - 1, BAND, g, hd)
    vp = jnp.pad(v, ((0, 0), (WIN_C, 0), (0, 0), (0, 0))).reshape(b, nb + nw - 1, BAND, g, hd)
    bidx = jnp.arange(nb)[:, None] + jnp.arange(nw)[None, :]
    kb = kp[:, bidx].reshape(b, nb, nw * BAND, g, hd)
    vb = vp[:, bidx].reshape(b, nb, nw * BAND, g, hd)
    qb = q.reshape(b, nb, BAND, g, r, hd)
    s = jnp.einsum('bnqgrd,bnkgd->bnqgrk', qb, kb).astype(jnp.float32) * SCALE
    qpos = jnp.arange(s_len).reshape(nb, BAND)
    kpos = (jnp.arange(nb) * BAND - WIN_C)[:, None] + jnp.arange(nw * BAND)[None, :]
    dist = qpos[:, :, None] - kpos[:, None, :]
    valid = ((dist >= 0) & (dist <= WIN_C))[None, :, :, None, None, :]
    p, _ = masked_softmax(s, valid, -1)
    o = jnp.einsum('bnqgrk,bnkgd->bnqgrd', p.astype(vb.dtype), vb)
    return o.reshape(b, s_len, g, r, hd)

def window_sample(q, k_ext, v_ext, buf_len):
    n_q = q.shape[1]
    qidx = buf_len + jnp.arange(n_q)
    dist = qidx[:, None] - jnp.arange(k_ext.shape[1])[None, :]
    valid = ((dist >= 0) & (dist <= WIN_C))[None, :, None, None, :]
    s = jnp.einsum('bqgrd,bkgd->bqgrk', q, k_ext).astype(jnp.float32) * SCALE
    p, _ = masked_softmax(s, valid, -1)
    return jnp.einsum('bqgrk,bkgd->bqgrd', p.astype(v_ext.dtype), v_ext)

def nsa_gate(g_c, o_cmp, o_slc, o_win):
    b, t = g_c.shape[:2]
    g = jax.nn.sigmoid(g_c).reshape(b, t, 3, C_KV, C_REP, 1)
    o = g[:, :, 0] * o_cmp + g[:, :, 1] * o_slc + g[:, :, 2] * o_win
    return o.reshape(b, t, C_WIDTH)

def merge_branches(p, o_a, o_b, o_c, w_up_a, w_up_b, w_up_c, w_out):
    b, t = o_a.shape[:2]
    gates = jax.nn.sigmoid(p['g_merge']).reshape(b, t, N_BRANCH, D_MODEL)
    m = (gates[:, :, 0] * ((o_a * jax.nn.silu(p['z_a'])) @ w_up_a)
         + gates[:, :, 1] * ((o_b * jax.nn.silu(p['z_b'])) @ w_up_b)
         + gates[:, :, 2] * ((o_c * jax.nn.silu(p['z_c'])) @ w_up_c))
    return (m @ w_out).astype(o_a.dtype)

def layer_prompt(x, lw):
    norm_g, w_in, conv_w, pe_k, pe_v, wk1, wk2, wv1, wv2, w_up_a, w_up_b, w_up_c, w_out = lw
    b, s, _ = x.shape
    pos = jnp.arange(s)
    p = project_layer(x, pos, norm_g, w_in)
    o_a = dilated_prompt(p['q_a'], p['k_a'], p['v_a'])
    dil_states = [jnp.stack([p['k_a'][:, s - min(win, s):, gi], p['v_a'][:, s - min(win, s):, gi]], axis=2)
                  for gi, (win, _) in enumerate(DIL_PATTERNS)]
    u = p['u_b']
    o_b = p['b_b'] * short_conv(jnp.pad(u, ((0, 0), (CONV_W - 1, 0), (0, 0))), conv_w)
    conv_state = u[:, s - (CONV_W - 1):]
    kc, vc, c_end = compress(p['k_cmp'], p['v_cmp'], pe_k, pe_v, wk1, wk2, wv1, wv2)
    ks_blk = to_select_blocks(p['k_slc'])
    vs_blk = to_select_blocks(p['v_slc'])
    ov = overlap_matrix(kc.shape[1], ks_blk.shape[2])
    nb = s // C_QBLOCK
    qb = p['q_c'].reshape(b, nb, C_QBLOCK, C_KV, C_REP, HEAD_DIM).swapaxes(0, 1)

    def nsa_block(args):
        q_blk, start = args
        return nsa_core(q_blk, start + jnp.arange(C_QBLOCK), kc, vc, c_end, ks_blk, vs_blk, ov)

    o_cmp, o_slc = lax.map(nsa_block, (qb, jnp.arange(nb) * C_QBLOCK))
    o_cmp = o_cmp.swapaxes(0, 1).reshape(b, s, C_KV, C_REP, HEAD_DIM)
    o_slc = o_slc.swapaxes(0, 1).reshape(b, s, C_KV, C_REP, HEAD_DIM)
    o_win = window_prompt(p['q_c'], p['k_win'], p['v_win'])
    o_c = nsa_gate(p['g_c'], o_cmp, o_slc, o_win)
    lw_len = min(WIN_C, s)
    win_state = jnp.stack([p['k_win'][:, s - lw_len:], p['v_win'][:, s - lw_len:]], axis=2)
    nsa_rows = jnp.stack([p['k_cmp'], p['v_cmp'], p['k_slc'], p['v_slc']], axis=2)
    y = merge_branches(p, o_a, o_b, o_c, w_up_a, w_up_b, w_up_c, w_out)
    return x + y, (dil_states[0], dil_states[1], dil_states[2], win_state, conv_state, nsa_rows)

def layer_sample(x, dil_caches, win_cache, conv_cache, nsa_pool, page_table, lw):
    norm_g, w_in, conv_w, pe_k, pe_v, wk1, wk2, wv1, wv2, w_up_a, w_up_b, w_up_c, w_out = lw
    b, n_q, _ = x.shape
    past = page_table.shape[1] * PAGE_SIZE
    pos = past + jnp.arange(n_q)
    p = project_layer(x, pos, norm_g, w_in)
    ks, vs, qidx, dil_new = [], [], [], []
    for gi in range(N_DIL):
        buf = dil_caches[gi]
        buf_len = buf.shape[1]
        k_ext = jnp.concatenate([buf[:, :, 0], p['k_a'][:, :, gi]], axis=1)
        v_ext = jnp.concatenate([buf[:, :, 1], p['v_a'][:, :, gi]], axis=1)
        ks.append(k_ext)
        vs.append(v_ext)
        qidx.append(buf_len + jnp.arange(n_q))
        dil_new.append(jnp.stack([k_ext[:, n_q:], v_ext[:, n_q:]], axis=2))
    o_a = combine_dilated(p['q_a'], ks, vs, qidx).reshape(b, n_q, A_WIDTH)
    u_ext = jnp.concatenate([conv_cache, p['u_b']], axis=1)
    o_b = p['b_b'] * short_conv(u_ext, conv_w)
    conv_new = u_ext[:, n_q:]
    hist = nsa_pool[page_table].reshape(b, past, N_NSA_ROWS, C_KV, HEAD_DIM)
    new_rows = jnp.stack([p['k_cmp'], p['v_cmp'], p['k_slc'], p['v_slc']], axis=2)
    rows = jnp.concatenate([hist, new_rows], axis=1)
    kc, vc, c_end = compress(rows[:, :, 0], rows[:, :, 1], pe_k, pe_v, wk1, wk2, wv1, wv2)
    ks_blk = to_select_blocks(rows[:, :, 2])
    vs_blk = to_select_blocks(rows[:, :, 3])
    ov = overlap_matrix(kc.shape[1], ks_blk.shape[2])
    o_cmp, o_slc = nsa_core(p['q_c'], pos, kc, vc, c_end, ks_blk, vs_blk, ov)
    buf_len = win_cache.shape[1]
    kw_ext = jnp.concatenate([win_cache[:, :, 0], p['k_win']], axis=1)
    vw_ext = jnp.concatenate([win_cache[:, :, 1], p['v_win']], axis=1)
    o_win = window_sample(p['q_c'], kw_ext, vw_ext, buf_len)
    win_new = jnp.stack([kw_ext[:, n_q:], vw_ext[:, n_q:]], axis=2)
    o_c = nsa_gate(p['g_c'], o_cmp, o_slc, o_win)
    y = merge_branches(p, o_a, o_b, o_c, w_up_a, w_up_b, w_up_c, w_out)
    return x + y, (dil_new[0], dil_new[1], dil_new[2], win_new, conv_new, new_rows)

def setup_inputs(seed: int = 0) -> dict:
    key = jax.random.key(seed)
    ks = jax.random.split(key, 24)
    f32 = jnp.float32

    def nrm(k, shape, scale=1.0):
        return scale * jax.random.normal(k, shape, f32)

    n_pages = PAST_LEN // PAGE_SIZE
    n_used = DEC_BATCH * n_pages
    n_phys = n_used + n_used // 4
    page_table = jax.random.permutation(ks[8], n_phys)[:n_used].reshape(DEC_BATCH, n_pages).astype(jnp.int32)
    kv_a = (2, A_KV, HEAD_DIM)
    return {
        'x_prompt': nrm(ks[0], (BATCH, SEQ, D_MODEL)),
        'x_sample': nrm(ks[1], (DEC_BATCH, DEC_SEQ, D_MODEL)),
        'cache_dil1_kv': nrm(ks[2], (DEPTH, DEC_BATCH, min(DIL_PATTERNS[0][0], PAST_LEN)) + kv_a),
        'cache_dil4_kv': nrm(ks[3], (DEPTH, DEC_BATCH, min(DIL_PATTERNS[1][0], PAST_LEN)) + kv_a),
        'cache_dil16_kv': nrm(ks[4], (DEPTH, DEC_BATCH, min(DIL_PATTERNS[2][0], PAST_LEN)) + kv_a),
        'cache_win_kv': nrm(ks[5], (DEPTH, DEC_BATCH, min(WIN_C, PAST_LEN), 2, C_KV, HEAD_DIM)),
        'state_conv': nrm(ks[6], (DEPTH, DEC_BATCH, CONV_W - 1, B_WIDTH)),
        'cache_nsa_kv': nrm(ks[7], (DEPTH, n_phys, PAGE_SIZE, N_NSA_ROWS, C_KV, HEAD_DIM)),
        'page_table': page_table,
        'norm_g': 1.0 + nrm(ks[9], (DEPTH, D_MODEL), 0.02),
        'w_in': nrm(ks[10], (DEPTH, D_MODEL, N_IN), D_MODEL ** -0.5),
        'conv_w': nrm(ks[11], (DEPTH, CONV_W, B_WIDTH), CONV_W ** -0.5),
        'cmp_pe_k': nrm(ks[12], (DEPTH, CMP_LEN, HEAD_DIM), 0.1),
        'cmp_pe_v': nrm(ks[13], (DEPTH, CMP_LEN, HEAD_DIM), 0.1),
        'cmp_wk1': nrm(ks[14], (DEPTH, CMP_LEN * HEAD_DIM, CMP_HIDDEN), (CMP_LEN * HEAD_DIM) ** -0.5),
        'cmp_wk2': nrm(ks[15], (DEPTH, CMP_HIDDEN, HEAD_DIM), CMP_HIDDEN ** -0.5),
        'cmp_wv1': nrm(ks[16], (DEPTH, CMP_LEN * HEAD_DIM, CMP_HIDDEN), (CMP_LEN * HEAD_DIM) ** -0.5),
        'cmp_wv2': nrm(ks[17], (DEPTH, CMP_HIDDEN, HEAD_DIM), CMP_HIDDEN ** -0.5),
        'w_up_a': nrm(ks[18], (DEPTH, A_WIDTH, D_MODEL), A_WIDTH ** -0.5),
        'w_up_b': nrm(ks[19], (DEPTH, B_WIDTH, D_MODEL), B_WIDTH ** -0.5),
        'w_up_c': nrm(ks[20], (DEPTH, C_WIDTH, D_MODEL), C_WIDTH ** -0.5),
        'w_out': nrm(ks[21], (DEPTH, D_MODEL, D_MODEL), D_MODEL ** -0.5),
        'final_norm_g': 1.0 + nrm(ks[22], (D_MODEL,), 0.02),
    }

def reference(x_prompt, x_sample, cache_dil1_kv, cache_dil4_kv, cache_dil16_kv, cache_win_kv,
              state_conv, cache_nsa_kv, page_table, norm_g, w_in, conv_w, cmp_pe_k, cmp_pe_v,
              cmp_wk1, cmp_wk2, cmp_wv1, cmp_wv2, w_up_a, w_up_b, w_up_c, w_out, final_norm_g):
    xp = x_prompt
    xs = x_sample
    st_p = [[] for _ in range(6)]
    st_s = [[] for _ in range(6)]
    for l in range(DEPTH):
        lw = (norm_g[l], w_in[l], conv_w[l], cmp_pe_k[l], cmp_pe_v[l], cmp_wk1[l], cmp_wk2[l],
              cmp_wv1[l], cmp_wv2[l], w_up_a[l], w_up_b[l], w_up_c[l], w_out[l])
        xp, new_p = layer_prompt(xp, lw)
        xs, new_s = layer_sample(xs, (cache_dil1_kv[l], cache_dil4_kv[l], cache_dil16_kv[l]),
                                 cache_win_kv[l], state_conv[l], cache_nsa_kv[l], page_table, lw)
        for i in range(6):
            st_p[i].append(new_p[i])
            st_s[i].append(new_s[i])
    y_prompt = rms_norm(xp, final_norm_g)
    y_sample = rms_norm(xs, final_norm_g)
    new_dil1_prompt = jnp.stack(st_p[0])
    new_dil1_sample = jnp.stack(st_s[0])
    new_dil4_prompt = jnp.stack(st_p[1])
    new_dil4_sample = jnp.stack(st_s[1])
    new_dil16_prompt = jnp.stack(st_p[2])
    new_dil16_sample = jnp.stack(st_s[2])
    new_win_prompt = jnp.stack(st_p[3])
    new_win_sample = jnp.stack(st_s[3])
    new_conv_prompt = jnp.stack(st_p[4])
    new_conv_sample = jnp.stack(st_s[4])
    new_nsa_rows_prompt = jnp.stack(st_p[5])
    new_nsa_rows_sample = jnp.stack(st_s[5])
    return (y_prompt, y_sample, new_dil1_prompt, new_dil1_sample, new_dil4_prompt, new_dil4_sample,
            new_dil16_prompt, new_dil16_sample, new_win_prompt, new_win_sample,
            new_conv_prompt, new_conv_sample, new_nsa_rows_prompt, new_nsa_rows_sample)


_drawn_inputs = setup_inputs


def setup_inputs(seed=0):
    import zlib

    import numpy as np

    out = dict(_drawn_inputs(seed))
    spreads = {}
    factors = {'cmp_pe_k': 38.765, 'cmp_pe_v': 4.865, 'final_norm_g': 7.964}
    for name, (base, spread) in spreads.items():
        noise = np.random.default_rng([zlib.crc32(name.encode()), seed]).standard_normal(out[name].shape)
        drawn = base * np.exp(spread * noise) if base else spread * noise
        out[name] = jnp.asarray(drawn.astype(out[name].dtype))
    for name, factor in factors.items():
        out[name] = (out[name] * factor).astype(out[name].dtype)
    return out
```

```python
import concourse.bass as bass
from concourse import mybir
from contextlib import ExitStack
import numpy as np

FP32 = mybir.dt.float32
BF16 = mybir.dt.bfloat16
I32 = mybir.dt.int32
ALU = mybir.AluOpType
ACT = mybir.ActivationFunctionType
AX = mybir.AxisListType

P = 128
D_MODEL = 1024
KT = D_MODEL // P
DEPTH = 2
SEQ = 256
REQ = 8
NEW = 4
NS = REQ * NEW
T = SEQ + NS
PROMPT_STORES = 9
PAST = 1024
PAGE = 128
PAGES = PAST // PAGE
HD = 64
HALF_ROT = 8
THETA = 500000.0
KV = 2
REP = 4
HEADS = KV * REP
EPS = 1e-6
NEG = -1e30
SCALE = HD ** -0.5
WIDTH = 512
WT = WIDTH // P
CMP_LEN, CMP_STRIDE, SLC = 32, 16, 64
NCP = (SEQ - CMP_LEN) // CMP_STRIDE + 1
NCS = (PAST - CMP_LEN) // CMP_STRIDE + 1
NBLK = PAST // SLC
NPH = (REQ * PAGES * 5) // 4
D1, D4, D16, WIN = 128, 512, 1024, 512
K16 = D16 // 16 * NEW
HB = 2
RB = REQ // HB
PARTS = (P, P, NS)
TOK0 = (0, P, 2 * P)
G_TOK = 7
KVC = 3 * 512
PAIRS = ("d1", "d4", "d16", "win", "cmp", "slc")
KCOL = {n: 256 * i for i, n in enumerate(PAIRS)}
VCOL = {n: 256 * i + P for i, n in enumerate(PAIRS)}
KTYPE = {"d1": 0, "d4": 1, "d16": 2, "win": 3, "slc": 4}
VCOL["slc"], KCOL["slc"] = 4 * 256 + 384, 4 * 256 + 256
A_TYPES = ("d1", "d4", "d16")
MIX = P + K16 + 3 * NS
S_MIX, S_WIN = D4, D4 + MIX
S_WNEW = S_WIN + WIN
S_SNEW = S_WNEW + NS
S_SLC = S_SNEW + NS
S_CMP = S_SLC + PAST
S_ALL = S_CMP + 64
MASK_COLS = dict(a=3 * 256, c=256, cmp0=256, cmp1=256, sd4=D4, smix0=MIX, smix1=MIX, swin=WIN,
                 smisc0=P, smisc1=P)


def mask_at():
    at, out = 0, {}
    for name, n in MASK_COLS.items():
        out[name] = (at, at + n)
        at += n
    return out, at


class Signal:

    def __init__(self, nc, name, keys, by=1):
        self.sem, self.by, self.name = nc.alloc_semaphore(name), by, name
        self.place = {k: i + 1 for i, k in enumerate(keys)}
        assert len(self.place) == len(keys), name
        self.raised = 0

    def inc(self, key):
        self.raised += 1
        assert self.place[key] == self.raised, (self.name, key)
        return self.sem, self.by

    def at(self, key):
        return self.sem, self.by * self.place[key]


class Ring:

    def __init__(self, nc, name, keys, n, by=1, parts=1, free=True):
        self.n, self.by, self.parts, self.keys = n, by, parts, list(keys)
        self.place = {k: i for i, k in enumerate(keys)}
        assert len(self.place) == len(self.keys), name
        self.full = [nc.alloc_semaphore(f"{name}{b}_full") for b in range(n)]
        self.free = [nc.alloc_semaphore(f"{name}{b}_free") for b in range(n)] if free else None
        self.released = set()

    def buf(self, key):
        return self.place[key] % self.n

    def fill(self, key):
        return self.full[self.buf(key)], self.by

    def is_full(self, key):
        return self.full[self.buf(key)], self.by * self.parts * (self.place[key] // self.n + 1)

    def release(self, key):
        assert key not in self.released, key
        self.released.add(key)
        return self.free[self.buf(key)], 1

    def is_free(self, key):
        return self.free[self.buf(key)], self.place[key] // self.n

    def is_used(self, key):
        return self.free[self.buf(key)], self.place[key] // self.n + 1

    def before(self, key):
        i = self.place[key] - self.n
        return self.keys[i] if i >= 0 else None


def wait(eng, sem_value):
    if sem_value[1] > 0:
        eng.wait_ge(*sem_value)



def prompt_units():
    units = []
    for qt in range(2):
        units += [("A", qt, h) for h in range(HEADS)]
    for qt in range(2):
        units += [("C", qt, h) for h in range(HEADS)]
    return units


FEATS = [("za", kt) for kt in range(WT)] + [(kind, kt) for kt in range(WT) for kind in ("h", "c", "b", "zb")] + \
        [("zc", kt) for kt in range(WT)]


def unit_banks(u):
    br, qt, _ = u
    n = P * (qt + 1)
    if br == "A":
        return [(0, 3 * P)] if qt == 0 else [(0, 512), (512, 256)]
    return [(0, 2 * n)]


def unit_chunks(u):
    br, qt, _ = u
    return [(t, kb) for t in (A_TYPES if br == "A" else ("win", "slc")) for kb in range(qt + 1)]


def steps():
    out = []
    for tt in range(3):
        out += [("xn", tt)]
    toks = [(g, tt) for g in range(G_TOK) for tt in range(3)]
    for i, k in enumerate(toks):
        out.append(("tok",) + k)
        if i >= 2:
            out.append(("turn",) + toks[i - 2])
    out += [("gc", tt) for tt in range(3)]
    out += [("turn",) + k for k in toks[-2:]]
    units, feats = prompt_units(), list(FEATS)
    for i in range(len(units) + 2):
        if feats:
            out.append(("feat",) + feats.pop(0))
        if i < len(units):
            out.append(("score", units[i]))
        if 1 <= i <= len(units):
            out.append(("exp", units[i - 1]))
            out.append(("pturn", units[i - 1]))
        if i >= 2:
            u = units[i - 2]
            out.append(("pv", u))
            if u[2] == HEADS - 1:
                out.append(("out", u[0], u[1]))
                if u[0] == "A":
                    out.append(("gateA", u[1]))
    out += [("pe", 0), ("pe", 1), ("ghid", 0), ("ghid", 1), ("gkc",), ("gvc",), ("gkt",), ("gates",)]
    for qt in range(2):
        out += [("cscore", qt), ("cturn", qt), ("cpv", qt), ("gateC", qt)]
    for hb in range(HB):
        out += [("hid", hb, 0), ("sscore", hb, "d4"), ("hid", hb, 1), ("sscore", hb, "mix"), ("kc", hb), ("vc", hb),
                ("sexp", hb, "A"), ("kct", hb), ("sscore", hb, "win"), ("sscore", hb, "misc"),
                ("sexp", hb, "cmp"), ("sexp", hb, "win"),
                ("sscore", hb, "slc0"), ("sscore", hb, "slc1"),
                ("sturn", hb, "d4"), ("cmpt", hb), ("spv", hb, "d4"), ("sturn", hb, "mix"), ("imp", hb),
                ("spv", hb, "mix"), ("sturn", hb, "anew"), ("impsum", hb), ("spv", hb, "anew"), ("drop", hb),
                ("sexp", hb, "slc"), ("sturn", hb, "win"), ("soA", hb), ("spv", hb, "win"),
                ("sturn", hb, "cnew"), ("spv", hb, "cnew"), ("sgateA", hb),
                ("sturn", hb, "slc0"), ("spv", hb, "slc0"), ("sturn", hb, "slc1"), ("spv", hb, "slc1"),
                ("soC", hb), ("sgateC", hb)]
    for fh in range(2):
        for i in range(3):
            for q in range(4):
                out += [("gate", fh, i, q), ("up", fh, i, q)]
    out += [("down", nh, tt) for nh in range(2) for tt in range(3)]
    return out


def trunk_program(nc, a, o):
    STEPS = steps()
    UNITS = prompt_units()
    MASK, NMASK = mask_at()
    of = lambda *kinds: [s for s in STEPS if s[0] in kinds]

    def sb(name, shape, dt=FP32):
        return nc.alloc_sbuf_tensor(name, shape, dt)

    x = sb("x", [P, 3, D_MODEL])
    ident = sb("ident", [P, P])
    identb = sb("identb", [P, P], BF16)
    masks = sb("masks", [P, NMASK], BF16)
    rot_c = sb("rot_c", [P, 3, 16])
    rot_s = sb("rot_s", [P, 3, 16])
    blk_c = sb("blk_c", [64, 16])
    blk_s = sb("blk_s", [64, 16])
    overlap = sb("overlap", [64, NBLK + 1])
    same_q = sb("same_q", [P, P])
    pick = sb("pick", [NS, HB, P])
    row_head = sb("row_head", [P, HEADS])
    row_kv = sb("row_kv", [P, KV])
    n_pads = sb("n_pads", [P, 2])
    row_some = sb("row_some", [P, 1])
    number = sb("number", [P, NBLK])
    page_no = sb("page_no", [1, REQ * PAGES], I32)
    xnT = sb("xnT", [P, KT, T])
    gT = sb("gT", [P, KT])
    big = [sb(f"big{i}", [P, 4096]) for i in range(3)]
    paged = [sb(f"paged{i}", [P, 2 * PAGES * 256]) for i in range(2)]
    kvp = sb("kvp", [P, 3, KVC])
    old = kvp[:, 0:2, :].rearrange("p t n -> p (t n)")
    hid = [old[:, 512 * i:512 * (i + 1)] for i in range(2)]
    hidp, hidt = old[:, 1024:1536], old[:, 1536:2048]
    hidb = old[:, 2048:2048 + 516]
    kcT = old[:, 2564:2820].rearrange("p (b n) -> p b n", b=RB)
    w_gc = sb("w_gc", [P, KT, 24])
    gct = sb("gct", [P, 3, 24])
    oT = [sb(f"oT_{m}", [P, WT, T]) for m in "abc"]
    long = sb("long", [P, 4096])
    qTA = long[:, 0:3 * REP * SEQ].rearrange("p (t r n) -> p t r n", t=3, r=REP)
    w1 = long[:, :].rearrange("p (k l n) -> p k l n", k=2, l=16)
    mT = long[:, 0:KT * T].rearrange("p (k n) -> p k n", k=KT)
    qTC = sb("qTC", [P, REP, SEQ])
    kT = sb("kT", [P, 5, SEQ])
    ktf = kT[:, :, :].rearrange("p t n -> p (t n)")
    kcs, vcs = ktf[0:64, 0:WIDTH], ktf[0:64, WIDTH:2 * WIDTH]
    kTn = sb("kTn", [P, 5, NS])
    cT = sb("cT", [P, 2, KV, P])
    qblk = sb("qblk", [P, 4, HB, P])
    short = sb("short", [P, S_ALL + WIDTH])
    xn = short[:, 0:3 * D_MODEL].rearrange("p (t n) -> p t n", t=3)
    proj = short[:, 0:2048].rearrange("p (s n) -> p s n", s=4)
    prob = short[:, 0:1536].rearrange("p (s n) -> p s n", s=2)
    srow = short[:, 0:S_ALL]
    o_tmp = short[:, S_ALL:S_ALL + WIDTH]
    PT = sb("PT", [P, 2, 768])
    o_sb = sb("o_sb", [P, 2, WIDTH])
    n_ext = SEQ + 2 + REQ * 6
    hsb, uext = long[:, 3072:3072 + T], long[:, 3360:3360 + n_ext]
    ysb = long[:, 3666:3666 + n_ext]
    ustate = sb("ustate", [P, WT, 2 + REQ * 2])
    ustart = sb("ustart", [P, WT, REQ, 2])
    conv_w = sb("conv_w", [P, WT, 3])
    tanh = sb("tanh", [P, 2, T])
    prod = sb("prod", [P, T])
    rtmp = sb("rtmp", [P, 2, 8, 16])
    w2 = sb("w2", [P, 2, HD])
    pe_c = sb("pe_c", [P, 2, 16])
    pe_b = sb("pe_b", [P, 2])
    kcp = sb("kcp", [NCP, P])
    kcz = sb("kcz", [P, KV, 32])
    vcz = prob[:, 1, 0:512]
    PTc = sb("PTc", [64, P])
    small = sb("small", [P, 256])

    def col(at, n=1):
        return small[:, at:at + n]

    ss, rn = col(0, 3), col(3, 3)
    mx = [col(8 + 4 * s, 4) for s in range(2)]
    nmx = [col(16 + 4 * s, 4) for s in range(2)]
    den = {("A", q): col(24 + 8 * q, 8) for q in range(2)} | {("C", q): col(40 + 16 * q, 16) for q in range(2)}
    cmx, cden, crec = col(72, 8), col(80, 8), col(88, 8)
    rec = col(96, 16)
    smx, sden, srec = col(112, 4), col(116, 4), col(120, 4)
    sg = [col(124 + 4 * h, 3) for h in range(HB)]
    scoef = col(132, 8)
    impt, impv = col(140, 17), col(157, 16)
    least, which, hitv, dropv = col(173), col(174), col(176, 16), col(192, 16)
    sgt = col(208, 24)
    wneg = [col(232 + 8 * q, 8) for q in range(2)]

    ps = [nc.alloc_psum_tensor(f"bank{i}", [P, 512], FP32) for i in range(8)]
    pj_keys = []
    tr_keys, sc_keys, o_keys, pt_keys = [], [], [], []
    for s in STEPS:
        k = s[0]
        if k in ("tok", "gc", "feat", "pe", "gkc", "gvc", "kc", "vc", "gate", "up", "down", "imp", "impsum"):
            pj_keys.append(s)
        if k == "gates":
            pj_keys += [("gates", 0), ("gates", 1)]
        if k == "ghid":
            pj_keys.append(s)
        if k == "hid":
            pj_keys += [s + (0,), s + (1,)]
        if k == "xn":
            tr_keys += [s + (0,), s + (1,)]
        if k in ("turn", "gkt", "cturn", "kct", "cmpt", "sturn", "gateA", "gateC", "sgateA", "sgateC"):
            tr_keys.append(s)
        if k == "pturn":
            tr_keys += [s + (j,) for j in range(-(-len(unit_chunks(s[1])) // 4))]
        if k == "score":
            sc_keys += [s + (j,) for j in range(len(unit_banks(s[1])))]
        if k in ("cscore", "sscore"):
            sc_keys.append(s)
        if k == "pv" and s[1][2] == 0:
            o_keys += [("o", "A", s[1][1])] if s[1][0] == "A" else [("o", "W", s[1][1]), ("o", "S", s[1][1])]
        if k == "cpv":
            o_keys.append(("o", "c", s[1]))
        if k == "spv" and s[2] in ("d4", "win"):
            o_keys.append(("o", "sA" if s[2] == "d4" else "sC", s[1]))
        if k in ("pturn",):
            pt_keys.append(s)
        if k in ("cturn", "sturn"):
            pt_keys.append(s)
    PJ = Ring(nc, "proj_bank", pj_keys, 2)
    TR = Ring(nc, "turn_bank", tr_keys, 2)
    SC = Ring(nc, "score_bank", sc_keys, 2)
    O = Ring(nc, "out_bank", o_keys, 2)
    PTR = Ring(nc, "probT", pt_keys, 2, free=False)
    pj = lambda k: ps[PJ.buf(k)]
    tr = lambda k: ps[2 + TR.buf(k)]
    sc = lambda k: ps[4 + SC.buf(k)]
    ob = lambda k: ps[6 + O.buf(k)]
    ptb = lambda k: PT[:, PTR.buf(k), :]

    big_keys = [("tok", g) for g in range(G_TOK)] + [("feat", i) for i in range(6)]
    for hb in range(HB):
        big_keys += [("kA", hb), ("win", hb), ("vA", hb)]
    for fh in range(2):
        for i in range(3):
            big_keys += [("gate", fh, i), ("up", fh, i)]
    big_keys += [("down", nh) for nh in range(2)]
    BIG = Ring(nc, "big", big_keys, 3, by=16, free=False)
    bigb = lambda k: big[BIG.buf(k)]
    page_keys = [(kind, hb, bp) for hb in range(HB) for kind in ("cmp", "slc") for bp in range(2)]
    PG = Ring(nc, "pages", page_keys, 2, by=16, parts=2 * PAGES, free=False)
    pgb = lambda k: paged[PG.buf(k)][:, :].rearrange("p (b g k n) -> p b g k n", b=2, g=PAGES, k=2)

    sig = lambda name, keys, by=1: Signal(nc, name, keys, by)
    layer_in = sig("layer_in", ["all"], 16 * 6)
    w1_in = sig("w1_in", ["all"], 16)
    squares = sig("squares_done", list(range(3)))
    mean = sig("mean_done", list(range(3)))
    root = sig("root_done", list(range(3)))
    normed = sig("normed", list(range(3)))
    roped = sig("roped", [s[1:] for s in of("tok")])
    tanh_done = sig("tanh_done", [s for s in of("feat") if s[1][0] == "z"])
    u_state = sig("conv_state_ready", ["all"])
    maxed = sig("max_ready", UNITS)
    expd = sig("probs_ready", UNITS)
    c_normed = sig("mixer_c_normed", [("W", 0), ("W", 1), ("c", 0), ("c", 1)])
    hid_tanh = sig("hidden_tanh", of("ghid", "hid"))
    hid_done = sig("hidden_ready", of("ghid", "hid"))
    pad_exp = sig("pad_weight_ready", [0, 1])
    zeroed = sig("blocks_zeroed", ["all"])
    kc_done = sig("kc_roped", ["p", 0, 1])
    cexpd = sig("cmp_probs_ready", [0, 1])
    smaxed = sig("row_max_ready", [s[1:] for s in of("sexp")])
    sexpd = sig("row_probs_ready", [s[1:] for s in of("sexp")])
    cnormed = sig("cmp_probs_normed", [0, 1])
    so_done = sig("rows_out_ready", of("soA", "soC"))
    merged = sig("merged", [s[1:] for s in of("up") if s[2]])
    pv_done = sig("values_weighted", [s for s in of("pv", "spv")
                                      if not (s[0] == "pv" and s[1][2] == HEADS - 1) and s[2:] not in (("anew",), ("slc1",))])
    dchain = nc.alloc_semaphore("dve_link")
    stored, stored_new = nc.alloc_semaphore("prompt_stored"), nc.alloc_semaphore("new_stored")
    copied = nc.alloc_semaphore("caches_copied")
    per_layer = range(PJ.full[0].num, copied.num + 1)
    const_in = nc.alloc_semaphore("constants_in")
    set_up = nc.alloc_semaphore("set_up")
    y_squares, y_mean, y_root, y_link, y_ready, y_out = [
        nc.alloc_semaphore(n) for n in ("y_squares", "y_mean", "y_root", "y_link", "y_ready", "y_out")]

    tanhs = [s for s in STEPS if s[0] == "gate" or (s[0] == "feat" and s[1][0] == "z")]
    tanh_slot = {s: i % 2 for i, s in enumerate(tanhs)}

    def turned(g, tt):
        return TR.is_used(("turn", g, tt))

    def tanh_free(s):
        i = tanhs.index(s)
        if i < 2:
            return None
        before = tanhs[i - 2]
        return PJ.is_used(before if before[0] == "feat" else ("up",) + before[1:])

    def n_turns(u):
        return -(-len(unit_chunks(u)) // 4)

    def pt_full(key):
        return TR.is_used(key + (n_turns(key[1]) - 1,) if key[0] == "pturn" else key)

    def pt_used(key):
        if key[0] == "cturn":
            return O.is_full(("o", "c", key[1]))
        if key[0] == "pturn":
            br, qt, h = key[1]
            if h == HEADS - 1:
                return O.is_full(("o", "A" if br == "A" else "S", qt))
            return pv_done.at(("pv", key[1]))
        if key[2] in ("anew", "slc1"):
            return O.is_full(("o", "sA" if key[2] == "anew" else "sC", key[1]))
        return pv_done.at(("spv",) + key[1:])

    def pt_free(key):
        before = PTR.before(key)
        return pt_used(before) if before else (None, 0)

    def big_used(key):
        kind = key[0]
        if kind == "tok":
            return PJ.is_full(("tok", key[1], 2))
        if kind == "feat":
            return PJ.is_full(("feat",) + FEATS[4 * key[1] + 3])
        if kind == "kA":
            return SC.is_full(("sscore", key[1], "mix"))
        if kind == "win":
            return pv_done.at(("spv", key[1], "win"))
        if kind == "vA":
            return pv_done.at(("spv", key[1], "mix"))
        if kind in ("gate", "up"):
            return PJ.is_full(key + (3,))
        return PJ.is_full(("down", key[1], 2))

    def pages_used(key):
        kind, hb, _ = key
        return PJ.is_full(("hid", hb, 1, 1)) if kind == "cmp" else O.is_full(("o", "sC", hb))

    SROWS = {"d4": (("A",), [(P * c, P) for c in range(4)]),
             "mix": ((), [(S_MIX + P * c, P) for c in range(3)]),
             "anew": ((), [(S_MIX + P + K16 + NS * t, NS) for t in range(3)]),
             "win": (("win",), [(S_WIN + P * c, P) for c in range(4)]),
             "cnew": (("slc",), [(S_WNEW, NS), (S_SNEW, NS)]),
             "slc0": ((), [(S_SLC + P * c, P) for c in range(4)]),
             "slc1": ((), [(S_SLC + 512 + P * c, P) for c in range(4)])}
    SOFT = {"A": (0, 0, S_WIN, "mix"), "cmp": (1, S_CMP, 64, "misc"), "win": (2, S_WIN, WIN + NS, "misc"),
            "slc": (3, S_SNEW, NS + PAST, "slc1")}

    def conv_window(y):
        return y[:, SEQ + 2:SEQ + 2 + 6 * REQ].rearrange("p (b t) -> p b t", t=6)

    CONSTS = [(x[:, 0, :], a["x"][0:P, :]), (x[:, 1, :], a["x"][P:2 * P, :]), (x[0:NS, 2, :], a["x"][2 * P:T, :]),
              (ident[:, :], a["ident"]), (identb[:, :], a["identb"]), (masks[:, :], a["masks"]),
              (rot_c[:, :, :], a["rot_c"]), (rot_s[:, :, :], a["rot_s"]), (blk_c[:, :], a["blk_c"]),
              (blk_s[:, :], a["blk_s"]), (overlap[:, :], a["overlap"]), (same_q[:, :], a["same_q"]),
              (pick[:, :, :], a["pick"]), (row_head[:, :], a["row_head"]), (row_kv[:, :], a["row_kv"]),
              (row_some[:, :], a["row_some"]), (n_pads[:, :], a["n_pads"]), (number[:, :], a["number"]), (page_no[:, :], a["page_table"])]

    with nc.Block() as block:
        @block.sync
        def _(sp):
            for dst, src in CONSTS:
                sp.dma_start(dst, src).then_inc(const_in, 16)
            sp.wait_ge(const_in, 16 * len(CONSTS))

        @block.vector
        def _(dve):
            nc.vector.memset(qblk[:, :, :, :], 0.0).then_inc(set_up, 1)
            nc.vector.memset(kcz[:, :, :], 0.0).then_inc(set_up, 1)
            dve.wait_ge(set_up, 2)

    with nc.Fori(0, DEPTH) as layer:
        with nc.Block() as block:

            @block.sync
            def _(sp):
                for dst, src in ((gT[:, :], a["norm_g"][layer]), (w_gc[:, :, :], a["w_gc"][layer]),
                                 (conv_w[:, :, :], a["conv_w"][layer]), (ustart[:, :, :, :], a["conv_state"][layer]),
                                 (w2[:, :, :], a["w2"][layer]), (pe_c[:, :, :], a["cmp_pe"][layer])):
                    sp.dma_start(dst, src).then_inc(layer_in.sem, 16)
                n_copies = 0
                copies = [(n, b) for n in ("dil1", "dil4", "dil16", "win") for b in range(REQ)]

                def copy_cache(name, b):
                    old, new = a["cache_" + name], o["new_" + name + "_sample"]
                    n = old.shape[2]
                    src = old[layer, b, NEW:n, :].rearrange("n c -> (n c)").rearrange("(s e) -> s e", s=16)
                    dst = new[layer, b, 0:n - NEW, :].rearrange("n c -> (n c)").rearrange("(s e) -> s e", s=16)
                    sp.dma_start(dst, src).then_inc(copied, 16)

                for key in big_keys:
                    if BIG.before(key):
                        sp.wait_ge(*big_used(BIG.before(key)))
                    buf, kind = bigb(key), key[0]
                    if kind == "tok":
                        dst, src = buf[:, :], a["w_tok"][layer, key[1]]
                    elif kind == "feat":
                        dst, src = buf[:, :], a["w_feat"][layer, key[1]]
                    elif kind == "kA":
                        dst, src = buf[:, 0:RB * 896], a["k_a"][layer, key[1]]
                    elif kind == "vA":
                        dst, src = buf[:, 0:RB * 896], a["v_a"][layer, key[1]]
                    elif kind == "win":
                        dst, src = buf[:, :], a["kv_win"][layer, key[1]]
                    elif kind == "gate":
                        dst, src = buf[:, :], a["w_gate"][layer, key[1], key[2]]
                    elif kind == "up":
                        dst, src = buf[:, 0:2048], a["w_up"][layer, key[1], key[2]]
                    else:
                        dst, src = buf[:, :], a["w_out"][layer, key[1]]
                    sp.dma_start(dst, src).then_inc(*BIG.fill(key))
                    if key == ("kA", 0):
                        sp.wait_ge(*expd.at(("A", 1, HEADS - 1)))
                        sp.wait_ge(*PJ.is_used(("feat", "b", WT - 1)))
                        sp.dma_start(long[:, :], a["w1"][layer]).then_inc(*w1_in.inc("all"))
                    if n_copies < len(copies) and key not in (("tok", 0), ("tok", 1)):
                        for _ in range(2):
                            if n_copies < len(copies):
                                copy_cache(*copies[n_copies])
                                n_copies += 1
                assert n_copies == len(copies)
                sp.wait_ge(copied, 16 * n_copies)

            @block.gpsimd
            def _(pool):
                n_stores = 0

                def store(dst, src, done=stored_new):
                    pool.dma_start(dst, src).then_inc(done, 16)
                    return 1

                def load_pages(key):
                    kind, hb, bp = key
                    if PG.before(key):
                        pool.wait_ge(*pages_used(PG.before(key)))
                    k0 = 0 if kind == "cmp" else 2
                    for b in range(2):
                        for g in range(PAGES):
                            at = (hb * RB + bp * 2 + b) * PAGES + g
                            page = pool.value_load(page_no[0:1, at:at + 1], min_val=0, max_val=NPH - 1)
                            src = a["pool"][layer, bass.ds(page, 1), :, k0:k0 + 2, :]
                            pool.dma_start(pgb(key)[:, b, g, :, :], src.rearrange("a p k n -> (a p) k n"))\
                                .then_inc(*PG.fill(key))

                load_pages(page_keys[0])
                load_pages(page_keys[1])
                pool.wait_ge(*roped.at((G_TOK - 1, 2)))
                for tt in range(2):
                    rows = slice(tt * P, (tt + 1) * P)
                    if tt == 1:
                        n_stores += store(o["new_dil1_prompt"][layer], kvp[:, tt, 0:256], stored)
                    n_stores += store(o["new_dil4_prompt"][layer, rows, :], kvp[:, tt, 256:512], stored)
                    n_stores += store(o["new_dil16_prompt"][layer, rows, :], kvp[:, tt, 512:768], stored)
                    n_stores += store(o["new_win_prompt"][layer, rows, :], kvp[:, tt, 768:1024], stored)
                    n_stores += store(o["new_nsa_rows_prompt"][layer, rows, :], kvp[:, tt, 1024:1536], stored)
                assert n_stores == PROMPT_STORES
                n_new = 0
                for name, c in (("dil1", 0), ("dil4", 256), ("dil16", 512), ("win", 768)):
                    new = o["new_" + name + "_sample"]
                    n = new.shape[2]
                    n_new += store(new[layer, :, n - NEW:n, :], kvp[0:NS, 2, c:c + 256])
                n_new += store(o["new_nsa_rows_sample"][layer], kvp[0:NS, 2, 1024:1536])
                pool.wait_ge(*u_state.at("all"))
                n_new += store(o["conv_state_out"][layer], ustate[:, :, :])
                for key in page_keys[2:]:
                    load_pages(key)
                for key in page_keys[-2:]:
                    pool.wait_ge(*PG.is_full(key))
                pool.wait_ge(stored, 16 * PROMPT_STORES)
                pool.wait_ge(stored_new, 16 * n_new)

            @block.tensor
            def _(pe):
                mm = nc.tensor.matmul

                def transposes(key, parts):
                    wait(pe, TR.is_free(key))
                    for i, (out, in_) in enumerate(parts):
                        n = in_.shape[0]
                        last = nc.tensor.transpose(out, in_, ident[0:n, 0:n])
                    last.then_inc(*TR.fill(key))

                for s in STEPS:
                    k = s[0]
                    if k == "xn":
                        tt = s[1]
                        n = PARTS[tt]
                        pe.wait_ge(*normed.at(tt))
                        for hf in range(2):
                            bank = tr(s + (hf,))[:, 0:4 * n].rearrange("p (c t) -> p c t", c=4)
                            transposes(s + (hf,), [(bank[:, c, :], xn[0:n, tt, (4 * hf + c) * P:(4 * hf + c + 1) * P])
                                                   for c in range(4)])
                    elif k in ("tok", "gc"):
                        g, tt = s[1:] if k == "tok" else (None, s[1])
                        n = PARTS[tt]
                        wait(pe, PJ.is_free(s))
                        if k == "tok":
                            pe.wait_ge(*TR.is_used(("xn", tt, 1)))
                            pe.wait_ge(*TR.is_used(("xn", tt, 0)))
                            pe.wait_ge(*BIG.is_full(("tok", g)))
                            w = bigb(("tok", g))[:, :].rearrange("p (k n) -> p k n", k=KT)
                            cols = 512
                        else:
                            pe.wait_ge(*layer_in.at("all"))
                            w, cols = w_gc, 24
                        for c in range(KT):
                            last = mm(pj(s)[0:n, 0:cols], xnT[:, c, TOK0[tt]:TOK0[tt] + n], w[:, c, :],
                                      start=(c == 0), stop=(c == KT - 1))
                        last.then_inc(*PJ.fill(s))
                    elif k == "turn":
                        g, tt = s[1:]
                        n = PARTS[tt]
                        pe.wait_ge(*roped.at((g, tt)))
                        if g < 4:
                            src = proj[0:n, (3 * g + tt) % 4, :]
                            cols = [P * r for r in range(REP)]
                        else:
                            src = kvp[0:n, tt, :]
                            cols = {4: [KCOL["d1"], KCOL["d4"]], 5: [KCOL["d16"], KCOL["win"]],
                                    6: [KCOL["slc"], 1024, 1024 + P] if tt < 2 else [KCOL["slc"]]}[g]
                        transposes(s, [(tr(s)[:, n * i:n * (i + 1)], src[:, c:c + P]) for i, c in enumerate(cols)])
                    elif k == "feat":
                        i = FEATS.index(s[1:])
                        item = ("feat", i // 4)
                        pe.wait_ge(*BIG.is_full(item))
                        wait(pe, PJ.is_free(s))
                        w = bigb(item)[:, :].rearrange("p (k n) -> p k n", k=KT)
                        for c in range(KT):
                            last = mm(pj(s)[:, 0:T], w[:, c, P * (i % 4):P * (i % 4 + 1)], xnT[:, c, :],
                                      start=(c == 0), stop=(c == KT - 1))
                        last.then_inc(*PJ.fill(s))
                    elif k == "score":
                        u = s[1]
                        br, qt, h = u
                        g, r = divmod(h, REP)
                        q0 = qt * P
                        nk = P * (qt + 1)
                        if h == 0:
                            for gq in range(4):
                                pe.wait_ge(*turned(gq, qt))
                            for gk in (4, 5, 6):
                                pe.wait_ge(*turned(gk, qt))
                        for j, (c0, cols) in enumerate(unit_banks(u)):
                            key = s + (j,)
                            wait(pe, SC.is_free(key))
                            for z in range(cols // nk):
                                m1 = MASK["a"][0] + 256 * (c0 // nk + z + 1) if br == "A" else MASK["c"][1]
                                mm(sc(key)[:, z * nk:(z + 1) * nk], identb[:, :], masks[:, m1 - nk:m1],
                                   start=(z == 0), stop=False, skip_group_check=True)
                            types = [t for t in ((0, 1, 2) if br == "A" else (3, 4))]
                            for i, t in enumerate(types):
                                if c0 <= i * nk < c0 + cols:
                                    q = qTA[HD * g:HD * (g + 1), t, r, q0:q0 + P] if br == "A" else \
                                        qTC[HD * g:HD * (g + 1), r, q0:q0 + P]
                                    last = mm(sc(key)[:, i * nk - c0:(i + 1) * nk - c0], q,
                                              kT[HD * g:HD * (g + 1), t, 0:nk], start=False, stop=True,
                                              skip_group_check=True)
                            last.then_inc(*SC.fill(key))
                    elif k == "pturn":
                        u = s[1]
                        slot = UNITS.index(u) % 2
                        pe.wait_ge(*expd.at(u))
                        chunks = unit_chunks(u)
                        for j in range(n_turns(u)):
                            idx = range(4 * j, min(4 * j + 4, len(chunks)))
                            transposes(s + (j,), [(tr(s + (j,))[:, P * (i - 4 * j):P * (i - 4 * j + 1)],
                                                   prob[:, slot, P * i:P * (i + 1)]) for i in idx])
                    elif k == "pv":
                        u = s[1]
                        br, qt, h = u
                        g = h // REP
                        pkey = ("pturn", u)
                        pe.wait_ge(*pt_full(pkey))
                        chunks = unit_chunks(u)
                        for which_o, types in (("A", A_TYPES),) if br == "A" else (("W", ("win",)), ("S", ("slc",))):
                            okey = ("o", which_o, qt)
                            if h == 0:
                                wait(pe, O.is_free(okey))
                            mine = [i for i, (t, _) in enumerate(chunks) if t in types]
                            for i in mine:
                                t, kb = chunks[i]
                                last = mm(ob(okey)[:, HD * h:HD * (h + 1)], ptb(pkey)[:, P * i:P * (i + 1)],
                                          kvp[:, kb, VCOL[t] + HD * g:VCOL[t] + HD * (g + 1)],
                                          start=(i == mine[0]), stop=(i == mine[-1]))
                            if h == HEADS - 1:
                                last.then_inc(*O.fill(okey))
                            elif which_o != "W":
                                last.then_inc(*pv_done.inc(s))
                    elif k in ("gateA", "gateC"):
                        qt = s[1]
                        pe.wait_ge(*(O.is_used(("o", "A", qt)) if k == "gateA" else c_normed.at(("c", qt))))
                        transposes(s, [(tr(s)[:, P * c:P * (c + 1)], o_sb[:, qt, P * c:P * (c + 1)])
                                       for c in range(WT)])
                    elif k == "pe":
                        kind = s[1]
                        if kind == 0:
                            pe.wait_ge(*w1_in.at("all"))
                            pe.wait_ge(*layer_in.at("all"))
                        wait(pe, PJ.is_free(s))
                        for l in range(16):
                            last = mm(pj(s)[:, 0:1], w1[:, kind, l, :], pe_c[:, kind, l:l + 1],
                                      start=(l == 0), stop=(l == 15))
                        last.then_inc(*PJ.fill(s))
                    elif k == "ghid":
                        kind = s[1]
                        wait(pe, PJ.is_free(s))
                        for l in range(16):
                            rhs = cT[:, kind, :, l:l + 8 * (NCP - 1) + 1:8]
                            last = mm(pj(s)[:, 0:KV * NCP].rearrange("p (g n) -> p g n", g=KV), w1[:, kind, l, :],
                                      rhs, start=(l == 0), stop=(l == 15))
                        last.then_inc(*PJ.fill(s))
                    elif k in ("gkc", "gvc"):
                        kind = 0 if k == "gkc" else 1
                        pe.wait_ge(*hid_done.at(("ghid", kind)))
                        wait(pe, PJ.is_free(s))
                        for g in range(KV):
                            last = mm(pj(s)[0:NCP, HD * g:HD * (g + 1)],
                                      hid[kind][:, NCP * g:NCP * (g + 1)],
                                      w2[:, kind, :], start=True, stop=True)
                        last.then_inc(*PJ.fill(s))
                    elif k == "gkt":
                        pe.wait_ge(*kc_done.at("p"))
                        transposes(s, [(tr(s)[:, 0:NCP], kcp[:, :])])
                    elif k == "gates":
                        pe.wait_ge(*PJ.is_used(("gc", 2)))
                        for hb in range(HB):
                            wait(pe, PJ.is_free(("gates", hb)))
                            mm(pj(("gates", hb))[:, 0:24], pick[:, hb, :], gct[0:NS, 2, :], start=True, stop=True)\
                                .then_inc(*PJ.fill(("gates", hb)))
                    elif k == "cscore":
                        qt = s[1]
                        wait(pe, SC.is_free(s))
                        pe.wait_ge(*TR.is_used(("gkt",)))
                        m0, m1 = MASK["cmp%d" % qt]
                        mm(sc(s)[:, 0:256], identb[:, :], masks[:, m0:m1], start=True, stop=False,
                           skip_group_check=True)
                        both = sc(s)[:, 0:256].rearrange("p (g r n) -> p r g n", g=KV, r=REP)
                        for r in range(REP):
                            last = mm(both[:, r, :, :], qTC[:, r, qt * P:(qt + 1) * P], kcz[:, :, :], start=False,
                                      stop=True, skip_group_check=True)
                        last.then_inc(*SC.fill(s))
                    elif k == "cturn":
                        pe.wait_ge(*cexpd.at(s[1]))
                        transposes(s, [(tr(s)[:, P * i:P * (i + 1)], prob[:, 0, P * i:P * (i + 1)])
                                       for i in range(2)])
                    elif k == "cpv":
                        qt = s[1]
                        okey, pkey = ("o", "c", qt), ("cturn", qt)
                        pe.wait_ge(*pt_full(pkey))
                        pe.wait_ge(*PJ.is_used(("gvc",)))
                        wait(pe, O.is_free(okey))
                        for g in range(KV):
                            last = mm(ob(okey)[:, 256 * g:256 * (g + 1)], ptb(pkey)[:, P * g:P * (g + 1)],
                                      vcz[:, 256 * g:256 * (g + 1)], start=True, stop=True)
                        last.then_inc(*O.fill(okey))
                    elif k == "hid":
                        _, hb, kind = s
                        for part in range(2):
                            key = s + (part,)
                            wait(pe, PJ.is_free(key))
                            for bp in range(2):
                                pe.wait_ge(*PG.is_full(("cmp", hb, bp)))
                                pages = pgb(("cmp", hb, bp)).rearrange("p b g k (l n) -> p (b g) k l n", l=8)
                                for l in range(8):
                                    last = mm(pj(key)[:, 256 * bp:256 * (bp + 1)], w1[:, kind, 8 * part + l, :],
                                              pages[:, :, kind, l, :], start=(l == 0), stop=(l == 7))
                            last.then_inc(*PJ.fill(key))
                    elif k in ("kc", "vc"):
                        hb, kind = s[1], 0 if k == "kc" else 1
                        pe.wait_ge(*hid_done.at(("hid", hb, kind)))
                        wait(pe, PJ.is_free(s))
                        for b in range(RB):
                            for g in range(KV):
                                last = mm(pj(s)[0:64, P * b + HD * g:P * b + HD * (g + 1)],
                                          hid[kind][:, 256 * g + 64 * b:256 * g + 64 * (b + 1)], w2[:, kind, :],
                                          start=True, stop=True)
                        last.then_inc(*PJ.fill(s))
                    elif k == "kct":
                        pe.wait_ge(*kc_done.at(s[1]))
                        transposes(s, [(tr(s)[:, 64 * b:64 * (b + 1)], kcs[:, P * b:P * (b + 1)]) for b in range(RB)])
                    elif k == "sscore":
                        _, hb, what = s
                        wait(pe, SC.is_free(s))
                        if what in ("d4", "mix"):
                            pe.wait_ge(*BIG.is_full(("kA", hb)))
                            keys = bigb(("kA", hb))[:, 0:RB * 896].rearrange("p (b n) -> p b n", b=RB)
                        elif what == "win":
                            pe.wait_ge(*BIG.is_full(("win", hb)))
                            keys = bigb(("win", hb))[:, :].rearrange("p (b n) -> p b n", b=RB)
                        bank = sc(s)

                        def q(t, b=None):
                            return qblk[:, t, hb, :] if b is None else qblk[:, t, hb, 32 * b:32 * (b + 1)]

                        def mask(name, cols):
                            m0 = MASK[name][0]
                            mm(bank[:, 0:cols], identb[:, :], masks[:, m0:m0 + cols], start=True, stop=False,
                               skip_group_check=True)

                        def add(out, qs, ks):
                            return mm(out, qs, ks, start=False, stop=True, skip_group_check=True)

                        if what == "d4":
                            mask("sd4", D4)
                            for b in range(RB):
                                last = add(bank[32 * b:32 * (b + 1), :], q(1, b), keys[:, b, 0:D4])
                        elif what == "mix":
                            mask("smix%d" % hb, MIX)
                            for b in range(RB):
                                add(bank[32 * b:32 * (b + 1), 0:P], q(0, b), keys[:, b, D4:D4 + P])
                                add(bank[32 * b:32 * (b + 1), P:P + K16], q(2, b), keys[:, b, D4 + P:D4 + P + K16])
                            for t in range(3):
                                last = add(bank[:, P + K16 + NS * t:P + K16 + NS * (t + 1)], q(t), kTn[:, t, :])
                        elif what == "win":
                            mask("swin", WIN)
                            for b in range(RB):
                                last = add(bank[32 * b:32 * (b + 1), :], q(3, b), keys[:, b, 0:WIN])
                        elif what == "misc":
                            pe.wait_ge(*TR.is_used(("kct", hb)))
                            mask("smisc%d" % hb, P)
                            add(bank[:, 0:NS], q(3), kTn[:, 3, :])
                            add(bank[:, NS:2 * NS], q(3), kTn[:, 4, :])
                            for b in range(RB):
                                last = add(bank[32 * b:32 * (b + 1), 64:64 + NCS], q(3, b), kcT[:, b, 0:NCS])
                        else:
                            z = int(what[-1])
                            for b in range(RB):
                                pkey = ("slc", hb, b // 2)
                                pe.wait_ge(*PG.is_full(pkey))
                                last = mm(bank[32 * b:32 * (b + 1), :].rearrange("p (g n) -> p g n", g=4),
                                          q(3, b), pgb(pkey)[:, b % 2, 4 * z:4 * z + 4, 0, :], start=True, stop=True)
                        last.then_inc(*SC.fill(s))
                    elif k == "cmpt":
                        hb = s[1]
                        pe.wait_ge(*cnormed.at(hb))
                        transposes(s, [(tr(s)[0:64, 0:P], srow[:, S_CMP:S_CMP + 64])])
                    elif k == "imp":
                        hb = s[1]
                        pe.wait_ge(*TR.is_used(("cmpt", hb)))
                        wait(pe, PJ.is_free(s))
                        mm(pj(s)[:, 0:NBLK + 1], PTc[0:NCS, :], overlap[0:NCS, :], start=True, stop=True)\
                            .then_inc(*PJ.fill(s))
                    elif k == "impsum":
                        hb = s[1]
                        pe.wait_ge(*PJ.is_used(("imp", hb)))
                        wait(pe, PJ.is_free(s))
                        mm(pj(s)[:, 0:NBLK + 1], same_q[:, :], impt, start=True, stop=True).then_inc(*PJ.fill(s))
                    elif k == "sturn":
                        _, hb, what = s
                        branch, parts = SROWS[what]
                        for br in branch:
                            pe.wait_ge(*sexpd.at((hb, br)))
                        outs, at = [], 0
                        for c0, n in parts:
                            outs.append((tr(s)[0:n, at:at + P], srow[:, c0:c0 + n]))
                            at += P
                        transposes(s, outs)
                    elif k == "spv":
                        _, hb, what = s
                        okey = ("o", "sA", hb) if what in ("d4", "mix", "anew") else ("o", "sC", hb)
                        pkey = ("sturn", hb, what)
                        if what in ("d4", "win"):
                            wait(pe, O.is_free(okey))
                        pe.wait_ge(*pt_full(pkey))
                        pt, out = ptb(pkey), ob(okey)
                        if what in ("d4", "mix"):
                            pe.wait_ge(*BIG.is_full(("vA", hb)))
                            vals = bigb(("vA", hb))[:, 0:RB * 896].rearrange("p (b c n) -> p b c n", b=RB, c=7)
                            n, c0 = (4, 0) if what == "d4" else (3, 4)
                            for b in range(RB):
                                for c in range(n):
                                    last = mm(out[32 * b:32 * (b + 1), 0:P], pt[:, P * c + 32 * b:P * c + 32 * (b + 1)],
                                              vals[:, b, c0 + c, :], start=(what == "d4" and c == 0), stop=False,
                                              skip_group_check=True)
                        elif what == "anew":
                            for t, name in enumerate(A_TYPES):
                                last = mm(out[:, 0:P], pt[0:NS, P * t:P * (t + 1)],
                                          kvp[0:NS, 2, VCOL[name]:VCOL[name] + P], start=False, stop=True,
                                          skip_group_check=True)
                        elif what == "win":
                            vals = bigb(("win", hb))[:, :].rearrange("p (b c n) -> p b c n", b=RB, c=8)
                            for b in range(RB):
                                for c in range(4):
                                    last = mm(out[32 * b:32 * (b + 1), 0:P], pt[:, P * c + 32 * b:P * c + 32 * (b + 1)],
                                              vals[:, b, 4 + c, :], start=(c == 0), stop=False, skip_group_check=True)
                        elif what == "cnew":
                            pe.wait_ge(*PJ.is_used(("vc", hb)))
                            mm(out[:, 0:P], pt[0:NS, 0:P], kvp[0:NS, 2, VCOL["win"]:VCOL["win"] + P], start=False,
                               stop=True, skip_group_check=True)
                            for b in range(RB):
                                mm(out[32 * b:32 * (b + 1), 2 * P:3 * P], PTc[0:NCS, 32 * b:32 * (b + 1)],
                                   vcs[0:NCS, P * b:P * (b + 1)], start=True, stop=True, skip_group_check=True)
                            last = mm(out[:, P:2 * P], pt[0:NS, P:2 * P], kvp[0:NS, 2, VCOL["slc"]:VCOL["slc"] + P],
                                      start=True, stop=False, skip_group_check=True)
                        else:
                            z = int(what[-1])
                            for b in range(RB):
                                for c in range(4):
                                    last = mm(out[32 * b:32 * (b + 1), P:2 * P],
                                              pt[:, P * c + 32 * b:P * c + 32 * (b + 1)],
                                              pgb(("slc", hb, b // 2))[:, b % 2, 4 * z + c, 1, :], start=False,
                                              stop=(z == 1 and c == 3), skip_group_check=True)
                        last.then_inc(*(O.fill(okey) if what in ("anew", "slc1") else pv_done.inc(s)))
                    elif k in ("sgateA", "sgateC"):
                        hb = s[1]
                        pe.wait_ge(*so_done.at(("so" + k[-1], hb)))
                        transposes(s, [(tr(s)[:, 0:P], o_sb[:, 0, 0:P])])
                    elif k == "gate":
                        _, fh, i, q4 = s
                        item = ("gate", fh, i)
                        pe.wait_ge(*BIG.is_full(item))
                        wait(pe, PJ.is_free(s))
                        w = bigb(item)[:, :].rearrange("p (k n) -> p k n", k=KT)
                        for c in range(KT):
                            last = mm(pj(s)[:, 0:T], w[:, c, P * q4:P * (q4 + 1)], xnT[:, c, :],
                                      start=(c == 0), stop=(c == KT - 1))
                        last.then_inc(*PJ.fill(s))
                    elif k == "up":
                        _, fh, i, q4 = s
                        item = ("up", fh, i)
                        pe.wait_ge(*BIG.is_full(item))
                        if (fh, i, q4) == (0, 0, 0):
                            pe.wait_ge(*TR.is_used(("sgateC", 1)))
                        wait(pe, PJ.is_free(s))
                        w = bigb(item)[:, 0:2048].rearrange("p (k n) -> p k n", k=WT)
                        for c in range(WT):
                            last = mm(pj(s)[:, 0:T], w[:, c, P * q4:P * (q4 + 1)], oT[i][:, c, :],
                                      start=(c == 0), stop=(c == WT - 1))
                        last.then_inc(*PJ.fill(s))
                    elif k == "down":
                        _, nh, tt = s
                        n = PARTS[tt]
                        if nh == 0 and tt == 0:
                            pe.wait_ge(*merged.at((1, 2, 3)))
                        pe.wait_ge(*BIG.is_full(("down", nh)))
                        wait(pe, PJ.is_free(s))
                        w = bigb(("down", nh))[:, :].rearrange("p (k n) -> p k n", k=KT)
                        for c in range(KT):
                            last = mm(pj(s)[0:n, :], mT[:, c, TOK0[tt]:TOK0[tt] + n], w[:, c, :],
                                      start=(c == 0), stop=(c == KT - 1))
                        last.then_inc(*PJ.fill(s))

            @block.scalar
            def _(act):
                f = nc.scalar.activation
                for s in STEPS:
                    k = s[0]
                    if k == "xn":
                        tt = s[1]
                        n = PARTS[tt]
                        f(xn[0:n, tt, :], x[0:n, tt, :], ACT.Square, accum_out=ss[0:n, tt:tt + 1])\
                            .then_inc(*squares.inc(tt))
                        act.wait_ge(*mean.at(tt))
                        f(rn[0:n, tt:tt + 1], ss[0:n, tt:tt + 1], ACT.Sqrt).then_inc(*root.inc(tt))
                    elif k == "tok":
                        g, tt = s[1:]
                        n = PARTS[tt]
                        act.wait_ge(*PJ.is_full(s))
                        i = 3 * g + tt
                        if g < 4:
                            if i >= 4:
                                act.wait_ge(*TR.is_full(("turn",) + divmod(i - 4, 3)))
                            dst = proj[0:n, i % 4, :]
                        else:
                            dst = kvp[0:n, tt, 512 * (g - 4):512 * (g - 3)]
                        f(dst, pj(s)[0:n, :], ACT.Copy).then_inc(*PJ.release(s))
                    elif k == "turn":
                        g, tt = s[1:]
                        if g >= 4:
                            continue
                        n = PARTS[tt]
                        act.wait_ge(*TR.is_full(s))
                        if tt < 2:
                            dst = qTA[:, g, :, tt * P:(tt + 1) * P] if g < 3 else qTC[:, :, tt * P:(tt + 1) * P]
                            f(dst, tr(s)[:, :].rearrange("p (r n) -> p r n", r=REP), ACT.Copy, scale=SCALE)\
                                .then_inc(*TR.release(s))
                        else:
                            for kv in range(KV):
                                rows = slice(HD * kv, HD * (kv + 1))
                                src = tr(s)[rows, 0:REP * NS].rearrange("p (r b t) -> p b r t", r=REP, b=REQ)
                                dst = qblk[rows, g, :, :].rearrange("p h (b k r t) -> p (h b) k r t", b=RB, k=KV, r=REP)
                                last = f(dst[:, :, kv, :, :], src, ACT.Copy, scale=SCALE)
                            last.then_inc(*TR.release(s))
                    elif k == "gc":
                        tt = s[1]
                        n = PARTS[tt]
                        act.wait_ge(*PJ.is_full(s))
                        f(gct[0:n, tt, :], pj(s)[0:n, 0:24], ACT.Tanh, scale=0.5).then_inc(*PJ.release(s))
                    elif k == "feat":
                        kind, kt = s[1:]
                        if kind == "h":
                            act.wait_ge(*PJ.is_full(s))
                            if kt:
                                act.wait_ge(*PJ.is_used(("feat", "c", kt - 1)))
                            f(hsb[:, :], pj(s)[:, 0:T], ACT.Copy).then_inc(*PJ.release(s))
                        elif kind[0] == "z":
                            act.wait_ge(*PJ.is_full(s))
                            if tanh_free(s):
                                act.wait_ge(*tanh_free(s))
                            f(tanh[:, tanh_slot[s], :], pj(s)[:, 0:T], ACT.Tanh, scale=0.5)\
                                .then_inc(*tanh_done.inc(s))
                    elif k == "exp":
                        u = s[1]
                        slot = UNITS.index(u) % 2
                        br, qt, h = u
                        act.wait_ge(*maxed.at(u))
                        nk = P * (qt + 1)
                        if br == "A":
                            f(prob[:, slot, 0:3 * nk], prob[:, slot, 0:3 * nk], ACT.Exp, bias=nmx[slot][:, 0:1],
                              accum_out=den[br, qt][:, h:h + 1]).then_inc(*expd.inc(u))
                        else:
                            for z in range(2):
                                bias = wneg[qt][:, h:h + 1] if z == 0 else nmx[slot][:, 0:1]
                                last = f(prob[:, slot, z * nk:(z + 1) * nk], prob[:, slot, z * nk:(z + 1) * nk],
                                         ACT.Exp, bias=bias,
                                         accum_out=den[br, qt][:, 8 * z + h:8 * z + h + 1])
                            last.then_inc(*expd.inc(u))
                            if h == HEADS - 1:
                                act.wait_ge(*expd.at(u))
                                f(wneg[qt], wneg[qt], ACT.Exp).then_inc(*pad_exp.inc(qt))
                    elif k == "pturn":
                        u = s[1]
                        chunks = unit_chunks(u)
                        wait(act, pt_free(s))
                        for j in range(n_turns(u)):
                            key = s + (j,)
                            cols = P * (min(4 * j + 4, len(chunks)) - 4 * j)
                            act.wait_ge(*TR.is_full(key))
                            f(ptb(s)[:, 512 * j:512 * j + cols], tr(key)[:, 0:cols], ACT.Copy)\
                                .then_inc(*TR.release(key))
                    elif k in ("ghid", "hid"):
                        act.wait_ge(*PJ.is_used(s if k == "ghid" else s + (0,)))
                        cols = KV * NCP if k == "ghid" else 512
                        f(hidt[:, 0:cols], hidp[:, 0:cols], ACT.Tanh, scale=0.5).then_inc(*hid_tanh.inc(s))
                    elif k in ("gkc", "kc"):
                        act.wait_ge(*PJ.is_full(s))
                        dst, src = (kcp[:, :], pj(s)[0:NCP, 0:P]) if k == "gkc" else (kcs[:, :], pj(s)[0:64, :])
                        f(dst, src, ACT.Copy, scale=0.5).then_inc(*PJ.release(s))
                    elif k == "vc":
                        act.wait_ge(*PJ.is_full(s))
                        f(vcs[:, :], pj(s)[0:64, :], ACT.Copy, scale=0.5).then_inc(*PJ.release(s))
                    elif k == "gvc":
                        act.wait_ge(*PJ.is_full(s))
                        act.wait_ge(*zeroed.at("all"))
                        blocks = vcz.rearrange("p (g j d) -> p g j d", g=KV, j=REP)
                        for j in range(REP):
                            last = f(blocks[32 * j:32 * j + NCP, :, j, :],
                                     pj(s)[0:NCP, 0:P].rearrange("p (g d) -> p g d", g=KV), ACT.Copy, scale=0.5)
                        last.then_inc(*PJ.release(s))
                    elif k == "cscore":
                        qt = s[1]
                        act.wait_ge(*SC.is_used(s))
                        f(prob[:, 0, 0:256], prob[:, 0, 0:256], ACT.Exp).then_inc(*cexpd.inc(qt))
                    elif k in ("cturn", "sturn"):
                        act.wait_ge(*TR.is_full(s))
                        wait(act, pt_free(s))
                        if k == "cturn":
                            f(ptb(s)[:, 0:256], tr(s)[:, 0:256], ACT.Copy).then_inc(*TR.release(s))
                        else:
                            parts = SROWS[s[2]][1]
                            n, cols = parts[0][1], P * len(parts)
                            f(ptb(s)[0:n, 0:cols], tr(s)[0:n, 0:cols], ACT.Copy).then_inc(*TR.release(s))
                    elif k == "sscore":
                        _, hb, what = s
                        act.wait_ge(*SC.is_full(s))
                        c0, n = {"d4": (0, D4), "mix": (S_MIX, MIX), "win": (S_WIN, WIN), "slc0": (S_SLC, 512),
                                 "slc1": (S_SLC + 512, 512), "misc": (S_WNEW, 2 * NS)}[what]
                        last = f(srow[:, c0:c0 + n], sc(s)[:, 0:n], ACT.Copy)
                        if what == "misc":
                            last = f(srow[:, S_CMP:S_CMP + 64], sc(s)[:, 64:128], ACT.Copy)
                        last.then_inc(*SC.release(s))
                    elif k == "sexp":
                        _, hb, what = s
                        i, c0, n, _ = SOFT[what]
                        act.wait_ge(*smaxed.at((hb, what)))
                        f(srow[:, c0:c0 + n], srow[:, c0:c0 + n], ACT.Exp, bias=smx[:, i:i + 1],
                          accum_out=sden[:, i:i + 1]).then_inc(*sexpd.inc((hb, what)))
                    elif k == "cmpt":
                        act.wait_ge(*TR.is_full(s))
                        f(PTc[:, :], tr(s)[0:64, 0:P], ACT.Copy).then_inc(*TR.release(s))
                    elif k == "gate":
                        act.wait_ge(*PJ.is_full(s))
                        act.wait_ge(*tanh_free(s))
                        f(tanh[:, tanh_slot[s], :], pj(s)[:, 0:T], ACT.Tanh, scale=0.5).then_inc(*PJ.release(s))

            @block.vector
            def _(dve):
                n_link = [0]

                def link(ins):
                    n_link[0] += 1
                    ins.then_inc(dchain, 1)
                    dve.wait_ge(dchain, n_link[0])

                v = nc.vector

                def rope(rows, src, dst, tc, ts, mid):
                    shape = [rows] + mid + [16]
                    half = [rows] + mid + [8]
                    names = "abc"[:len(mid)]
                    ta = rtmp[0:rows, 0, 0:int(np.prod(mid)), :]
                    tb = rtmp[0:rows, 1, 0:int(np.prod(mid)), :]
                    if len(mid) == 2:
                        ta = ta.rearrange("p (a b) n -> p a b n", a=mid[0])
                        tb = tb.rearrange("p (a b) n -> p a b n", a=mid[0])

                    def bc(t, sh):
                        for _ in mid:
                            t = t.unsqueeze(1)
                        return t.to_broadcast(sh)

                    v.tensor_tensor(ta, src[..., 0:16], bc(tc, shape), ALU.mult)
                    v.tensor_tensor(tb[..., 0:8], src[..., 8:16], bc(ts[:, 0:8], half), ALU.mult)
                    link(v.tensor_tensor(tb[..., 8:16], src[..., 0:8], bc(ts[:, 8:16], half), ALU.mult))
                    return v.tensor_tensor(dst[..., 0:16], ta, tb, ALU.add)

                for s in STEPS:
                    k = s[0]
                    if k == "xn":
                        tt = s[1]
                        n = PARTS[tt]
                        dve.wait_ge(*squares.at(tt))
                        v.tensor_scalar(ss[0:n, tt:tt + 1], ss[0:n, tt:tt + 1], 1.0 / D_MODEL, EPS, ALU.mult,
                                        ALU.add).then_inc(*mean.inc(tt))
                        dve.wait_ge(*root.at(tt))
                        link(v.reciprocal(rn[0:n, tt:tt + 1], rn[0:n, tt:tt + 1]))
                        v.tensor_scalar(xn[0:n, tt, :], x[0:n, tt, :], rn[0:n, tt:tt + 1], None, ALU.mult)\
                            .then_inc(*normed.inc(tt))
                        if tt == 0:
                            dve.wait_ge(*layer_in.at("all"))
                        for hf in range(2):
                            key = s + (hf,)
                            dve.wait_ge(*TR.is_full(key))
                            v.tensor_tensor(xnT[:, 4 * hf:4 * hf + 4, TOK0[tt]:TOK0[tt] + n],
                                            tr(key)[:, 0:4 * n].rearrange("p (c t) -> p c t", c=4),
                                            gT[:, 4 * hf:4 * hf + 4].unsqueeze(2).to_broadcast([P, 4, n]), ALU.mult)\
                                .then_inc(*TR.release(key))
                    elif k == "tok":
                        g, tt = s[1:]
                        n = PARTS[tt]
                        dve.wait_ge(*PJ.is_used(s))
                        if (g, tt) != (0, 0):
                            dve.wait_ge(*roped.at((g, tt - 1) if tt else (g - 1, 2)))
                        tc, ts = rot_c[0:n, tt, :], rot_s[0:n, tt, :]
                        if g < 4:
                            view = proj[0:n, (3 * g + tt) % 4, :].rearrange("p (h d) -> p h d", h=8)
                            last = rope(n, view, view, tc, ts, [8])
                        elif g < 6:
                            view = kvp[0:n, tt, 512 * (g - 4):512 * (g - 3)]\
                                .rearrange("p (j z h d) -> p j z h d", j=2, z=2, h=KV)[:, :, 0, :, :]
                            last = rope(n, view, view, tc, ts, [2, KV])
                        else:
                            view = kvp[0:n, tt, KCOL["slc"]:KCOL["slc"] + P].rearrange("p (h d) -> p h d", h=KV)
                            last = rope(n, view, view, tc, ts, [KV])
                        last.then_inc(*roped.inc((g, tt)))
                    elif k == "turn":
                        g, tt = s[1:]
                        if g < 4:
                            continue
                        n = PARTS[tt]
                        dve.wait_ge(*TR.is_full(s))
                        t0 = 2 * (g - 4)
                        nt = 2 if g < 6 else 1
                        dst = kT[:, t0:t0 + nt, tt * P:(tt + 1) * P] if tt < 2 else kTn[:, t0:t0 + nt, :]
                        last = v.tensor_copy(dst, tr(s)[:, 0:nt * n].rearrange("p (t n) -> p t n", t=nt))
                        if g == 6 and tt < 2:
                            for kv in range(KV):
                                for par in range(2):
                                    src = tr(s)[HD * kv:HD * (kv + 1), P:3 * P]\
                                        .rearrange("p (k n z) -> p k n z", k=2, z=2)[:, :, :, par]
                                    last = v.tensor_copy(cT[HD * par:HD * (par + 1), :, kv, 64 * tt:64 * (tt + 1)], src)
                        last.then_inc(*TR.release(s))
                    elif k == "feat":
                        kind, kt = s[1:]
                        if kind == "h":
                            if kt == 0:
                                dve.wait_ge(*layer_in.at("all"))
                                v.memset(uext[:, 0:2], 0.0)
                            v.tensor_copy(uext[:, SEQ + 2:].rearrange("p (b t) -> p b t", t=6)[:, :, 0:2],
                                          ustart[:, kt, :, :])
                            continue
                        dve.wait_ge(*PJ.is_full(s))
                        un = uext[:, SEQ + 2:].rearrange("p (b t) -> p b t", t=6)
                        if kind == "c":
                            dve.wait_ge(*PJ.is_used(("feat", "h", kt)))
                            v.tensor_tensor(uext[:, 2:SEQ + 2], pj(s)[:, 0:SEQ], hsb[:, 0:SEQ], ALU.mult)
                            v.tensor_tensor(un[:, :, 2:6], pj(s)[:, SEQ:T].rearrange("p (b t) -> p b t", t=NEW),
                                            hsb[:, SEQ:T].rearrange("p (b t) -> p b t", t=NEW), ALU.mult)\
                                .then_inc(*PJ.release(s))
                            dve.wait_ge(*PJ.is_used(s))
                            m = SEQ + REQ * 6
                            link(v.tensor_scalar(ysb[:, 0:m], uext[:, 0:m], conv_w[:, kt, 0:1], None, ALU.mult))
                            link(v.scalar_tensor_tensor(ysb[:, 0:m], uext[:, 1:m + 1], conv_w[:, kt, 1:2], ysb[:, 0:m],
                                                        ALU.mult, ALU.add))
                            link(v.scalar_tensor_tensor(ysb[:, 0:m], uext[:, 2:m + 2], conv_w[:, kt, 2:3], ysb[:, 0:m],
                                                        ALU.mult, ALU.add))
                            v.tensor_copy(ustate[:, kt, 0:2], uext[:, SEQ:SEQ + 2])
                            last = v.tensor_copy(ustate[:, kt, 2:].rearrange("p (b t) -> p b t", t=2), un[:, :, 4:6])
                            if kt == WT - 1:
                                last.then_inc(*u_state.inc("all"))
                        elif kind == "b":
                            v.tensor_tensor(prod[:, 0:SEQ], pj(s)[:, 0:SEQ], ysb[:, 0:SEQ], ALU.mult)
                            v.tensor_tensor(prod[:, SEQ:T].rearrange("p (b t) -> p b t", t=NEW),
                                            pj(s)[:, SEQ:T].rearrange("p (b t) -> p b t", t=NEW),
                                            conv_window(ysb)[:, :, 0:NEW], ALU.mult).then_inc(*PJ.release(s))
                        elif kind == "zb":
                            dve.wait_ge(*tanh_done.at(s))
                            tn = tanh[:, tanh_slot[s], :]
                            v.scalar_tensor_tensor(o_tmp[:, 0:T], tn, 1.0, pj(s)[:, 0:T], ALU.add, ALU.mult)\
                                .then_inc(*PJ.release(s))
                            dve.wait_ge(*PJ.is_used(s))
                            link(v.tensor_tensor(oT[1][:, kt, :], o_tmp[:, 0:T], prod[:, :], ALU.mult))
                        else:
                            dve.wait_ge(*tanh_done.at(s))
                            tn = tanh[:, tanh_slot[s], :]
                            v.scalar_tensor_tensor(oT[0 if kind == "za" else 2][:, kt, :], tn, 1.0, pj(s)[:, 0:T],
                                                   ALU.add, ALU.mult).then_inc(*PJ.release(s))
                    elif k == "score":
                        u = s[1]
                        br, qt, h = u
                        i = UNITS.index(u)
                        slot = i % 2
                        if i >= 2:
                            u2 = UNITS[i - 2]
                            dve.wait_ge(*TR.is_full(("pturn", u2, n_turns(u2) - 1)))
                        nk = P * (qt + 1)
                        if br == "A":
                            for j, (c0, cols) in enumerate(unit_banks(u)):
                                key = s + (j,)
                                dve.wait_ge(*SC.is_full(key))
                                v.tensor_scalar(prob[:, slot, c0:c0 + cols], sc(key)[:, 0:cols], 0.0, -3e38, ALU.add,
                                                ALU.max, accum_out=mx[slot][:, j:j + 1]).then_inc(*SC.release(key))
                            dve.wait_ge(*SC.is_used(key))
                            if j:
                                dve.wait_ge(*SC.is_used(s + (0,)))
                                v.tensor_scalar(nmx[slot][:, 0:1], mx[slot][:, 0:1], mx[slot][:, 1:2], -1.0, ALU.max,
                                                ALU.mult).then_inc(*maxed.inc(u))
                            else:
                                v.tensor_scalar(nmx[slot][:, 0:1], mx[slot][:, 0:1], -1.0, None, ALU.mult)\
                                    .then_inc(*maxed.inc(u))
                        else:
                            key = s + (0,)
                            dve.wait_ge(*SC.is_full(key))
                            for z in range(2):
                                last = v.tensor_scalar(prob[:, slot, z * nk:(z + 1) * nk],
                                                       sc(key)[:, z * nk:(z + 1) * nk], 0.0, -3e38, ALU.add, ALU.max,
                                                       accum_out=mx[slot][:, z:z + 1])
                            last.then_inc(*SC.release(key))
                            dve.wait_ge(*SC.is_used(key))
                            v.tensor_scalar(wneg[qt][:, h:h + 1], mx[slot][:, 0:1], -1.0, 0.0, ALU.mult, ALU.min)
                            v.tensor_scalar(nmx[slot][:, 0:1], mx[slot][:, 1:2], -1.0, None, ALU.mult)\
                                .then_inc(*maxed.inc(u))
                    elif k == "out":
                        _, br, qt = s
                        d8 = [P, HEADS, HD]
                        nden = 8 if br == "A" else 16
                        dve.wait_ge(*O.is_full(("o", "A" if br == "A" else "S", qt)))
                        if br == "C":
                            dve.wait_ge(*pad_exp.at(qt))
                            link(v.scalar_tensor_tensor(den[br, qt][:, 0:8], wneg[qt], n_pads[:, qt:qt + 1],
                                                        den[br, qt][:, 0:8], ALU.mult, ALU.add))
                        link(v.reciprocal(rec[:, 0:nden], den[br, qt]))
                        view = o_sb[:, qt, :].rearrange("p (h d) -> p h d", h=HEADS)
                        if br == "A":
                            dve.wait_ge(*O.is_full(("o", "A", qt)))
                            v.tensor_tensor(view, ob(("o", "A", qt))[:, :].rearrange("p (h d) -> p h d", h=HEADS),
                                            rec[:, 0:8].unsqueeze(2).to_broadcast(d8), ALU.mult)\
                                .then_inc(*O.release(("o", "A", qt)))
                        else:
                            dve.wait_ge(*PJ.is_used(("gc", qt)))
                            link(v.tensor_scalar(rec[:, 0:16], rec[:, 0:16], 0.5, None, ALU.mult))
                            for z, b3 in ((0, 2), (1, 1)):
                                last = v.scalar_tensor_tensor(rec[:, 8 * z:8 * z + 8], gct[:, qt, 8 * b3:8 * b3 + 8],
                                                              1.0, rec[:, 8 * z:8 * z + 8], ALU.add, ALU.mult)
                            link(last)
                            tmp = o_tmp[:, :].rearrange("p (h d) -> p h d", h=HEADS)
                            dve.wait_ge(*TR.is_full(("gateA", qt)))
                            for z, key in ((0, ("o", "W", qt)), (1, ("o", "S", qt))):
                                dve.wait_ge(*O.is_full(key))
                                v.tensor_tensor(view if z == 0 else tmp,
                                                ob(key)[:, :].rearrange("p (h d) -> p h d", h=HEADS),
                                                rec[:, 8 * z:8 * z + 8].unsqueeze(2).to_broadcast(d8), ALU.mult)\
                                    .then_inc(*O.release(key))
                                dve.wait_ge(*O.is_used(key))
                            v.tensor_tensor(o_sb[:, qt, :], o_sb[:, qt, :], o_tmp[:, :], ALU.add)\
                                .then_inc(*c_normed.inc(("W", qt)))
                    elif k in ("gateA", "gateC"):
                        qt = s[1]
                        o_t = oT[0] if k == "gateA" else oT[2]
                        dve.wait_ge(*TR.is_full(s))
                        part = o_t[:, :, qt * P:(qt + 1) * P]
                        dve.wait_ge(*PJ.is_used(("feat", "za" if k == "gateA" else "zc", WT - 1)))
                        v.tensor_tensor(part, tr(s)[:, :].rearrange("p (c n) -> p c n", c=WT), part, ALU.mult)\
                            .then_inc(*TR.release(s))
                    elif k == "pe":
                        if s[1] == 0:
                            dve.wait_ge(*TR.is_full(("pturn", UNITS[-1], n_turns(UNITS[-1]) - 1)))
                            v.memset(vcz, 0.0).then_inc(*zeroed.inc("all"))
                        dve.wait_ge(*PJ.is_full(s))
                        v.tensor_copy(pe_b[:, s[1]:s[1] + 1], pj(s)[:, 0:1]).then_inc(*PJ.release(s))
                        dve.wait_ge(*PJ.is_used(s))
                    elif k == "ghid":
                        kind = s[1]
                        dve.wait_ge(*PJ.is_full(s))
                        n = KV * NCP
                        if kind == 0:
                            dve.wait_ge(*O.is_full(("o", "S", 1)))
                            dve.wait_ge(stored, 16 * PROMPT_STORES)
                            v.memset(hidb[:, 512:516], 0.0)
                        else:
                            dve.wait_ge(*hid_done.at(("ghid", 0)))
                        v.tensor_scalar(hidp[:, 0:n], pj(s)[:, 0:n], pe_b[:, kind:kind + 1], None, ALU.add)\
                            .then_inc(*PJ.release(s))
                        dve.wait_ge(*hid_tanh.at(s))
                        v.scalar_tensor_tensor(hid[kind][:, 0:n], hidt[:, 0:n], 1.0, hidp[:, 0:n], ALU.add, ALU.mult)\
                            .then_inc(*hid_done.inc(s))
                    elif k == "hid":
                        _, hb, kind = s
                        ka, kb = s + (0,), s + (1,)
                        sv = lambda key: pj(key)[:, :].rearrange("p (m g i) -> p m g i", g=KV, i=8)
                        dve.wait_ge(*PJ.is_full(kb))
                        before = of("ghid", "hid")
                        dve.wait_ge(*hid_done.at(before[before.index(s) - 1]))
                        for g in range(KV):
                            last = v.tensor_copy(hidb[:, 256 * g:256 * (g + 1)].rearrange("p (m i) -> p m i", i=8),
                                                 sv(kb)[:, :, g, :])
                        last.then_inc(*PJ.release(kb))
                        dve.wait_ge(*PJ.is_used(kb))
                        dve.wait_ge(*PJ.is_full(ka))
                        for g in range(KV):
                            last = v.scalar_tensor_tensor(
                                hidp[:, 256 * g:256 * (g + 1)].rearrange("p (m i) -> p m i", i=8),
                                sv(ka)[:, :, g, :], pe_b[:, kind:kind + 1],
                                hidb[:, 256 * g + 1:256 * (g + 1) + 1].rearrange("p (m i) -> p m i", i=8),
                                ALU.add, ALU.add)
                        last.then_inc(*PJ.release(ka))
                        dve.wait_ge(*hid_tanh.at(s))
                        v.scalar_tensor_tensor(hid[kind], hidt, 1.0, hidp, ALU.add, ALU.mult)\
                            .then_inc(*hid_done.inc(s))
                    elif k in ("gkc", "kc"):
                        who = "p" if k == "gkc" else s[1]
                        dve.wait_ge(*PJ.is_used(s))
                        dve.wait_ge(*(roped.at((G_TOK - 1, 2)) if who == "p" else kc_done.at("p" if who == 0 else 0)))
                        if k == "gkc":
                            view = kcp[:, :].rearrange("p (h d) -> p h d", h=KV)
                            last = rope(NCP, view, view, blk_c[0:NCP, :], blk_s[0:NCP, :], [KV])
                        else:
                            view = kcs[:, :].rearrange("p (h d) -> p h d", h=8)
                            last = rope(64, view, view, blk_c[:, :], blk_s[:, :], [8])
                        last.then_inc(*kc_done.inc(who))
                    elif k in ("gkt", "kct"):
                        dve.wait_ge(*TR.is_full(s))
                        if k == "gkt":
                            for g in range(KV):
                                rows = slice(HD * g, HD * (g + 1))
                                last = v.tensor_copy(kcz[rows, g, 0:NCP], tr(s)[rows, 0:NCP])
                        else:
                            last = v.tensor_copy(kcT[:, :, :], tr(s)[:, 0:256].rearrange("p (b n) -> p b n", b=RB))
                        last.then_inc(*TR.release(s))
                    elif k == "gates":
                        for hb in range(HB):
                            key = ("gates", hb)
                            dve.wait_ge(*PJ.is_full(key))
                            v.tensor_tensor(sgt.rearrange("p (b h) -> p b h", b=3),
                                            pj(key)[:, 0:24].rearrange("p (b h) -> p b h", b=3),
                                            row_head[:, :].unsqueeze(1).to_broadcast([P, 3, HEADS]), ALU.mult)\
                                .then_inc(*PJ.release(key))
                            dve.wait_ge(*PJ.is_used(key))
                            link(v.reduce_sum(sg[hb], sgt.rearrange("p (b h) -> p b h", b=3), AX.X))
                            link(v.tensor_scalar(sg[hb], sg[hb], 1.0, 0.5, ALU.add, ALU.mult))
                    elif k == "cscore":
                        qt = s[1]
                        dve.wait_ge(*SC.is_full(s))
                        sv = sc(s)[:, 0:256].rearrange("p (h n) -> p h n", h=HEADS)
                        pv = prob[:, 0, 0:256].rearrange("p (h n) -> p h n", h=HEADS)
                        link(v.reduce_max(cmx, sv, AX.X))
                        if qt == 1:
                            dve.wait_ge(*TR.is_full(("cturn", 0)))
                        v.tensor_tensor(pv, sv, cmx.unsqueeze(2).to_broadcast([P, HEADS, 32]), ALU.subtract)\
                            .then_inc(*SC.release(s))
                        dve.wait_ge(*cexpd.at(qt))
                        link(v.reduce_sum(cden, pv, AX.X))
                        link(v.reciprocal(crec, cden))
                        if qt == 0:
                            link(v.tensor_scalar(crec, crec, row_some[:, 0:1], None, ALU.mult))
                        link(v.tensor_scalar(crec, crec, 0.5, None, ALU.mult))
                        link(v.scalar_tensor_tensor(crec, gct[:, qt, 0:8], 1.0, crec, ALU.add, ALU.mult))
                    elif k == "cpv":
                        qt = s[1]
                        key = ("o", "c", qt)
                        dve.wait_ge(*O.is_full(key))
                        v.tensor_tensor(o_tmp[:, :].rearrange("p (h d) -> p h d", h=HEADS),
                                        ob(key)[:, :].rearrange("p (h d) -> p h d", h=HEADS),
                                        crec.unsqueeze(2).to_broadcast([P, HEADS, HD]), ALU.mult)\
                            .then_inc(*O.release(key))
                        dve.wait_ge(*O.is_used(key))
                        v.tensor_tensor(o_sb[:, qt, :], o_sb[:, qt, :], o_tmp[:, :], ALU.add)\
                            .then_inc(*c_normed.inc(("c", qt)))
                    elif k == "sexp":
                        _, hb, what = s
                        i, c0, n, scores = SOFT[what]
                        dve.wait_ge(*SC.is_used(("sscore", hb, scores)))
                        v.tensor_reduce(smx[:, i:i + 1], srow[:, c0:c0 + n], AX.X, ALU.max, negate=True)\
                            .then_inc(*smaxed.inc((hb, what)))
                        dve.wait_ge(*sexpd.at((hb, what)))
                        link(v.reciprocal(srec[:, i:i + 1], sden[:, i:i + 1]))
                        if what == "cmp":
                            v.tensor_scalar(srow[:, c0:c0 + n], srow[:, c0:c0 + n], srec[:, i:i + 1], None, ALU.mult)\
                                .then_inc(*cnormed.inc(hb))
                    elif k == "imp":
                        hb = s[1]
                        dve.wait_ge(*PJ.is_full(s))
                        v.tensor_copy(impt, pj(s)[:, 0:NBLK + 1]).then_inc(*PJ.release(s))
                    elif k == "impsum":
                        hb = s[1]
                        dve.wait_ge(*PJ.is_full(s))
                        v.tensor_copy(impv, pj(s)[:, 0:NBLK]).then_inc(*PJ.release(s))
                        dve.wait_ge(*PJ.is_used(s))
                        link(v.tensor_reduce(least, impv[:, 1:NBLK], AX.X, ALU.min))
                        link(v.tensor_scalar(hitv, impv, least, None, ALU.is_equal))
                        link(v.tensor_tensor(hitv, hitv, number[:, :], ALU.mult))
                        link(v.tensor_reduce(which, hitv[:, 1:NBLK], AX.X, ALU.max))
                        link(v.tensor_scalar(dropv, number[:, :], which, NEG, ALU.is_equal, ALU.mult))
                    elif k == "drop":
                        hb = s[1]
                        dve.wait_ge(*SC.is_used(("sscore", hb, "slc1")))
                        part = srow[:, S_SLC:S_SLC + PAST].rearrange("p (m n) -> p m n", m=NBLK)
                        link(v.tensor_tensor(part, part, dropv.unsqueeze(2).to_broadcast([P, NBLK, SLC]), ALU.add))
                    elif k in ("soA", "soC"):
                        hb = s[1]
                        okey = ("o", "s" + k[-1], hb)
                        dve.wait_ge(*O.is_full(okey))
                        if k == "soA":
                            link(v.tensor_scalar(scoef[:, 0:2], row_kv[:, :], srec[:, 0:1], None, ALU.mult))
                            terms = [(0, scoef[:, 0:1]), (HD, scoef[:, 1:2])]
                            if hb == 0:
                                dve.wait_ge(*TR.is_full(("gateC", 0)))
                            else:
                                dve.wait_ge(*TR.is_full(("sgateC", hb - 1)))
                        else:
                            terms = []
                            for j, (i, b3, c) in enumerate(((2, 2, 0), (3, 1, P), (1, 0, 2 * P))):
                                cc = scoef[:, 2 * j:2 * j + 2]
                                link(v.tensor_scalar(cc, row_kv[:, :], sg[hb][:, b3:b3 + 1],
                                                     srec[:, i:i + 1] if i != 1 else 1.0, ALU.mult, ALU.mult))
                                terms += [(c, cc[:, 0:1]), (c + HD, cc[:, 1:2])]
                            dve.wait_ge(*TR.is_full(("sgateA", hb)))
                        acc = o_sb[:, 0, 0:HD]
                        for j, (c, coef) in enumerate(terms):
                            src = ob(okey)[:, c:c + HD]
                            if j == 0:
                                link(v.tensor_scalar(acc, src, coef, None, ALU.mult))
                            elif j < len(terms) - 1:
                                link(v.scalar_tensor_tensor(acc, src, coef, acc, ALU.mult, ALU.add))
                            else:
                                v.scalar_tensor_tensor(acc, src, coef, acc, ALU.mult, ALU.add)\
                                    .then_inc(*O.release(okey))
                        dve.wait_ge(*O.is_used(okey))
                        v.tensor_copy(o_sb[:, 0, HD:2 * HD], acc).then_inc(*so_done.inc(s))
                    elif k in ("sgateA", "sgateC"):
                        hb = s[1]
                        o_t = oT[0] if k == "sgateA" else oT[2]
                        dve.wait_ge(*TR.is_full(s))
                        for par in range(2):
                            rows = slice(HD * par, HD * (par + 1))
                            src = tr(s)[rows, 0:P].rearrange("p (b c z t) -> p c z b t", b=RB, z=2, t=NEW)[:, :, par, :, :]
                            part = o_t[rows, :, SEQ + 16 * hb:SEQ + 16 * (hb + 1)]
                            part = part.rearrange("p c (b t) -> p c b t", t=NEW)
                            last = v.tensor_tensor(part, src, part, ALU.mult)
                        last.then_inc(*TR.release(s))
                    elif k == "up":
                        _, fh, i, q4 = s
                        gkey = ("gate", fh, i, q4)
                        dve.wait_ge(*PJ.is_used(gkey))
                        dve.wait_ge(*PJ.is_full(s))
                        tn = tanh[:, tanh_slot[gkey], :]
                        ft = 4 * fh + q4
                        dst = mT[:, ft, :] if i == 0 else prod[:, :]
                        v.scalar_tensor_tensor(dst, tn, 1.0, pj(s)[:, 0:T], ALU.add, ALU.mult)\
                            .then_inc(*PJ.release(s))
                        dve.wait_ge(*PJ.is_used(s))
                        if i:
                            v.tensor_tensor(mT[:, ft, :], mT[:, ft, :], prod[:, :], ALU.add)\
                                .then_inc(*merged.inc(s[1:]))
                            dve.wait_ge(*merged.at(s[1:]))
                    elif k == "down":
                        _, nh, tt = s
                        n = PARTS[tt]
                        dve.wait_ge(*PJ.is_full(s))
                        part = x[0:n, tt, 512 * nh:512 * (nh + 1)]
                        v.scalar_tensor_tensor(part, pj(s)[0:n, :], 0.25, part, ALU.mult, ALU.add)\
                            .then_inc(*PJ.release(s))


        with nc.Block() as block:
            @block.gpsimd
            def _(pool):
                pool.dma_reset(per_layer)
                pool.sem_clear(per_layer)

    y = paged[0][:, 0:3 * D_MODEL].rearrange("p (t n) -> p t n", t=3)
    last_g = paged[1][:, 0:D_MODEL]
    with nc.Block() as block:
        @block.sync
        def _(sp):
            sp.dma_start(last_g, a["final_g"]).then_inc(y_out, 16)
            for tt in range(3):
                n = PARTS[tt]
                sp.wait_ge(y_ready, tt + 1)
                sp.dma_start(o["y"][TOK0[tt]:TOK0[tt] + n, :], y[0:n, tt, :]).then_inc(y_out, 16)
            sp.wait_ge(y_out, 16 * 4)

        @block.scalar
        def _(act):
            for tt in range(3):
                n = PARTS[tt]
                nc.scalar.activation(y[0:n, tt, :], x[0:n, tt, :], ACT.Square, accum_out=ss[0:n, tt:tt + 1])\
                    .then_inc(y_squares, 1)
                act.wait_ge(y_mean, tt + 1)
                nc.scalar.activation(rn[0:n, tt:tt + 1], ss[0:n, tt:tt + 1], ACT.Sqrt).then_inc(y_root, 1)

        @block.vector
        def _(dve):
            for tt in range(3):
                n = PARTS[tt]
                dve.wait_ge(y_squares, tt + 1)
                nc.vector.tensor_scalar(ss[0:n, tt:tt + 1], ss[0:n, tt:tt + 1], 1.0 / D_MODEL, EPS, ALU.mult, ALU.add)\
                    .then_inc(y_mean, 1)
                dve.wait_ge(y_root, tt + 1)
                nc.vector.reciprocal(rn[0:n, tt:tt + 1], rn[0:n, tt:tt + 1]).then_inc(y_link, 1)
                dve.wait_ge(y_link, 2 * tt + 1)
                nc.vector.tensor_scalar(y[0:n, tt, :], x[0:n, tt, :], rn[0:n, tt:tt + 1], None, ALU.mult)\
                    .then_inc(y_link, 1)
                dve.wait_ge(y_link, 2 * tt + 2)
                if tt == 0:
                    dve.wait_ge(y_out, 16)
                nc.vector.tensor_tensor(y[0:n, tt, :], y[0:n, tt, :], last_g[0:n, :], ALU.mult).then_inc(y_ready, 1)



def constants():
    f = np.float32
    c = {}
    c["ident"] = np.eye(P, dtype=f)
    inv = (np.float32(THETA) ** (-(2.0 / 16) * np.arange(HALF_ROT, dtype=f))).astype(f)

    def rot(pos):
        ang = pos.astype(f)[:, None] * inv[None, :]
        cos, sin = np.cos(ang).astype(f), np.sin(ang).astype(f)
        return np.concatenate([cos, cos], 1), np.concatenate([-sin, sin], 1)

    pos = np.zeros((3, P))
    pos[0], pos[1] = np.arange(P), P + np.arange(P)
    pos[2, 0:NS] = PAST + np.arange(NS) % NEW
    rc, rs = rot(pos.reshape(-1))
    c["rot_c"] = np.ascontiguousarray(rc.reshape(3, P, 16).transpose(1, 0, 2))
    c["rot_s"] = np.ascontiguousarray(rs.reshape(3, P, 16).transpose(1, 0, 2))
    c["blk_c"], c["blk_s"] = rot(CMP_STRIDE * np.arange(64) + CMP_LEN - 1.0)
    cs, ss = CMP_STRIDE * np.arange(64)[:, None], SLC * np.arange(NBLK + 1)[None, :]
    ov = np.clip(np.minimum(cs + CMP_LEN, ss + SLC) - np.maximum(cs, ss), 0, None) / CMP_STRIDE
    ov[NCS:] = 0
    c["overlap"] = ov.astype(f)
    row = np.arange(P)
    rb, rg, rr, rt = row // 32, row // 16 % 2, row // 4 % 4, row % 4
    key = rb * 1000 + rg * 100 + rt
    c["same_q"] = (key[:, None] == key[None, :]).astype(f)
    pick = np.zeros((NS, HB, P), f)
    for hb in range(HB):
        pick[NEW * (RB * hb + rb) + rt, hb, row] = 1
    c["pick"] = pick
    c["row_head"] = (REP * rg + rr == np.arange(HEADS)[:, None]).T.astype(f)
    c["row_kv"] = (rg == np.arange(KV)[:, None]).T.astype(f)
    c["row_some"] = (row >= CMP_LEN - 1).astype(f)[:, None]
    c["n_pads"] = (WIN - row[:, None] - P * np.arange(2)).astype(f)
    c["number"] = np.broadcast_to(np.arange(NBLK, dtype=f), (P, NBLK))
    m = {}
    q, k = row[:, None] + P, np.arange(SEQ)[None, :]
    dist = q - k
    m["a"] = np.concatenate([(dist >= 0) & (dist <= 128), (dist >= 0) & (dist % 4 == 0),
                             (dist >= 0) & (dist % 16 == 0)], 1)
    m["c"] = dist >= 0
    n = np.arange(32)
    for qt in range(2):
        ok = (CMP_STRIDE * n + CMP_LEN - 1 <= row[:, None] + P * qt) & (n < NCP)
        m["cmp%d" % qt] = np.tile(ok, (1, HEADS))
    t = rt[:, None]
    j = np.arange(512)[None, :]
    m["sd4"] = (j % 4 == t)
    m["swin"] = j >= t
    jn = np.arange(NS)[None, :]
    for hb in range(HB):
        mine = jn // NEW == RB * hb + rb[:, None]
        upto, same = mine & (jn % NEW <= t), mine & (jn % NEW == t)
        m["smix%d" % hb] = np.concatenate([np.arange(P)[None, :] >= t, np.arange(K16)[None, :] % 4 == t,
                                           upto, same, same], 1)
        m["smisc%d" % hb] = np.concatenate([upto, upto, np.broadcast_to(np.arange(64) < NCS, (P, 64))], 1)
    at, total = mask_at()
    masks = np.zeros((P, total), f)
    for name, (m0, m1) in at.items():
        masks[:, m0:m1] = np.where(m[name], 0.0, NEG)
    bf = mybir.dt.np(BF16)
    c["masks"], c["identb"] = masks.astype(bf), np.eye(P, dtype=f).astype(bf)
    return {k2: np.ascontiguousarray(v2) for k2, v2 in c.items()}


SPLITS = dict(q_a=3 * WIDTH, k_a=384, v_a=384, z_a=WIDTH, h_b=WIDTH, b_b=WIDTH, c_b=WIDTH, z_b=WIDTH, q_c=WIDTH,
              kv_c=768, g_c=24, z_c=WIDTH, g_merge=3 * D_MODEL)


def tiles(w, n):
    d, kk, cols = w.shape
    return np.ascontiguousarray(w.reshape(d, kk // P, P, cols // n, n).transpose(0, 3, 2, 1, 4)
                                .reshape(d, cols // n, P, kk // P * n))


def layouts(x_prompt, x_sample, cache_dil1_kv, cache_dil4_kv, cache_dil16_kv, cache_win_kv, state_conv, cache_nsa_kv,
            page_table, norm_g, w_in, conv_w, cmp_pe_k, cmp_pe_v, cmp_wk1, cmp_wk2, cmp_wv1, cmp_wv2, w_up_a, w_up_b,
            w_up_c, w_out, final_norm_g):
    A = {}
    D = DEPTH
    A["x"] = np.concatenate([x_prompt.reshape(SEQ, D_MODEL), x_sample.reshape(NS, D_MODEL)])
    at, cols = 0, {}
    for name, n in SPLITS.items():
        cols[name] = w_in[:, :, at:at + n]
        at += n

    def by_rep(w):
        return w.reshape(D, D_MODEL, KV, REP, HD).transpose(0, 1, 3, 2, 4).reshape(D, D_MODEL, WIDTH)

    ka, va = (cols[n].reshape(D, D_MODEL, 3, P) for n in ("k_a", "v_a"))
    kvc = cols["kv_c"].reshape(D, D_MODEL, 6, P)
    pairs = [z[:, :, i] for i in range(3) for z in (ka, va)] + [kvc[:, :, i] for i in (4, 5, 0, 1, 2, 3)]
    tok = [by_rep(cols["q_a"][:, :, WIDTH * i:WIDTH * (i + 1)]) for i in range(3)] + [by_rep(cols["q_c"])] + pairs
    A["w_tok"] = tiles(np.concatenate(tok, 2), 512)
    col = {"h": "h_b", "c": "c_b", "b": "b_b", "zb": "z_b", "za": "z_a", "zc": "z_c"}
    A["w_feat"] = tiles(np.concatenate([cols[col[k]][:, :, P * t:P * (t + 1)] for k, t in FEATS], 2), 512)
    A["w_gc"] = tiles(cols["g_c"], 24)[:, 0].reshape(D, P, KT, 24)
    g = tiles(cols["g_merge"], 512).reshape(D, 3, 2, P, KT * 512)
    A["w_gate"] = np.ascontiguousarray(g.transpose(0, 2, 1, 3, 4))
    up = np.stack([tiles(w, 512) for w in (w_up_a, w_up_b, w_up_c)], 1)
    A["w_up"] = np.ascontiguousarray(up.transpose(0, 2, 1, 3, 4))
    A["w_out"] = tiles(w_out, 512)
    A["norm_g"] = np.ascontiguousarray(norm_g.reshape(D, KT, P).transpose(0, 2, 1))
    A["final_g"] = np.broadcast_to(final_norm_g, (P, D_MODEL))
    A["conv_w"] = conv_w.reshape(D, 3, WT, P).transpose(0, 3, 2, 1)
    A["conv_state"] = state_conv.reshape(D, REQ, 2, WT, P).transpose(0, 4, 3, 1, 2)
    A["cmp_pe"] = np.stack([p.reshape(D, 16, P).transpose(0, 2, 1) for p in (cmp_pe_k, cmp_pe_v)], 2)
    A["w1"] = np.stack([w.reshape(D, 16, P, P).transpose(0, 2, 1, 3) for w in (cmp_wk1, cmp_wv1)], 2)\
        .reshape(D, P, 4096)
    A["w2"] = np.stack([cmp_wk2, cmp_wv2], 2)
    k4, v4 = cache_dil4_kv[:, :, :, 0], cache_dil4_kv[:, :, :, 1]
    k1, v1 = cache_dil1_kv[:, :, :, 0], cache_dil1_kv[:, :, :, 1]
    near = cache_dil16_kv.reshape(D, REQ, D16 // 16, 16, 2, KV, HD)[:, :, :, 0:NEW].reshape(D, REQ, K16, 2, KV, HD)
    k16, v16 = near[:, :, :, 0], near[:, :, :, 1]
    kw, vw = cache_win_kv[:, :, :, 0], cache_win_kv[:, :, :, 1]

    def keys(*ks):
        z = np.concatenate(ks, 2).reshape(D, HB, RB, -1, P)
        return z.transpose(0, 1, 4, 2, 3)

    def values(*vs):
        z = np.concatenate(vs, 2).reshape(D, HB, RB, -1, P, P)
        return z.transpose(0, 1, 4, 2, 3, 5).reshape(D, HB, P, RB, -1)

    A["k_a"] = keys(k4, k1, k16).reshape(D, HB, P, -1)
    A["v_a"] = values(v4, v1, v16).reshape(D, HB, P, -1)
    A["kv_win"] = np.concatenate([keys(kw), values(vw)], 4).reshape(D, HB, P, -1)
    nph = cache_nsa_kv.shape[1]
    raw = cache_nsa_kv[:, :, :, 0:2].reshape(D, nph, 8, 8, 2, 2, KV, HD).transpose(0, 1, 4, 7, 5, 3, 6, 2)
    raw = raw.reshape(D, nph, P, 2, P)
    ks = cache_nsa_kv[:, :, :, 2].reshape(D, nph, PAGE, P).transpose(0, 1, 3, 2)[:, :, :, None]
    vs = cache_nsa_kv[:, :, :, 3].reshape(D, nph, PAGE, P)[:, :, :, None]
    A["pool"] = np.concatenate([raw, ks, vs], 3)
    A["page_table"] = page_table.reshape(1, REQ * PAGES)
    for n, z in (("dil1", cache_dil1_kv), ("dil4", cache_dil4_kv), ("dil16", cache_dil16_kv), ("win", cache_win_kv)):
        A["cache_" + n] = z.reshape(D, REQ, z.shape[2], 2 * P)
    return A


OUTS = {"y": (T, D_MODEL), "conv_state_out": (DEPTH, P, WT, 2 + 2 * REQ)}
for _n, _w in (("dil1", D1), ("dil4", D4), ("dil16", D16), ("win", WIN)):
    OUTS[f"new_{_n}_prompt"] = (DEPTH, min(_w, SEQ), 2 * P)
    OUTS[f"new_{_n}_sample"] = (DEPTH, REQ, _w, 2 * P)
OUTS["new_nsa_rows_prompt"] = (DEPTH, SEQ, 4 * P)
OUTS["new_nsa_rows_sample"] = (DEPTH, NS, 4 * P)


def kernel(**inputs):
    import concourse.bacc as bacc
    from concourse.bass_utils import run_bass_kernel_spmd

    arrays = layouts(**{k: np.asarray(v) for k, v in inputs.items()})
    arrays.update(constants())
    arrays = {"in_" + k: np.ascontiguousarray(v) for k, v in arrays.items()}
    nc = bacc.Bacc("TRN2", target_bir_lowering=False, num_devices=1)
    a = {k[3:]: nc.dram_tensor(k, v.shape, mybir.dt.from_np(v.dtype), kind="ExternalInput").ap()
         for k, v in arrays.items()}
    o = {k: nc.dram_tensor("out_" + k, shape, FP32, kind="ExternalOutput").ap() for k, shape in OUTS.items()}
    trunk_program(nc, a, o)
    res = run_bass_kernel_spmd(nc, [arrays], core_ids=[0]).results[0]
    r = {k: res["out_" + k] for k in OUTS}
    y = r["y"]
    state = r["conv_state_out"].transpose(0, 3, 2, 1).reshape(DEPTH, 2 + 2 * REQ, WIDTH)
    outs = [y[0:SEQ].reshape(1, SEQ, D_MODEL), y[SEQ:].reshape(REQ, NEW, D_MODEL)]
    for n in ("dil1", "dil4", "dil16", "win"):
        z = r[f"new_{n}_prompt"]
        outs.append(z.reshape(DEPTH, 1, z.shape[1], 2, KV, HD))
        z = r[f"new_{n}_sample"]
        outs.append(z.reshape(DEPTH, REQ, z.shape[2], 2, KV, HD))
    outs.append(np.ascontiguousarray(state[:, 0:2]).reshape(DEPTH, 1, 2, WIDTH))
    outs.append(np.ascontiguousarray(state[:, 2:]).reshape(DEPTH, REQ, 2, WIDTH))
    outs.append(r["new_nsa_rows_prompt"].reshape(DEPTH, 1, SEQ, 4, KV, HD))
    outs.append(r["new_nsa_rows_sample"].reshape(DEPTH, REQ, NEW, 4, KV, HD))
    return tuple(outs)
```

```python
import concourse.bass as bass
from concourse import mybir
from contextlib import ExitStack
import numpy as np

FP32 = mybir.dt.float32
BF16 = mybir.dt.bfloat16
I32 = mybir.dt.int32
R32 = mybir.dt.float32r
ALU = mybir.AluOpType
ACT = mybir.ActivationFunctionType
AX = mybir.AxisListType

P = 128
D_MODEL = 1024
KT = D_MODEL // P
DEPTH = 2
SEQ = 256
REQ = 8
NEW = 4
NS = REQ * NEW
T = SEQ + NS
PROMPT_STORES = 9
POOL_PAGES = 5
NEW_STORES = 6
PAST = 1024
PAGE = 128
PAGES = PAST // PAGE
HD = 64
HALF_ROT = 8
THETA = 500000.0
KV = 2
REP = 4
HEADS = KV * REP
EPS = 1e-6
NEG = -1e30
SCALE = HD ** -0.5
WIDTH = 512
WT = WIDTH // P
CMP_LEN, CMP_STRIDE, SLC = 32, 16, 64
NCP = (SEQ - CMP_LEN) // CMP_STRIDE + 1
NROW = (SEQ // 2 + 16) // 8
POS_ROW = SEQ // 2 // 8
NCS = (PAST - CMP_LEN) // CMP_STRIDE + 1
NBLK = PAST // SLC
NPH = (REQ * PAGES * 5) // 4
D1, D4, D16, WIN = 128, 512, 1024, 512
K16 = D16 // 16 * NEW
HB = 2
RB = REQ // HB
PARTS = (P, P, NS)
TOK0 = (0, P, 2 * P)
G_TOK = 7
KVC = 3 * 512
PAIRS = ("d1", "d4", "d16", "win", "cmp", "slc")
KCOL = {n: 256 * i for i, n in enumerate(PAIRS)}
VCOL = {n: 256 * i + P for i, n in enumerate(PAIRS)}
KTYPE = {"d1": 0, "d4": 1, "d16": 2, "win": 3, "slc": 4}
VCOL["slc"], KCOL["slc"] = 4 * 256 + 384, 4 * 256 + 256
A_TYPES = ("d1", "d4", "d16")
MIX = P + K16 + 3 * NS
S_MIX, S_WIN = D4, D4 + MIX
S_WNEW = S_WIN + WIN
S_SNEW = S_WNEW + NS
S_SLC = S_SNEW + NS
S_CMP = S_SLC + PAST
S_ALL = S_CMP + 64
MASK_COLS = dict(a=3 * 256, c=256, cmp0=256, cmp1=256, sd4=D4, smix0=MIX, smix1=MIX, swin=WIN,
                 smisc0=P, smisc1=P)


def mask_at():
    at, out = 0, {}
    for name, n in MASK_COLS.items():
        out[name] = (at, at + n)
        at += n
    return out, at


class Signal:

    def __init__(self, nc, name, keys, by=1):
        self.sem, self.by, self.name = nc.alloc_semaphore(name), by, name
        self.place = {k: i + 1 for i, k in enumerate(keys)}
        assert len(self.place) == len(keys), name
        self.raised = 0

    def inc(self, key):
        self.raised += 1
        assert self.place[key] == self.raised, (self.name, key)
        return self.sem, self.by

    def at(self, key):
        return self.sem, self.by * self.place[key]


class Ring:

    def __init__(self, nc, name, keys, n, by=1, parts=1, free=True, given=0):
        self.given = given
        self.n, self.by, self.parts, self.keys = n, by, parts, list(keys)
        self.place = {k: i for i, k in enumerate(keys)}
        assert len(self.place) == len(self.keys), name
        self.full = [nc.alloc_semaphore(f"{name}{b}_full") for b in range(n)]
        self.free = [nc.alloc_semaphore(f"{name}{b}_free") for b in range(n)] if free else None
        self.released = set()

    def buf(self, key):
        return self.place[key] % self.n

    def fill(self, key):
        return self.full[self.buf(key)], self.by

    def is_full(self, key):
        fills = self.place[key] // self.n + (self.buf(key) >= self.given)
        return self.full[self.buf(key)], self.by * self.parts * fills

    def release(self, key):
        assert key not in self.released, key
        self.released.add(key)
        return self.free[self.buf(key)], 1

    def is_free(self, key):
        return self.free[self.buf(key)], self.place[key] // self.n

    def is_used(self, key):
        return self.free[self.buf(key)], self.place[key] // self.n + 1

    def before(self, key):
        i = self.place[key] - self.n
        return self.keys[i] if i >= 0 else None


def wait(eng, sem_value):
    if sem_value[1] > 0:
        eng.wait_ge(*sem_value)



def prompt_units():
    units = []
    for qt in range(2):
        units += [("A", qt, h) for h in range(HEADS)]
    for qt in range(2):
        units += [("C", qt, h) for h in range(HEADS)]
    return units


FEATS = [("za", kt) for kt in range(WT)] + [(kind, kt) for kt in range(WT) for kind in ("h", "c", "b", "zb")] + \
        [("zc", kt) for kt in range(WT)]


def unit_banks(u):
    br, qt, _ = u
    n = P * (qt + 1)
    if br == "A":
        return [(0, 3 * P)] if qt == 0 else [(0, 512), (512, 256)]
    return [(0, 2 * n)]


def unit_chunks(u):
    br, qt, _ = u
    return [(t, kb) for t in (A_TYPES if br == "A" else ("win", "slc")) for kb in range(qt + 1)]


def steps():
    out = []
    def splits(item, *quarters):
        return [("split", item, q) for q in quarters]

    out += [("nm", tt) for tt in range(3)]
    for tt in range(3):
        out += [("xn", tt)] + splits(("tok", 0), tt)
    out += splits(("tok", 0), 3)
    toks = [(g, tt) for g in range(G_TOK) for tt in range(3)]
    for i, k in enumerate(toks):
        out.append(("tok",) + k)
        g, tt = k
        if k == (1, 0):
            out.append(("gsplit",))
        out += splits(("tok", g + 1), *((0, 1), (2,), (3,))[tt]) if g + 1 < G_TOK else \
            splits(("feat", 0), *((0,), (1,), ())[tt])
        if i >= 2:
            out.append(("turn",) + toks[i - 2])
    out += [("gc",)]
    out += [("turn",) + k for k in toks[-2:]] + [("gct",)]
    units, feats, late = prompt_units(), list(FEATS), []
    for i in range(len(units) + 2):
        if i < len(units):
            out += [("score", units[i]), ("exp", units[i])]
        out += late
        late = []
        if feats and i % 4 < 3:
            n = len(FEATS) - len(feats)
            out.append(("feat",) + feats.pop(0))
            if n + 2 < len(FEATS):
                out += splits(("feat", (n + 2) // 4), (n + 2) % 4)
        if 1 <= i <= len(units):
            out.append(("pturn", units[i - 1]))
        if i >= 2:
            u = units[i - 2]
            out.append(("pv", u))
            if u[2] == HEADS - 1:
                out.append(("out", u[0], u[1]))
                if u[0] == "A":
                    late = [("gateA", u[1])]
    out += [("ghid", 0), ("ghid", 1), ("ghidt", 0), ("ghidt", 1), ("gkc",), ("gvc",), ("gkt",), ("gates",)]
    out += [("cscore", 0), ("hid", 0, 0), ("cturn", 0), ("cpv", 0), ("cscore", 1), ("gateC", 0), ("hid", 0, 1),
            ("cturn", 1), ("cpv", 1), ("sscore", 0, "d4"), ("sscore", 0, "mix"), ("kc", 0), ("vc", 0),
            ("gateC", 1), ("kct", 0)]

    def weigh(hb, *whats):
        turns, products = ([(k, hb, w) for w in whats] for k in ("sturn", "spv"))
        pairs = [s for z in zip(turns[1:], products) for s in z]
        return turns[:1] + pairs + products[-1:]

    out += [("sexp", 0, "A"), ("sscore", 0, "win"), ("sscore", 0, "misc"),
            ("sexp", 0, "cmp"), ("sexp", 0, "win"), ("sturn", 0, "d4"), ("hid", 1, 0), ("cmpt", 0), ("spv", 0, "d4"),
            ("sturn", 0, "mix"), ("imp", 0), ("spv", 0, "mix"), ("hid", 1, 1), ("sturn", 0, "anew"), ("impsum", 0),
            ("spv", 0, "anew"), ("kc", 1), ("vc", 1), ("kct", 1),
            ("sturn", 0, "win"), ("soA", 0), ("spv", 0, "win"), ("sgateA", 0),
            ("sscore", 1, "d4"), ("sscore", 0, "slc0"), ("sscore", 0, "slc1"), ("drop", 0), ("sexp", 0, "slc"),
            ("sscore", 1, "mix")]
    selected = weigh(0, "cnew", "slc0", "slc1")
    out += selected[:4] + [("sexp", 1, "A")] + selected[4:]
    out += [("soC", 0)] + weigh(1, "d4") + [("sgateC", 0)] + weigh(1, "mix", "anew")
    out += [("sscore", 1, "win"), ("sscore", 1, "misc"), ("sexp", 1, "cmp"), ("sexp", 1, "win"), ("soA", 1),
            ("cmpt", 1), ("sscore", 1, "slc0"), ("imp", 1), ("sscore", 1, "slc1"), ("impsum", 1), ("sgateA", 1),
            ("drop", 1), ("sturn", 1, "win"), ("sexp", 1, "slc"), ("spv", 1, "win")]
    out += weigh(1, "cnew", "slc0", "slc1")
    out += [("soC", 1)] + splits(("gate", 0, 0), 0) + [("sgateC", 1)]
    out += splits(("gate", 0, 0), 1) + [("osplit", 0)] + splits(("up", 0, 0), 0, 1)
    items = [(fh, i) for fh in range(2) for i in range(3)]
    for j, (fh, i) in enumerate(items):
        for q in range(4):
            out += [("gate", fh, i, q)]
            ahead, q2 = divmod(4 * j + q + 2, 4)
            if ahead < 6:
                out += splits(("gate",) + items[ahead], q2)
            out += [("up", fh, i, q)]
            if ahead == 6:
                out += splits(("down", 0), 2 * q2, 2 * q2 + 1)
            if q == 1 and j < 2:
                out += [("osplit", j + 1)]
            if ahead < 6:
                out += splits(("up",) + items[ahead], q2)
    out += splits(("down", 1), 0, 1, 2, 3)
    out += [("down", nh, tt) for nh in range(2) for tt in range(3)]
    return out


def trunk_program(nc, a, o):
    STEPS = steps()
    UNITS = prompt_units()
    MASK, NMASK = mask_at()
    SBUF_BASE = -(-nc.sbuf_base // 32) * 32
    of = lambda *kinds: [s for s in STEPS if s[0] in kinds]

    place, row_end = {}, [0]

    def sb(name, shape, dt=FP32):
        place[name] = row_end[0]
        n = int(np.prod(shape[1:])) * (2 if dt == BF16 else 4)
        row_end[0] += -(-n // 32) * 32
        return nc.alloc_sbuf_tensor_at(name, shape, dt, offset=SBUF_BASE + place[name])

    def rounded(name, shape):
        return nc.alloc_sbuf_tensor_at(name + "_r", shape, R32, offset=SBUF_BASE + place[name])

    x = sb("x", [P, 3, D_MODEL])
    ident = sb("ident", [P, P])
    identb = sb("identb", [P, P], BF16)
    masks = sb("masks", [P, NMASK], BF16)
    rot_c = sb("rot_c", [P, 3, 16])
    rot_s = sb("rot_s", [P, 3, 16])
    blk_c = sb("blk_c", [64, 16])
    blk_s = sb("blk_s", [64, 16])
    overlap = sb("overlap", [64, NBLK + 1])
    same_q = sb("same_q", [P, P])
    pick = sb("pick", [NS, HB, P])
    row_head = sb("row_head", [P, HEADS])
    row_kv = sb("row_kv", [P, KV])
    n_pads = sb("n_pads", [P, 2])
    row_some = sb("row_some", [P, 1])
    number = sb("number", [P, NBLK])
    page_no = sb("page_no", [1, REQ * PAGES], I32)
    xnT = sb("xnT", [P, KT, T])
    xnT_high, xnT_low = rounded("x", [P, KT, T]), rounded("xnT", [P, KT, T])
    x_saved_at = nc.dram_tensor("x_saved_at", (T, D_MODEL), FP32, kind="Internal").ap()
    gT = sb("gT", [P, KT])
    big = [sb(f"big{i}", [P, 4096]) for i in range(3)]
    paged = [sb(f"paged{i}", [P, 2 * PAGES * 256]) for i in range(2)]
    kvp = sb("kvp", [P, 3, KVC])
    old = kvp[:, 0:2, :].rearrange("p t n -> p (t n)")
    hid = [old[:, 512 * i:512 * (i + 1)] for i in range(2)]
    hidp, hidt = old[:, 1024:1536], old[:, 1536:2048]
    hidb = old[:, 2048:2048 + 516]
    w_gc = sb("w_gc", [P, KT, 24])
    gct = sb("gct", [P, 3, 24])
    oT = [sb(f"oT_{m}", [P, WT, T]) for m in "abc"]
    long = sb("long", [P, 4096])
    qTA = long[:, 0:3 * REP * SEQ].rearrange("p (t r n) -> p t r n", t=3, r=REP)
    w1 = long[:, :].rearrange("p (k l n) -> p k l n", k=2, l=16)
    mT = long[:, 0:KT * T].rearrange("p (k n) -> p k n", k=KT)
    qTC = sb("qTC", [P, REP, SEQ])
    kT = sb("kT", [P, 5, SEQ])
    ktf = kT[:, :, :].rearrange("p t n -> p (t n)")
    kcs = ktf[0:64, 0:WIDTH]
    kTn = sb("kTn", [P, 5, NS])
    cT = sb("cT", [P, 2, KV, P + 16])
    vcs = [ktf[0:64, WIDTH:2 * WIDTH], cT[0:64, :, :, :].rearrange("p k g n -> p (k g n)")[:, 0:WIDTH]]
    ROWS = KV * NROW - 1
    hid_rows = hidb[0:ROWS, 0:2 * P].rearrange("p (k n) -> p k n", k=2)
    kcT = [z.rearrange("p (b n) -> p b n", b=RB) for z in (old[:, 2564:2820], ktf[:, 2 * WIDTH:2 * WIDTH + 256])]
    qblk = sb("qblk", [P, 4, HB, P])
    short = sb("short", [P, S_ALL + WIDTH])
    xn = short[:, 0:3 * D_MODEL].rearrange("p (t n) -> p t n", t=3)
    proj = short[:, 0:2048].rearrange("p (s n) -> p s n", s=4)
    prob = short[:, 0:1536].rearrange("p (s n) -> p s n", s=2)
    srow = short[:, 0:S_ALL]
    o_tmp = short[:, S_ALL:S_ALL + WIDTH]
    PT = sb("PT", [P, 2, 768])
    short_r, PT_r = rounded("short", [P, S_ALL + WIDTH]), rounded("PT", [P, WT, T])
    oT_high = [short_r[:, WT * T * i:WT * T * (i + 1)].rearrange("p (k n) -> p k n", k=WT) for i in range(2)] + \
        [PT_r[:, :, :]]
    gc_high, gc_low = short_r[:, 2048:2048 + KT * 24].rearrange("p (k n) -> p k n", k=KT), rounded("w_gc", [P, KT, 24])
    gcT = short[0:24, 2048 + KT * 24:2048 + KT * 24 + T]
    oT_low = [rounded(f"oT_{m}", [P, WT, T]) for m in "abc"]
    long_r, qTC_r = rounded("long", [P, 14, T]), rounded("qTC", [P, 2, T])
    m_low = [long_r[:, ft, :] for ft in range(KT)]
    m_high = [long_r[:, KT + ft, :] for ft in range(6)] + [qTC_r[:, i, :] for i in range(2)]
    big_r = [rounded(f"big{i}", [P, 4096]) for i in range(3)]
    paged_r = [rounded(f"paged{i}", [P, 4096]) for i in range(2)]
    kvp_r = rounded("kvp", [P, 2, 2048])
    o_sb = sb("o_sb", [P, 2, WIDTH])
    n_ext = SEQ + 2 + REQ * 6
    hsb, uext = long[:, 3072:3072 + T], long[:, 3360:3360 + n_ext]
    ysb = long[:, 3666:3666 + n_ext]
    ustate = sb("ustate", [P, WT, 2 + REQ * 2])
    ustart = sb("ustart", [P, WT, REQ, 2])
    conv_w = sb("conv_w", [P, WT, 3])
    tanh = sb("tanh", [P, 2, T])
    prod = sb("prod", [P, T])
    rtmp = sb("rtmp", [P, 2, 8, 16])
    w2 = sb("w2", [P, 2, HD])
    pe_c = sb("pe_c", [P, 2, 16])
    pe_b = sb("pe_b", [P, 2])
    kcp = sb("kcp", [NCP, P])
    kcz = sb("kcz", [P, KV, 32])
    vcz = prob[:, 1, 0:512]
    PTc = sb("PTc", [64, P])
    small = sb("small", [P, 256])

    def col(at, n=1):
        return small[:, at:at + n]

    ss, rn = col(0, 3), col(3, 3)
    mx = [col(8 + 4 * s, 4) for s in range(2)]
    nmx = [col(16 + 4 * s, 4) for s in range(2)]
    den = {("A", q): col(24 + 8 * q, 8) for q in range(2)} | {("C", q): col(40 + 16 * q, 16) for q in range(2)}
    cmx, cden, crec = col(72, 8), col(80, 8), col(88, 8)
    rec = col(96, 16)
    smx, sden, srec = col(112, 4), col(116, 4), col(120, 4)
    sg = [col(124 + 4 * h, 3) for h in range(HB)]
    scoef = col(132, 8)
    impt, impv = col(140, 17), col(157, 16)
    least, which, hitv, dropv = col(173), col(174), col(176, 16), col(192, 16)
    sgt = col(208, 24)
    wneg = [col(232 + 8 * q, 8) for q in range(2)]

    ps = [nc.alloc_psum_tensor(f"bank{i}", [P, 512], FP32) for i in range(8)]
    pj_keys = []
    tr_keys, sc_keys, o_keys, pt_keys = [], [], [], []
    for s in STEPS:
        k = s[0]
        if k in ("tok", "gc", "feat", "gkc", "gvc", "kc", "vc", "gate", "up", "down", "imp", "impsum"):
            pj_keys.append(s)
        if k == "gates":
            pj_keys += [("gates", 0), ("gates", 1)]
        if k == "ghid":
            pj_keys.append(s)
        if k == "hid":
            pj_keys += [s + (0,), s + (1,)]
        if k == "xn":
            tr_keys += [s + (0,), s + (1,)]
        if k in ("turn", "gct", "ghidt", "gkt", "cturn", "kct", "cmpt", "sturn", "gateA", "gateC", "sgateA", "sgateC"):
            tr_keys.append(s)
        if k == "pturn":
            tr_keys += [s + (j,) for j in range(-(-len(unit_chunks(s[1])) // 4))]
        if k == "score":
            sc_keys += [s + (j,) for j in range(len(unit_banks(s[1])))]
        if k in ("cscore", "sscore"):
            sc_keys.append(s)
        if k == "pv" and s[1][2] == 0:
            o_keys += [("o", "A", s[1][1])] if s[1][0] == "A" else [("o", "W", s[1][1]), ("o", "S", s[1][1])]
        if k == "cpv":
            o_keys.append(("o", "c", s[1]))
        if k == "spv" and s[2] in ("d4", "win"):
            o_keys.append(("o", "sA" if s[2] == "d4" else "sC", s[1]))
        if k in ("pturn",):
            pt_keys.append(s)
        if k in ("cturn", "sturn"):
            pt_keys.append(s)
    PJ = Ring(nc, "proj_bank", pj_keys, 2)
    TR = Ring(nc, "turn_bank", tr_keys, 2)
    SC = Ring(nc, "score_bank", sc_keys, 2)
    O = Ring(nc, "out_bank", o_keys, 2)
    PTR = Ring(nc, "probT", pt_keys, 2, free=False)
    pj = lambda k: ps[PJ.buf(k)]
    tr = lambda k: ps[2 + TR.buf(k)]
    sc = lambda k: ps[4 + SC.buf(k)]
    ob = lambda k: ps[6 + O.buf(k)]
    ptb = lambda k: PT[:, PTR.buf(k), :]

    big_keys = [("tok", g) for g in range(G_TOK)] + [("feat", i) for i in range(6)]
    for hb in range(HB):
        big_keys += [("kA", hb), ("win", hb), ("vA", hb)]
    BIG = Ring(nc, "big", big_keys, 3, by=16, free=False, given=1)
    gate_keys = [("gate", fh, i) for fh in range(2) for i in range(3)] + [("down", nh) for nh in range(2)]
    up_keys = [("up", fh, i) for fh in range(2) for i in range(3)]
    GW = Ring(nc, "gate_weights", gate_keys, 2, by=16, free=False)
    UW = Ring(nc, "up_weights", up_keys, 2, by=16, free=False)
    loads = list(big_keys)
    for gk, uk in zip(gate_keys, up_keys):
        loads += [gk, uk]
    loads += gate_keys[-2:]

    def ring_of(k):
        return GW if k in gate_keys else UW if k in up_keys else BIG

    def bigb(k, big=big):
        if k in gate_keys:
            return big[GW.buf(k)][:, :]
        if k in up_keys:
            return big[2][:, 2048 * UW.buf(k):2048 * (UW.buf(k) + 1)]
        return big[(BIG.buf(k) + 2) % 3][:, :]

    def low(k):
        return bigb(k, big_r)

    def place_used_by(k):
        if ring_of(k).before(k):
            return ring_of(k).before(k)
        if k in gate_keys or k in up_keys:
            buf = GW.buf(k) if k in gate_keys else 2
            return [b for b in big_keys if (BIG.buf(b) + 2) % 3 == buf][-1]
        return None

    split_keys = [k for k in big_keys if k[0] in ("tok", "feat")]

    def high(k):
        if k in up_keys:
            return kvp_r[:, UW.buf(k), :]
        return paged_r[(gate_keys.index(k) if k in gate_keys else split_keys.index(k) + 1) % 2][:, :]

    def split_part(z, k, q):
        if k[0] in ("tok", "down"):
            return z[:, 1024 * q:1024 * (q + 1)]
        return z.rearrange("p (k n) -> p k n", n=512)[:, :, P * q:P * (q + 1)]

    def high_used_by(k):
        for keys in (gate_keys, up_keys, split_keys):
            if k in keys:
                return keys[keys.index(k) - 2] if keys.index(k) >= 2 else None
    page_keys = [(kind, hb, bp) for kind in ("cmp", "slc") for hb in range(HB) for bp in range(2)]
    PAGE_SHARE = [range(0, POOL_PAGES), range(POOL_PAGES, 2 * PAGES)]
    PG = [Ring(nc, f"pages_{who}", page_keys, 2, by=16, parts=len(share), free=False)
          for who, share in zip(("pool", "sp"), PAGE_SHARE)]
    pgb = lambda k: paged[PG[0].buf(k)][:, :].rearrange("p (b g k n) -> p b g k n", b=2, g=PAGES, k=2)

    sig = lambda name, keys, by=1: Signal(nc, name, keys, by)
    layer_in = sig("layer_in", ["all"], 16 * 6)
    w1_in = sig("w1_in", ["all"], 16)
    squares = sig("squares_done", list(range(3)))
    mean = sig("mean_done", list(range(3)))
    root = sig("root_done", list(range(3)))
    normed = sig("normed", list(range(3)))
    x_saved = sig("x_saved", ["all"], 16 * 3)
    next_in = sig("next_weights_in", ["all"], 16)
    x_back = sig("x_back", ["all"], 16 * 3)
    xn_split = sig("xn_split", list(range(3)))
    high_done = sig("weights_rounded", [s[1] + (s[2],) for s in of("split")])
    split_done = sig("weights_split", [s[1] + (s[2],) for s in of("split")])
    gc_split = sig("gate_weights_split", ["all"])
    o_split = sig("outputs_split", list(range(3)))
    roped = sig("roped", [s[1:] for s in of("tok")])
    tanh_done = sig("tanh_done", [s for s in of("feat") if s[1][0] == "z"])
    u_state = sig("conv_state_ready", ["all"])
    maxed = sig("max_ready", UNITS)
    expd = sig("probs_ready", UNITS)
    c_normed = sig("mixer_c_normed", [("W", 0), ("W", 1), ("c", 0), ("c", 1)])
    hid_tanh = sig("hidden_tanh", of("ghidt", "hid"))
    hid_done = sig("hidden_ready", of("ghidt", "hid"))
    pad_exp = sig("pad_weight_ready", [0, 1])
    zeroed = sig("blocks_zeroed", ["all"])
    kc_done = sig("kc_roped", ["p", 0, 1])
    cexpd = sig("cmp_probs_ready", [0, 1])
    smaxed = sig("row_max_ready", [s[1:] for s in of("sexp")])
    sexpd = sig("row_probs_ready", [s[1:] for s in of("sexp")])
    cnormed = sig("cmp_probs_normed", [0, 1])
    so_done = sig("rows_out_ready", of("soA", "soC"))
    merged = sig("merged", [s[1:] for s in of("up") if s[2]])
    pv_done = sig("values_weighted", [s for s in of("pv", "spv")
                                      if not (s[0] == "pv" and s[1][2] == HEADS - 1) and s[2:] not in (("anew",), ("slc1",))])
    dchain = nc.alloc_semaphore("dve_link")
    stored, stored_new = nc.alloc_semaphore("prompt_stored"), nc.alloc_semaphore("new_stored")
    copied = nc.alloc_semaphore("caches_copied")
    per_layer = range(PJ.full[0].num, copied.num + 1)
    x_in, first_in, const_in, late_in = [
        nc.alloc_semaphore(n) for n in ("residual_in", "first_weights_in", "constants_in", "late_constants_in")]
    set_up = nc.alloc_semaphore("set_up")
    y_squares, y_mean, y_root, y_link, y_ready, y_out = [
        nc.alloc_semaphore(n) for n in ("y_squares", "y_mean", "y_root", "y_link", "y_ready", "y_out")]

    tanhs = [s for s in STEPS if s[0] == "gate" or (s[0] == "feat" and s[1][0] == "z")]
    tanh_slot = {s: i % 2 for i, s in enumerate(tanhs)}

    def turned(g, tt):
        return TR.is_used(("turn", g, tt))

    def tanh_free(s):
        i = tanhs.index(s)
        if i < 2:
            return None
        before = tanhs[i - 2]
        return PJ.is_used(before if before[0] == "feat" else ("up",) + before[1:])

    def n_turns(u):
        return -(-len(unit_chunks(u)) // 4)

    def pt_full(key):
        return TR.is_used(key + (n_turns(key[1]) - 1,) if key[0] == "pturn" else key)

    def pt_used(key):
        if key[0] == "cturn":
            return O.is_full(("o", "c", key[1]))
        if key[0] == "pturn":
            br, qt, h = key[1]
            if h == HEADS - 1:
                return O.is_full(("o", "A" if br == "A" else "S", qt))
            return pv_done.at(("pv", key[1]))
        if key[2] in ("anew", "slc1"):
            return O.is_full(("o", "sA" if key[2] == "anew" else "sC", key[1]))
        return pv_done.at(("spv",) + key[1:])

    def pt_free(key):
        before = PTR.before(key)
        return pt_used(before) if before else (None, 0)

    def big_used(key):
        kind = key[0]
        if kind == "tok":
            return PJ.is_full(("tok", key[1], 2))
        if kind == "feat":
            return PJ.is_full(("feat",) + FEATS[4 * key[1] + 3])
        if kind == "kA":
            return SC.is_full(("sscore", key[1], "mix"))
        if kind == "win":
            return pv_done.at(("spv", key[1], "win"))
        if kind == "vA":
            return pv_done.at(("spv", key[1], "mix"))
        if kind in ("gate", "up"):
            return PJ.is_full(key + (3,))
        return PJ.is_full(("down", key[1], 2))

    def pages_used(key):
        kind, hb, _ = key
        return PJ.is_full(("hid", hb, 1, 1)) if kind == "cmp" else O.is_full(("o", "sC", hb))

    SROWS = {"d4": (("A",), [(P * c, P) for c in range(4)]),
             "mix": ((), [(S_MIX + P * c, P) for c in range(3)]),
             "anew": ((), [(S_MIX + P + K16 + NS * t, NS) for t in range(3)]),
             "win": (("win",), [(S_WIN + P * c, P) for c in range(4)]),
             "cnew": (("slc",), [(S_WNEW, NS), (S_SNEW, NS)]),
             "slc0": ((), [(S_SLC + P * c, P) for c in range(4)]),
             "slc1": ((), [(S_SLC + 512 + P * c, P) for c in range(4)])}
    SOFT = {"A": (0, 0, S_WIN, "mix"), "cmp": (1, S_CMP, 64, "misc"), "win": (2, S_WIN, WIN + NS, "misc"),
            "slc": (3, S_SNEW, NS + PAST, "slc1")}

    def conv_window(y):
        return y[:, SEQ + 2:SEQ + 2 + 6 * REQ].rearrange("p (b t) -> p b t", t=6)

    CONSTS = [(ident[:, :], a["ident"]), (rot_c[:, :, :], a["rot_c"]), (rot_s[:, :, :], a["rot_s"])]
    LATE = [(page_no[:, :], a["page_table"]), (identb[:, :], a["identb"]), (masks[:, :], a["masks"]),
            (blk_c[:, :], a["blk_c"]), (blk_s[:, :], a["blk_s"]), (overlap[:, :], a["overlap"]),
            (same_q[:, :], a["same_q"]), (pick[:, :, :], a["pick"]), (row_head[:, :], a["row_head"]),
            (row_kv[:, :], a["row_kv"]), (row_some[:, :], a["row_some"]), (n_pads[:, :], a["n_pads"]), (number[:, :], a["number"])]

    with nc.Block() as block:
        @block.sync
        def _(sp):
            for tt in range(3):
                sp.dma_start(x[0:PARTS[tt], tt, :], a["x"][TOK0[tt]:TOK0[tt] + PARTS[tt], :]).then_inc(x_in, 16)
            sp.dma_start(bigb(("tok", 0)), a["w_first"][0]).then_inc(first_in, 16)
            for dst, src in CONSTS:
                sp.dma_start(dst, src).then_inc(const_in, 16)

        @block.scalar
        def _(act):
            for dst, src in LATE:
                act.dma_start(dst, src).then_inc(late_in, 16)

        @block.vector
        def _(dve):
            nc.vector.memset(qblk[:, :, :, :], 0.0).then_inc(set_up, 1)
            nc.vector.memset(kcz[:, :, :], 0.0).then_inc(set_up, 1)
            dve.wait_ge(set_up, 2)

    with nc.Fori(0, DEPTH) as layer:
        def page_numbers(queue, key, z):
            _, hb, bp = key
            queue.wait_ge(late_in, 16 * len(LATE))
            at = (hb * RB + bp * 2) * PAGES
            return [queue.value_load(page_no[0:1, at + i:at + i + 1], min_val=0, max_val=NPH - 1)
                    for i in PAGE_SHARE[z]]

        def load_pages(queue, keys, z):
            numbers = [page_numbers(queue, key, z) for key in keys]
            for key, pages in zip(keys, numbers):
                load_numbered(queue, key, z, pages)

        def load_numbered(queue, key, z, numbers):
            kind, hb, bp = key
            before = PG[z].before(key)
            queue.wait_ge(*(pages_used(before) if before else big_used(split_keys[PG[z].buf(key) - 2])))
            k0 = 0 if kind == "cmp" else 2
            for i, page in zip(PAGE_SHARE[z], numbers):
                b, g = divmod(i, PAGES)
                src = a["pool"][layer, bass.ds(page, 1), :, k0:k0 + 2, :]
                queue.dma_start(pgb(key)[:, b, g, :, :], src.rearrange("a p k n -> (a p) k n"))\
                    .then_inc(*PG[z].fill(key))

        with nc.Block() as block:

            @block.sync
            def _(sp):
                for tt in range(3):
                    if tt == 0:
                        sp.wait_ge(x_in, 16 * 3)
                    sp.dma_start(x_saved_at[TOK0[tt]:TOK0[tt] + PARTS[tt], :], x[0:PARTS[tt], tt, :])\
                        .then_inc(x_saved.sem, 16)
                for dst, src in ((gT[:, :], a["norm_g"][layer]), (w_gc[:, :, :], a["w_gc"][layer]),
                                 (conv_w[:, :, :], a["conv_w"][layer]), (ustart[:, :, :, :], a["conv_state"][layer]),
                                 (w2[:, :, :], a["w2"][layer]), (pe_c[:, :, :], a["cmp_pe"][layer])):
                    sp.dma_start(dst, src).then_inc(layer_in.sem, 16)
                n_copies = 0
                copies = [(n, b) for n in ("dil1", "dil4", "dil16", "win") for b in range(REQ)]

                def copy_cache(name, b):
                    old, new = a["cache_" + name], o["new_" + name + "_sample"]
                    n = old.shape[2]
                    src = old[layer, b, NEW:n, :].rearrange("n c -> (n c)").rearrange("(s e) -> s e", s=16)
                    dst = new[layer, b, 0:n - NEW, :].rearrange("n c -> (n c)").rearrange("(s e) -> s e", s=16)
                    sp.dma_start(dst, src).then_inc(copied, 16)

                for key in loads[1:]:
                    place_of_pages = {("win", 0): 0, ("kA", 1): 2, ("win", 1): 4, ("gate", 0, 0): 6}
                    if key in place_of_pages:
                        load_pages(sp, page_keys[place_of_pages[key]:place_of_pages[key] + 2], 1)
                    if place_used_by(key):
                        sp.wait_ge(*big_used(place_used_by(key)))
                    buf, kind = bigb(key), key[0]
                    if kind == "tok":
                        dst, src = buf[:, :], a["w_tok"][layer, key[1]]
                    elif kind == "feat":
                        dst, src = buf[:, :], a["w_feat"][layer, key[1]]
                    elif kind == "kA":
                        dst, src = buf[:, 0:RB * 896], a["k_a"][layer, key[1]]
                    elif kind == "vA":
                        dst, src = buf[:, 0:RB * 896], a["v_a"][layer, key[1]]
                    elif kind == "win":
                        dst, src = buf[:, :], a["kv_win"][layer, key[1]]
                    elif kind == "gate":
                        dst, src = buf[:, :], a["w_gate"][layer, key[1], key[2]]
                    elif kind == "up":
                        dst, src = buf, a["w_up"][layer, key[1], key[2]]
                    else:
                        dst, src = buf[:, :], a["w_out"][layer, key[1]]
                    sp.dma_start(dst, src).then_inc(*ring_of(key).fill(key))
                    if key == ("kA", 0):
                        sp.wait_ge(*expd.at(("A", 1, HEADS - 1)))
                        sp.wait_ge(*PJ.is_used(("feat", "b", WT - 1)))
                        sp.dma_start(long[:, :], a["w1"][layer]).then_inc(*w1_in.inc("all"))
                    if n_copies < len(copies) and key not in (("tok", 0), ("tok", 1)):
                        for _ in range(2):
                            if n_copies < len(copies):
                                copy_cache(*copies[n_copies])
                                n_copies += 1
                assert n_copies == len(copies)
                sp.wait_ge(*x_saved.at("all"))
                sp.wait_ge(*PJ.is_full(("gate", 1, 2, 3)))
                for tt in range(3):
                    sp.dma_start(x[0:PARTS[tt], tt, :], x_saved_at[TOK0[tt]:TOK0[tt] + PARTS[tt], :])\
                        .then_inc(x_back.sem, 16)
                sp.wait_ge(*PJ.is_full(("up", 1, 2, 3)))
                sp.dma_start(bigb(("tok", 0)), a["w_first"][layer + 1]).then_inc(*next_in.inc("all"))
                sp.wait_ge(*next_in.at("all"))
                sp.wait_ge(copied, 16 * n_copies)

            @block.gpsimd
            def _(pool):
                n_stores = 0

                def store(dst, src, done=stored_new):
                    pool.dma_start(dst, src).then_inc(done, 16)
                    return 1

                pool.wait_ge(*roped.at((G_TOK - 1, 2)))
                for tt in range(2):
                    rows = slice(tt * P, (tt + 1) * P)
                    if tt == 1:
                        n_stores += store(o["new_dil1_prompt"][layer], kvp[:, tt, 0:256], stored)
                    n_stores += store(o["new_dil4_prompt"][layer, rows, :], kvp[:, tt, 256:512], stored)
                    n_stores += store(o["new_dil16_prompt"][layer, rows, :], kvp[:, tt, 512:768], stored)
                    n_stores += store(o["new_win_prompt"][layer, rows, :], kvp[:, tt, 768:1024], stored)
                    n_stores += store(o["new_nsa_rows_prompt"][layer, rows, :], kvp[:, tt, 1024:1536], stored)
                assert n_stores == PROMPT_STORES
                n_new = 0
                for name, c in (("dil1", 0), ("dil4", 256), ("dil16", 512), ("win", 768)):
                    new = o["new_" + name + "_sample"]
                    n = new.shape[2]
                    n_new += store(new[layer, :, n - NEW:n, :], kvp[0:NS, 2, c:c + 256])
                n_new += store(o["new_nsa_rows_sample"][layer], kvp[0:NS, 2, 1024:1536])
                load_pages(pool, page_keys[0:1], 0)
                pool.wait_ge(*u_state.at("all"))
                n_new += store(o["conv_state_out"][layer], ustate[:, :, :])
                load_pages(pool, page_keys[1:2], 0)
                for i in (2, 4, 6):
                    load_pages(pool, page_keys[i:i + 2], 0)
                for key in page_keys[-2:]:
                    pool.wait_ge(*PG[0].is_full(key))
                pool.wait_ge(stored, 16 * PROMPT_STORES)
                assert n_new == NEW_STORES
                pool.wait_ge(stored_new, 16 * NEW_STORES)

            @block.tensor
            def _(pe):
                mm = nc.tensor.matmul

                def precise(out, lhs, rhs, n, weights=None, quarter=None):
                    if quarter is not None:
                        pe.wait_ge(*split_done.at(weights + (quarter,)))
                    for c in range(n):
                        if quarter is None and 4 * c % n == 0:
                            pe.wait_ge(*split_done.at(weights + (4 * c // n,)))
                        (lh, ll), (rh, rl) = lhs(c), rhs(c)
                        for i, (l, r) in enumerate(((lh, rh), (lh, rl), (ll, rh))):
                            last = mm(out, l, r, start=(c == 0 and i == 0), stop=(c == n - 1 and i == 2))
                    return last

                def parts_of(key):
                    n = WT if key in up_keys else KT
                    return [z.rearrange("p (k n) -> p k n", k=n) for z in (high(key), low(key))]

                pe.wait_ge(const_in, 16 * len(CONSTS))

                def transposes(key, parts):
                    wait(pe, TR.is_free(key))
                    for i, (out, in_) in enumerate(parts):
                        n = in_.shape[0]
                        last = nc.tensor.transpose(out, in_, ident[0:n, 0:n])
                    last.then_inc(*TR.fill(key))

                for s in STEPS:
                    k = s[0]
                    if k == "xn":
                        tt = s[1]
                        n = PARTS[tt]
                        pe.wait_ge(*normed.at(tt))
                        for hf in range(2):
                            bank = tr(s + (hf,))[:, 0:4 * n].rearrange("p (c t) -> p c t", c=4)
                            transposes(s + (hf,), [(bank[:, c, :], xn[0:n, tt, (4 * hf + c) * P:(4 * hf + c + 1) * P])
                                                   for c in range(4)])
                    elif k == "tok":
                        g, tt = s[1:]
                        n = PARTS[tt]
                        wait(pe, PJ.is_free(s))
                        tokens = slice(TOK0[tt], TOK0[tt] + n)
                        pe.wait_ge(*xn_split.at(tt))
                        wh, wl = parts_of(("tok", g))
                        precise(pj(s)[0:n, :], lambda c: (xnT_high[:, c, tokens], xnT_low[:, c, tokens]),
                                lambda c: (wh[:, c, :], wl[:, c, :]), KT, ("tok", g)).then_inc(*PJ.fill(s))
                    elif k == "gc":
                        wait(pe, PJ.is_free(s))
                        pe.wait_ge(*gc_split.at("all"))
                        for c in range(KT):
                            for i, (w, part) in enumerate(((gc_high, xnT_high), (gc_high, xnT_low),
                                                           (gc_low, xnT_high))):
                                last = mm(pj(s)[0:24, 0:T], w[:, c, :], part[:, c, :],
                                          start=(c == 0 and i == 0), stop=(c == KT - 1 and i == 2))
                        last.then_inc(*PJ.fill(s))
                    elif k == "gct":
                        pe.wait_ge(*PJ.is_used(("gc",)))
                        transposes(s, [(tr(s)[0:PARTS[tt], 32 * tt:32 * tt + 24],
                                        gcT[:, TOK0[tt]:TOK0[tt] + PARTS[tt]]) for tt in range(3)])
                    elif k == "turn":
                        g, tt = s[1:]
                        n = PARTS[tt]
                        pe.wait_ge(*roped.at((g, tt)))
                        if g < 4:
                            src = proj[0:n, (3 * g + tt) % 4, :]
                            cols = [P * r for r in range(REP)]
                        else:
                            src = kvp[0:n, tt, :]
                            cols = {4: [KCOL["d1"], KCOL["d4"]], 5: [KCOL["d16"], KCOL["win"]],
                                    6: [KCOL["slc"], 1024, 1024 + P] if tt < 2 else [KCOL["slc"]]}[g]
                        transposes(s, [(tr(s)[:, n * i:n * (i + 1)], src[:, c:c + P]) for i, c in enumerate(cols)])
                    elif k == "feat":
                        i = FEATS.index(s[1:])
                        item = ("feat", i // 4)
                        wait(pe, PJ.is_free(s))
                        wh, wl = parts_of(item)
                        cols = slice(P * (i % 4), P * (i % 4 + 1))
                        precise(pj(s)[:, 0:T], lambda c: (wh[:, c, cols], wl[:, c, cols]),
                                lambda c: (xnT_high[:, c, :], xnT_low[:, c, :]), KT, item, i % 4).then_inc(*PJ.fill(s))
                    elif k == "score":
                        u = s[1]
                        br, qt, h = u
                        g, r = divmod(h, REP)
                        q0 = qt * P
                        nk = P * (qt + 1)
                        if u == UNITS[0]:
                            pe.wait_ge(late_in, 16 * len(LATE))
                        if h == 0:
                            for gq in range(4):
                                pe.wait_ge(*turned(gq, qt))
                            for gk in (4, 5, 6):
                                pe.wait_ge(*turned(gk, qt))
                        for j, (c0, cols) in enumerate(unit_banks(u)):
                            key = s + (j,)
                            wait(pe, SC.is_free(key))
                            for z in range(cols // nk):
                                m1 = MASK["a"][0] + 256 * (c0 // nk + z + 1) if br == "A" else MASK["c"][1]
                                mm(sc(key)[:, z * nk:(z + 1) * nk], identb[:, :], masks[:, m1 - nk:m1],
                                   start=(z == 0), stop=False, skip_group_check=True)
                            types = [t for t in ((0, 1, 2) if br == "A" else (3, 4))]
                            for i, t in enumerate(types):
                                if c0 <= i * nk < c0 + cols:
                                    q = qTA[HD * g:HD * (g + 1), t, r, q0:q0 + P] if br == "A" else \
                                        qTC[HD * g:HD * (g + 1), r, q0:q0 + P]
                                    last = mm(sc(key)[:, i * nk - c0:(i + 1) * nk - c0], q,
                                              kT[HD * g:HD * (g + 1), t, 0:nk], start=False, stop=True,
                                              skip_group_check=True)
                            last.then_inc(*SC.fill(key))
                    elif k == "pturn":
                        u = s[1]
                        slot = UNITS.index(u) % 2
                        pe.wait_ge(*expd.at(u))
                        chunks = unit_chunks(u)
                        for j in range(n_turns(u)):
                            idx = range(4 * j, min(4 * j + 4, len(chunks)))
                            transposes(s + (j,), [(tr(s + (j,))[:, P * (i - 4 * j):P * (i - 4 * j + 1)],
                                                   prob[:, slot, P * i:P * (i + 1)]) for i in idx])
                    elif k == "pv":
                        u = s[1]
                        br, qt, h = u
                        g = h // REP
                        pkey = ("pturn", u)
                        pe.wait_ge(*pt_full(pkey))
                        chunks = unit_chunks(u)
                        for which_o, types in (("A", A_TYPES),) if br == "A" else (("W", ("win",)), ("S", ("slc",))):
                            okey = ("o", which_o, qt)
                            if h == 0:
                                wait(pe, O.is_free(okey))
                            mine = [i for i, (t, _) in enumerate(chunks) if t in types]
                            for i in mine:
                                t, kb = chunks[i]
                                last = mm(ob(okey)[:, HD * h:HD * (h + 1)], ptb(pkey)[:, P * i:P * (i + 1)],
                                          kvp[:, kb, VCOL[t] + HD * g:VCOL[t] + HD * (g + 1)],
                                          start=(i == mine[0]), stop=(i == mine[-1]))
                            if h == HEADS - 1:
                                last.then_inc(*O.fill(okey))
                            elif which_o != "W":
                                last.then_inc(*pv_done.inc(s))
                    elif k in ("gateA", "gateC"):
                        qt = s[1]
                        pe.wait_ge(*(O.is_used(("o", "A", qt)) if k == "gateA" else c_normed.at(("c", qt))))
                        transposes(s, [(tr(s)[:, P * c:P * (c + 1)], o_sb[:, qt, P * c:P * (c + 1)])
                                       for c in range(WT)])
                    elif k == "ghid":
                        kind = s[1]
                        if kind == 0:
                            pe.wait_ge(*w1_in.at("all"))
                            pe.wait_ge(*TR.is_used(("turn", 6, 1)))
                        wait(pe, PJ.is_free(s))
                        for l in range(16):
                            pairs = cT[:, kind, :, :].rearrange("p g n -> p (g n)")
                            last = mm(pj(s)[0:ROWS, 0:P], pairs[:, l:l + 8 * (ROWS - 1) + 1:8],
                                      w1[:, kind, l, :], start=(l == 0), stop=(l == 15))
                        last.then_inc(*PJ.fill(s))
                    elif k == "ghidt":
                        kind = s[1]
                        pe.wait_ge(*PJ.is_used(("ghid", kind)))
                        transposes(s, [(tr(s)[:, 0:ROWS], hid_rows[:, kind, :])])
                    elif k in ("gkc", "gvc"):
                        kind = 0 if k == "gkc" else 1
                        pe.wait_ge(*hid_done.at(("ghidt", kind)))
                        wait(pe, PJ.is_free(s))
                        for g in range(KV):
                            last = mm(pj(s)[0:NCP, HD * g:HD * (g + 1)],
                                      hid[kind][:, NCP * g:NCP * (g + 1)],
                                      w2[:, kind, :], start=True, stop=True)
                        last.then_inc(*PJ.fill(s))
                    elif k == "gkt":
                        pe.wait_ge(*kc_done.at("p"))
                        transposes(s, [(tr(s)[:, 0:NCP], kcp[:, :])])
                    elif k == "gates":
                        pe.wait_ge(*TR.is_used(("gct",)))
                        for hb in range(HB):
                            wait(pe, PJ.is_free(("gates", hb)))
                            mm(pj(("gates", hb))[:, 0:24], pick[:, hb, :], gct[0:NS, 2, :], start=True, stop=True)\
                                .then_inc(*PJ.fill(("gates", hb)))
                    elif k == "cscore":
                        qt = s[1]
                        wait(pe, SC.is_free(s))
                        pe.wait_ge(*TR.is_used(("gkt",)))
                        m0, m1 = MASK["cmp%d" % qt]
                        mm(sc(s)[:, 0:256], identb[:, :], masks[:, m0:m1], start=True, stop=False,
                           skip_group_check=True)
                        both = sc(s)[:, 0:256].rearrange("p (g r n) -> p r g n", g=KV, r=REP)
                        for r in range(REP):
                            last = mm(both[:, r, :, :], qTC[:, r, qt * P:(qt + 1) * P], kcz[:, :, :], start=False,
                                      stop=True, skip_group_check=True)
                        last.then_inc(*SC.fill(s))
                    elif k == "cturn":
                        pe.wait_ge(*cexpd.at(s[1]))
                        transposes(s, [(tr(s)[:, P * i:P * (i + 1)], prob[:, 0, P * i:P * (i + 1)])
                                       for i in range(2)])
                    elif k == "cpv":
                        qt = s[1]
                        okey, pkey = ("o", "c", qt), ("cturn", qt)
                        pe.wait_ge(*pt_full(pkey))
                        pe.wait_ge(*PJ.is_used(("gvc",)))
                        wait(pe, O.is_free(okey))
                        for g in range(KV):
                            last = mm(ob(okey)[:, 256 * g:256 * (g + 1)], ptb(pkey)[:, P * g:P * (g + 1)],
                                      vcz[:, 256 * g:256 * (g + 1)], start=True, stop=True)
                        last.then_inc(*O.fill(okey))
                    elif k == "hid":
                        _, hb, kind = s
                        for part in range(2):
                            key = s + (part,)
                            wait(pe, PJ.is_free(key))
                            for bp in range(2):
                                for z in range(2):
                                    pe.wait_ge(*PG[z].is_full(("cmp", hb, bp)))
                                pages = pgb(("cmp", hb, bp)).rearrange("p b g k (l n) -> p (b g) k l n", l=8)
                                for l in range(8):
                                    last = mm(pj(key)[:, 256 * bp:256 * (bp + 1)], w1[:, kind, 8 * part + l, :],
                                              pages[:, :, kind, l, :], start=(l == 0), stop=(l == 7))
                            last.then_inc(*PJ.fill(key))
                    elif k in ("kc", "vc"):
                        hb, kind = s[1], 0 if k == "kc" else 1
                        pe.wait_ge(*hid_done.at(("hid", hb, kind)))
                        wait(pe, PJ.is_free(s))
                        for b in range(RB):
                            for g in range(KV):
                                last = mm(pj(s)[0:64, P * b + HD * g:P * b + HD * (g + 1)],
                                          hid[kind][:, 256 * g + 64 * b:256 * g + 64 * (b + 1)], w2[:, kind, :],
                                          start=True, stop=True)
                        last.then_inc(*PJ.fill(s))
                    elif k == "kct":
                        pe.wait_ge(*kc_done.at(s[1]))
                        transposes(s, [(tr(s)[:, 64 * b:64 * (b + 1)], kcs[:, P * b:P * (b + 1)]) for b in range(RB)])
                    elif k == "sscore":
                        _, hb, what = s
                        wait(pe, SC.is_free(s))
                        if what in ("d4", "mix"):
                            pe.wait_ge(*BIG.is_full(("kA", hb)))
                            keys = bigb(("kA", hb))[:, 0:RB * 896].rearrange("p (b n) -> p b n", b=RB)
                        elif what == "win":
                            pe.wait_ge(*BIG.is_full(("win", hb)))
                            keys = bigb(("win", hb))[:, :].rearrange("p (b n) -> p b n", b=RB)
                        bank = sc(s)

                        def q(t, b=None):
                            return qblk[:, t, hb, :] if b is None else qblk[:, t, hb, 32 * b:32 * (b + 1)]

                        def mask(name, cols):
                            m0 = MASK[name][0]
                            mm(bank[:, 0:cols], identb[:, :], masks[:, m0:m0 + cols], start=True, stop=False,
                               skip_group_check=True)

                        def add(out, qs, ks):
                            return mm(out, qs, ks, start=False, stop=True, skip_group_check=True)

                        if what == "d4":
                            mask("sd4", D4)
                            for b in range(RB):
                                last = add(bank[32 * b:32 * (b + 1), :], q(1, b), keys[:, b, 0:D4])
                        elif what == "mix":
                            mask("smix%d" % hb, MIX)
                            for b in range(RB):
                                add(bank[32 * b:32 * (b + 1), 0:P], q(0, b), keys[:, b, D4:D4 + P])
                                add(bank[32 * b:32 * (b + 1), P:P + K16], q(2, b), keys[:, b, D4 + P:D4 + P + K16])
                            for t in range(3):
                                last = add(bank[:, P + K16 + NS * t:P + K16 + NS * (t + 1)], q(t), kTn[:, t, :])
                        elif what == "win":
                            mask("swin", WIN)
                            for b in range(RB):
                                last = add(bank[32 * b:32 * (b + 1), :], q(3, b), keys[:, b, 0:WIN])
                        elif what == "misc":
                            pe.wait_ge(*TR.is_used(("kct", hb)))
                            mask("smisc%d" % hb, P)
                            add(bank[:, 0:NS], q(3), kTn[:, 3, :])
                            add(bank[:, NS:2 * NS], q(3), kTn[:, 4, :])
                            for b in range(RB):
                                last = add(bank[32 * b:32 * (b + 1), 64:64 + NCS], q(3, b), kcT[hb][:, b, 0:NCS])
                        else:
                            z = int(what[-1])
                            for b in range(RB):
                                pkey = ("slc", hb, b // 2)
                                for pg in PG:
                                    pe.wait_ge(*pg.is_full(pkey))
                                last = mm(bank[32 * b:32 * (b + 1), :].rearrange("p (g n) -> p g n", g=4),
                                          q(3, b), pgb(pkey)[:, b % 2, 4 * z:4 * z + 4, 0, :], start=True, stop=True)
                        last.then_inc(*SC.fill(s))
                    elif k == "cmpt":
                        hb = s[1]
                        pe.wait_ge(*cnormed.at(hb))
                        transposes(s, [(tr(s)[0:64, 0:P], srow[:, S_CMP:S_CMP + 64])])
                    elif k == "imp":
                        hb = s[1]
                        pe.wait_ge(*TR.is_used(("cmpt", hb)))
                        wait(pe, PJ.is_free(s))
                        mm(pj(s)[:, 0:NBLK + 1], PTc[0:NCS, :], overlap[0:NCS, :], start=True, stop=True)\
                            .then_inc(*PJ.fill(s))
                    elif k == "impsum":
                        hb = s[1]
                        pe.wait_ge(*PJ.is_used(("imp", hb)))
                        wait(pe, PJ.is_free(s))
                        mm(pj(s)[:, 0:NBLK + 1], same_q[:, :], impt, start=True, stop=True).then_inc(*PJ.fill(s))
                    elif k == "sturn":
                        _, hb, what = s
                        branch, parts = SROWS[what]
                        for br in branch:
                            pe.wait_ge(*sexpd.at((hb, br)))
                        outs, at = [], 0
                        for c0, n in parts:
                            outs.append((tr(s)[0:n, at:at + P], srow[:, c0:c0 + n]))
                            at += P
                        transposes(s, outs)
                    elif k == "spv":
                        _, hb, what = s
                        okey = ("o", "sA", hb) if what in ("d4", "mix", "anew") else ("o", "sC", hb)
                        pkey = ("sturn", hb, what)
                        if what in ("d4", "win"):
                            wait(pe, O.is_free(okey))
                        pe.wait_ge(*pt_full(pkey))
                        pt, out = ptb(pkey), ob(okey)
                        if what in ("d4", "mix"):
                            pe.wait_ge(*BIG.is_full(("vA", hb)))
                            vals = bigb(("vA", hb))[:, 0:RB * 896].rearrange("p (b c n) -> p b c n", b=RB, c=7)
                            n, c0 = (4, 0) if what == "d4" else (3, 4)
                            for b in range(RB):
                                for c in range(n):
                                    last = mm(out[32 * b:32 * (b + 1), 0:P], pt[:, P * c + 32 * b:P * c + 32 * (b + 1)],
                                              vals[:, b, c0 + c, :], start=(what == "d4" and c == 0), stop=False,
                                              skip_group_check=True)
                        elif what == "anew":
                            for t, name in enumerate(A_TYPES):
                                last = mm(out[:, 0:P], pt[0:NS, P * t:P * (t + 1)],
                                          kvp[0:NS, 2, VCOL[name]:VCOL[name] + P], start=False, stop=True,
                                          skip_group_check=True)
                        elif what == "win":
                            vals = bigb(("win", hb))[:, :].rearrange("p (b c n) -> p b c n", b=RB, c=8)
                            for b in range(RB):
                                for c in range(4):
                                    last = mm(out[32 * b:32 * (b + 1), 0:P], pt[:, P * c + 32 * b:P * c + 32 * (b + 1)],
                                              vals[:, b, 4 + c, :], start=(c == 0), stop=False, skip_group_check=True)
                        elif what == "cnew":
                            pe.wait_ge(*PJ.is_used(("vc", hb)))
                            mm(out[:, 0:P], pt[0:NS, 0:P], kvp[0:NS, 2, VCOL["win"]:VCOL["win"] + P], start=False,
                               stop=True, skip_group_check=True)
                            for b in range(RB):
                                mm(out[32 * b:32 * (b + 1), 2 * P:3 * P], PTc[0:NCS, 32 * b:32 * (b + 1)],
                                   vcs[hb][0:NCS, P * b:P * (b + 1)], start=True, stop=True, skip_group_check=True)
                            last = mm(out[:, P:2 * P], pt[0:NS, P:2 * P], kvp[0:NS, 2, VCOL["slc"]:VCOL["slc"] + P],
                                      start=True, stop=False, skip_group_check=True)
                        else:
                            z = int(what[-1])
                            for b in range(RB):
                                for c in range(4):
                                    last = mm(out[32 * b:32 * (b + 1), P:2 * P],
                                              pt[:, P * c + 32 * b:P * c + 32 * (b + 1)],
                                              pgb(("slc", hb, b // 2))[:, b % 2, 4 * z + c, 1, :], start=False,
                                              stop=(z == 1 and c == 3), skip_group_check=True)
                        last.then_inc(*(O.fill(okey) if what in ("anew", "slc1") else pv_done.inc(s)))
                    elif k in ("sgateA", "sgateC"):
                        hb = s[1]
                        pe.wait_ge(*so_done.at(("so" + k[-1], hb)))
                        transposes(s, [(tr(s)[:, 0:P], o_sb[:, 0, 0:P])])
                    elif k == "gate":
                        _, fh, i, q4 = s
                        wait(pe, PJ.is_free(s))
                        wh, wl = parts_of(("gate", fh, i))
                        cols = slice(P * q4, P * (q4 + 1))
                        precise(pj(s)[:, 0:T], lambda c: (wh[:, c, cols], wl[:, c, cols]),
                                lambda c: (xnT_high[:, c, :], xnT_low[:, c, :]), KT, ("gate", fh, i), q4)\
                            .then_inc(*PJ.fill(s))
                    elif k == "up":
                        _, fh, i, q4 = s
                        pe.wait_ge(*o_split.at(i))
                        wait(pe, PJ.is_free(s))
                        wh, wl = parts_of(("up", fh, i))
                        cols = slice(P * q4, P * (q4 + 1))
                        precise(pj(s)[:, 0:T], lambda c: (wh[:, c, cols], wl[:, c, cols]),
                                lambda c: (oT_high[i][:, c, :], oT_low[i][:, c, :]), WT, ("up", fh, i), q4)\
                            .then_inc(*PJ.fill(s))
                    elif k == "down":
                        _, nh, tt = s
                        n = PARTS[tt]
                        if nh == 0 and tt == 0:
                            pe.wait_ge(*merged.at((1, 2, 3)))
                        wait(pe, PJ.is_free(s))
                        wh, wl = parts_of(("down", nh))
                        tokens = slice(TOK0[tt], TOK0[tt] + n)
                        precise(pj(s)[0:n, :], lambda c: (m_high[c][:, tokens], m_low[c][:, tokens]),
                                lambda c: (wh[:, c, :], wl[:, c, :]), KT, ("down", nh)).then_inc(*PJ.fill(s))

            @block.scalar
            def _(act):
                f = nc.scalar.activation
                f(col(248), kcz[:, 0, 31:32], ACT.Sqrt)
                for s in STEPS:
                    k = s[0]
                    if k == "nm":
                        tt = s[1]
                        n = PARTS[tt]
                        if tt == 0:
                            act.wait_ge(x_in, 16 * 3)
                        f(xn[0:n, tt, :], x[0:n, tt, :], ACT.Square, accum_out=ss[0:n, tt:tt + 1])\
                            .then_inc(*squares.inc(tt))
                        act.wait_ge(*mean.at(tt))
                        f(rn[0:n, tt:tt + 1], ss[0:n, tt:tt + 1], ACT.Sqrt).then_inc(*root.inc(tt))
                    elif k == "tok":
                        g, tt = s[1:]
                        n = PARTS[tt]
                        act.wait_ge(*PJ.is_full(s))
                        i = 3 * g + tt
                        if g < 4:
                            if i >= 4:
                                act.wait_ge(*TR.is_full(("turn",) + divmod(i - 4, 3)))
                            dst = proj[0:n, i % 4, :]
                        else:
                            dst = kvp[0:n, tt, 512 * (g - 4):512 * (g - 3)]
                        f(dst, pj(s)[0:n, :], ACT.Copy).then_inc(*PJ.release(s))
                    elif k == "turn":
                        g, tt = s[1:]
                        if g >= 4:
                            continue
                        n = PARTS[tt]
                        act.wait_ge(*TR.is_full(s))
                        if tt < 2:
                            dst = qTA[:, g, :, tt * P:(tt + 1) * P] if g < 3 else qTC[:, :, tt * P:(tt + 1) * P]
                            f(dst, tr(s)[:, :].rearrange("p (r n) -> p r n", r=REP), ACT.Copy, scale=SCALE)\
                                .then_inc(*TR.release(s))
                        else:
                            for kv in range(KV):
                                rows = slice(HD * kv, HD * (kv + 1))
                                src = tr(s)[rows, 0:REP * NS].rearrange("p (r b t) -> p b r t", r=REP, b=REQ)
                                dst = qblk[rows, g, :, :].rearrange("p h (b k r t) -> p (h b) k r t", b=RB, k=KV, r=REP)
                                last = f(dst[:, :, kv, :, :], src, ACT.Copy, scale=SCALE)
                            last.then_inc(*TR.release(s))
                    elif k == "split":
                        item, q = s[1:]
                        if item == loads[0]:
                            act.wait_ge(first_in, 16)
                        else:
                            act.wait_ge(*ring_of(item).is_full(item))
                        if high_used_by(item):
                            act.wait_ge(*big_used(high_used_by(item)))
                        if item in (("gate", 0, 0), ("gate", 0, 1), ("up", 0, 0), ("up", 0, 1)):
                            act.wait_ge(*O.is_full(("o", "sC", 1)))
                            act.wait_ge(stored_new, 16 * NEW_STORES)
                        f(split_part(high(item), item, q), split_part(bigb(item), item, q), ACT.Copy)\
                            .then_inc(*high_done.inc(item + (q,)))
                    elif k == "gc":
                        act.wait_ge(*PJ.is_full(s))
                        f(gcT, pj(s)[0:24, 0:T], ACT.Tanh, scale=0.5).then_inc(*PJ.release(s))
                    elif k == "feat":
                        kind, kt = s[1:]
                        if kind == "h":
                            act.wait_ge(*PJ.is_full(s))
                            if kt:
                                act.wait_ge(*PJ.is_used(("feat", "c", kt - 1)))
                            f(hsb[:, :], pj(s)[:, 0:T], ACT.Copy).then_inc(*PJ.release(s))
                        elif kind[0] == "z":
                            act.wait_ge(*PJ.is_full(s))
                            if tanh_free(s):
                                act.wait_ge(*tanh_free(s))
                            f(tanh[:, tanh_slot[s], :], pj(s)[:, 0:T], ACT.Tanh, scale=0.5)\
                                .then_inc(*tanh_done.inc(s))
                    elif k == "exp":
                        u = s[1]
                        slot = UNITS.index(u) % 2
                        br, qt, h = u
                        act.wait_ge(*maxed.at(u))
                        nk = P * (qt + 1)
                        if br == "A":
                            f(prob[:, slot, 0:3 * nk], prob[:, slot, 0:3 * nk], ACT.Exp, bias=nmx[slot][:, 0:1],
                              accum_out=den[br, qt][:, h:h + 1]).then_inc(*expd.inc(u))
                        else:
                            for z in range(2):
                                bias = wneg[qt][:, h:h + 1] if z == 0 else nmx[slot][:, 0:1]
                                last = f(prob[:, slot, z * nk:(z + 1) * nk], prob[:, slot, z * nk:(z + 1) * nk],
                                         ACT.Exp, bias=bias,
                                         accum_out=den[br, qt][:, 8 * z + h:8 * z + h + 1])
                            last.then_inc(*expd.inc(u))
                            if h == HEADS - 1:
                                act.wait_ge(*expd.at(u))
                                f(wneg[qt], wneg[qt], ACT.Exp).then_inc(*pad_exp.inc(qt))
                    elif k == "pturn":
                        u = s[1]
                        chunks = unit_chunks(u)
                        wait(act, pt_free(s))
                        for j in range(n_turns(u)):
                            key = s + (j,)
                            cols = P * (min(4 * j + 4, len(chunks)) - 4 * j)
                            act.wait_ge(*TR.is_full(key))
                            f(ptb(s)[:, 512 * j:512 * j + cols], tr(key)[:, 0:cols], ACT.Copy)\
                                .then_inc(*TR.release(key))
                    elif k == "ghid":
                        if s[1] == 0:
                            act.wait_ge(*O.is_full(("o", "S", 1)))
                            act.wait_ge(stored, 16 * PROMPT_STORES)
                        act.wait_ge(*PJ.is_full(s))
                        f(hid_rows[:, s[1], :], pj(s)[0:ROWS, 0:P], ACT.Copy).then_inc(*PJ.release(s))
                    elif k in ("ghidt", "hid"):
                        act.wait_ge(*(TR.is_used(s) if k == "ghidt" else PJ.is_used(s + (0,))))
                        cols = KV * NCP if k == "ghidt" else 512
                        f(hidt[:, 0:cols], hidp[:, 0:cols], ACT.Tanh, scale=0.5).then_inc(*hid_tanh.inc(s))
                    elif k in ("gkc", "kc"):
                        act.wait_ge(*PJ.is_full(s))
                        dst, src = (kcp[:, :], pj(s)[0:NCP, 0:P]) if k == "gkc" else (kcs[:, :], pj(s)[0:64, :])
                        f(dst, src, ACT.Copy, scale=0.5).then_inc(*PJ.release(s))
                    elif k == "vc":
                        act.wait_ge(*PJ.is_full(s))
                        f(vcs[s[1]], pj(s)[0:64, :], ACT.Copy, scale=0.5).then_inc(*PJ.release(s))
                    elif k == "gvc":
                        act.wait_ge(*PJ.is_full(s))
                        act.wait_ge(*zeroed.at("all"))
                        blocks = vcz.rearrange("p (g j d) -> p g j d", g=KV, j=REP)
                        for j in range(REP):
                            last = f(blocks[32 * j:32 * j + NCP, :, j, :],
                                     pj(s)[0:NCP, 0:P].rearrange("p (g d) -> p g d", g=KV), ACT.Copy, scale=0.5)
                        last.then_inc(*PJ.release(s))
                    elif k == "cscore":
                        qt = s[1]
                        act.wait_ge(*SC.is_used(s))
                        f(prob[:, 0, 0:256], prob[:, 0, 0:256], ACT.Exp).then_inc(*cexpd.inc(qt))
                    elif k in ("cturn", "sturn"):
                        act.wait_ge(*TR.is_full(s))
                        wait(act, pt_free(s))
                        if k == "cturn":
                            f(ptb(s)[:, 0:256], tr(s)[:, 0:256], ACT.Copy).then_inc(*TR.release(s))
                        else:
                            parts = SROWS[s[2]][1]
                            n, cols = parts[0][1], P * len(parts)
                            f(ptb(s)[0:n, 0:cols], tr(s)[0:n, 0:cols], ACT.Copy).then_inc(*TR.release(s))
                    elif k == "sscore":
                        _, hb, what = s
                        act.wait_ge(*SC.is_full(s))
                        c0, n = {"d4": (0, D4), "mix": (S_MIX, MIX), "win": (S_WIN, WIN), "slc0": (S_SLC, 512),
                                 "slc1": (S_SLC + 512, 512), "misc": (S_WNEW, 2 * NS)}[what]
                        last = f(srow[:, c0:c0 + n], sc(s)[:, 0:n], ACT.Copy)
                        if what == "misc":
                            last = f(srow[:, S_CMP:S_CMP + 64], sc(s)[:, 64:128], ACT.Copy)
                        last.then_inc(*SC.release(s))
                    elif k == "sexp":
                        _, hb, what = s
                        i, c0, n, _ = SOFT[what]
                        act.wait_ge(*smaxed.at((hb, what)))
                        f(srow[:, c0:c0 + n], srow[:, c0:c0 + n], ACT.Exp, bias=smx[:, i:i + 1],
                          accum_out=sden[:, i:i + 1]).then_inc(*sexpd.inc((hb, what)))
                    elif k == "cmpt":
                        act.wait_ge(*TR.is_full(s))
                        f(PTc[:, :], tr(s)[0:64, 0:P], ACT.Copy).then_inc(*TR.release(s))
                    elif k == "gate":
                        act.wait_ge(*PJ.is_full(s))
                        act.wait_ge(*tanh_free(s))
                        f(tanh[:, tanh_slot[s], :], pj(s)[:, 0:T], ACT.Tanh, scale=0.5).then_inc(*PJ.release(s))

            @block.vector
            def _(dve):
                n_link = [0]

                def link(ins):
                    n_link[0] += 1
                    ins.then_inc(dchain, 1)
                    dve.wait_ge(dchain, n_link[0])

                v = nc.vector

                def split(high, low, full):
                    link(v.tensor_copy(high, full))
                    return v.tensor_tensor(low, full, high.bitcast(FP32), ALU.subtract)

                def rope(rows, src, dst, tc, ts, mid):
                    shape = [rows] + mid + [16]
                    half = [rows] + mid + [8]
                    names = "abc"[:len(mid)]
                    ta = rtmp[0:rows, 0, 0:int(np.prod(mid)), :]
                    tb = rtmp[0:rows, 1, 0:int(np.prod(mid)), :]
                    if len(mid) == 2:
                        ta = ta.rearrange("p (a b) n -> p a b n", a=mid[0])
                        tb = tb.rearrange("p (a b) n -> p a b n", a=mid[0])

                    def bc(t, sh):
                        for _ in mid:
                            t = t.unsqueeze(1)
                        return t.to_broadcast(sh)

                    v.tensor_tensor(ta, src[..., 0:16], bc(tc, shape), ALU.mult)
                    v.tensor_tensor(tb[..., 0:8], src[..., 8:16], bc(ts[:, 0:8], half), ALU.mult)
                    link(v.tensor_tensor(tb[..., 8:16], src[..., 0:8], bc(ts[:, 8:16], half), ALU.mult))
                    return v.tensor_tensor(dst[..., 0:16], ta, tb, ALU.add)

                for s in STEPS:
                    k = s[0]
                    if k == "nm":
                        tt = s[1]
                        n = PARTS[tt]
                        if tt == 0:
                            dve.wait_ge(x_in, 16 * 3)
                            dve.wait_ge(first_in, 16)
                            dve.wait_ge(const_in, 16 * len(CONSTS))
                        dve.wait_ge(*squares.at(tt))
                        v.tensor_scalar(ss[0:n, tt:tt + 1], ss[0:n, tt:tt + 1], 1.0 / D_MODEL, EPS, ALU.mult,
                                        ALU.add).then_inc(*mean.inc(tt))
                        dve.wait_ge(*root.at(tt))
                        link(v.reciprocal(rn[0:n, tt:tt + 1], rn[0:n, tt:tt + 1]))
                        v.tensor_scalar(xn[0:n, tt, :], x[0:n, tt, :], rn[0:n, tt:tt + 1], None, ALU.mult)\
                            .then_inc(*normed.inc(tt))
                    elif k == "xn":
                        tt = s[1]
                        n = PARTS[tt]
                        if tt == 0:
                            dve.wait_ge(*layer_in.at("all"))
                            dve.wait_ge(*normed.at(2))
                            dve.wait_ge(*x_saved.at("all"))
                        for hf in range(2):
                            key = s + (hf,)
                            dve.wait_ge(*TR.is_full(key))
                            v.tensor_tensor(xnT[:, 4 * hf:4 * hf + 4, TOK0[tt]:TOK0[tt] + n],
                                            tr(key)[:, 0:4 * n].rearrange("p (c t) -> p c t", c=4),
                                            gT[:, 4 * hf:4 * hf + 4].unsqueeze(2).to_broadcast([P, 4, n]), ALU.mult)\
                                .then_inc(*TR.release(key))
                            dve.wait_ge(*TR.is_used(key))
                        tokens = slice(TOK0[tt], TOK0[tt] + n)
                        split(xnT_high[:, :, tokens], xnT_low[:, :, tokens], xnT[:, :, tokens]).then_inc(*xn_split.inc(tt))
                    elif k == "split":
                        item, q = s[1:]
                        h_part, l_part, full = (split_part(z, item, q) for z in (high(item), low(item), bigb(item)))
                        dve.wait_ge(*high_done.at(item + (q,)))
                        v.tensor_tensor(l_part, full, h_part.bitcast(FP32), ALU.subtract)\
                            .then_inc(*split_done.inc(item + (q,)))
                    elif k == "gsplit":
                        split(gc_high, gc_low[:, :, :], w_gc[:, :, :]).then_inc(*gc_split.inc("all"))
                    elif k == "gct":
                        dve.wait_ge(*TR.is_full(s))
                        both = tr(s)[:, 0:64].rearrange("p (t n) -> p t n", t=2)
                        v.tensor_copy(gct[:, 0:2, :], both[:, :, 0:24])
                        v.tensor_copy(gct[0:NS, 2, :], tr(s)[0:NS, 64:88]).then_inc(*TR.release(s))
                    elif k == "osplit":
                        i = s[1]
                        dve.wait_ge(*O.is_full(("o", "sC", 1)))
                        dve.wait_ge(*TR.is_used(("sgateC", 1)))
                        split(oT_high[i], oT_low[i][:, :, :], oT[i][:, :, :]).then_inc(*o_split.inc(i))
                    elif k == "tok":
                        g, tt = s[1:]
                        n = PARTS[tt]
                        dve.wait_ge(*PJ.is_used(s))
                        if (g, tt) != (0, 0):
                            dve.wait_ge(*roped.at((g, tt - 1) if tt else (g - 1, 2)))
                        tc, ts = rot_c[0:n, tt, :], rot_s[0:n, tt, :]
                        if g < 4:
                            view = proj[0:n, (3 * g + tt) % 4, :].rearrange("p (h d) -> p h d", h=8)
                            last = rope(n, view, view, tc, ts, [8])
                        elif g < 6:
                            view = kvp[0:n, tt, 512 * (g - 4):512 * (g - 3)]\
                                .rearrange("p (j z h d) -> p j z h d", j=2, z=2, h=KV)[:, :, 0, :, :]
                            last = rope(n, view, view, tc, ts, [2, KV])
                        else:
                            view = kvp[0:n, tt, KCOL["slc"]:KCOL["slc"] + P].rearrange("p (h d) -> p h d", h=KV)
                            last = rope(n, view, view, tc, ts, [KV])
                        last.then_inc(*roped.inc((g, tt)))
                    elif k == "turn":
                        g, tt = s[1:]
                        if g < 4:
                            continue
                        n = PARTS[tt]
                        dve.wait_ge(*TR.is_full(s))
                        t0 = 2 * (g - 4)
                        nt = 2 if g < 6 else 1
                        dst = kT[:, t0:t0 + nt, tt * P:(tt + 1) * P] if tt < 2 else kTn[:, t0:t0 + nt, :]
                        last = v.tensor_copy(dst, tr(s)[:, 0:nt * n].rearrange("p (t n) -> p t n", t=nt))
                        if g == 6 and tt == 0:
                            for kv in range(KV):
                                v.tensor_copy(cT[:, :, kv, P:P + 16], pe_c[:, :, :])
                        if g == 6 and tt < 2:
                            for kv in range(KV):
                                for par in range(2):
                                    src = tr(s)[HD * kv:HD * (kv + 1), P:3 * P]\
                                        .rearrange("p (k n z) -> p k n z", k=2, z=2)[:, :, :, par]
                                    last = v.tensor_copy(cT[HD * par:HD * (par + 1), :, kv, 64 * tt:64 * (tt + 1)], src)
                        last.then_inc(*TR.release(s))
                    elif k == "feat":
                        kind, kt = s[1:]
                        if kind == "h":
                            if kt == 0:
                                dve.wait_ge(*layer_in.at("all"))
                                v.memset(uext[:, 0:2], 0.0)
                            v.tensor_copy(uext[:, SEQ + 2:].rearrange("p (b t) -> p b t", t=6)[:, :, 0:2],
                                          ustart[:, kt, :, :])
                            continue
                        dve.wait_ge(*PJ.is_full(s))
                        un = uext[:, SEQ + 2:].rearrange("p (b t) -> p b t", t=6)
                        if kind == "c":
                            dve.wait_ge(*PJ.is_used(("feat", "h", kt)))
                            v.tensor_tensor(uext[:, 2:SEQ + 2], pj(s)[:, 0:SEQ], hsb[:, 0:SEQ], ALU.mult)
                            v.tensor_tensor(un[:, :, 2:6], pj(s)[:, SEQ:T].rearrange("p (b t) -> p b t", t=NEW),
                                            hsb[:, SEQ:T].rearrange("p (b t) -> p b t", t=NEW), ALU.mult)\
                                .then_inc(*PJ.release(s))
                            dve.wait_ge(*PJ.is_used(s))
                            m = SEQ + REQ * 6
                            link(v.tensor_scalar(ysb[:, 0:m], uext[:, 0:m], conv_w[:, kt, 0:1], None, ALU.mult))
                            link(v.scalar_tensor_tensor(ysb[:, 0:m], uext[:, 1:m + 1], conv_w[:, kt, 1:2], ysb[:, 0:m],
                                                        ALU.mult, ALU.add))
                            link(v.scalar_tensor_tensor(ysb[:, 0:m], uext[:, 2:m + 2], conv_w[:, kt, 2:3], ysb[:, 0:m],
                                                        ALU.mult, ALU.add))
                            v.tensor_copy(ustate[:, kt, 0:2], uext[:, SEQ:SEQ + 2])
                            last = v.tensor_copy(ustate[:, kt, 2:].rearrange("p (b t) -> p b t", t=2), un[:, :, 4:6])
                            if kt == WT - 1:
                                last.then_inc(*u_state.inc("all"))
                        elif kind == "b":
                            v.tensor_tensor(prod[:, 0:SEQ], pj(s)[:, 0:SEQ], ysb[:, 0:SEQ], ALU.mult)
                            v.tensor_tensor(prod[:, SEQ:T].rearrange("p (b t) -> p b t", t=NEW),
                                            pj(s)[:, SEQ:T].rearrange("p (b t) -> p b t", t=NEW),
                                            conv_window(ysb)[:, :, 0:NEW], ALU.mult).then_inc(*PJ.release(s))
                        elif kind == "zb":
                            dve.wait_ge(*tanh_done.at(s))
                            tn = tanh[:, tanh_slot[s], :]
                            v.scalar_tensor_tensor(o_tmp[:, 0:T], tn, 1.0, pj(s)[:, 0:T], ALU.add, ALU.mult)\
                                .then_inc(*PJ.release(s))
                            dve.wait_ge(*PJ.is_used(s))
                            link(v.tensor_tensor(oT[1][:, kt, :], o_tmp[:, 0:T], prod[:, :], ALU.mult))
                        else:
                            dve.wait_ge(*tanh_done.at(s))
                            tn = tanh[:, tanh_slot[s], :]
                            v.scalar_tensor_tensor(oT[0 if kind == "za" else 2][:, kt, :], tn, 1.0, pj(s)[:, 0:T],
                                                   ALU.add, ALU.mult).then_inc(*PJ.release(s))
                    elif k == "score":
                        u = s[1]
                        br, qt, h = u
                        i = UNITS.index(u)
                        slot = i % 2
                        if i >= 2:
                            u2 = UNITS[i - 2]
                            dve.wait_ge(*TR.is_full(("pturn", u2, n_turns(u2) - 1)))
                        nk = P * (qt + 1)
                        if br == "A":
                            for j, (c0, cols) in enumerate(unit_banks(u)):
                                key = s + (j,)
                                dve.wait_ge(*SC.is_full(key))
                                v.tensor_scalar(prob[:, slot, c0:c0 + cols], sc(key)[:, 0:cols], 0.0, -3e38, ALU.add,
                                                ALU.max, accum_out=mx[slot][:, j:j + 1]).then_inc(*SC.release(key))
                            dve.wait_ge(*SC.is_used(key))
                            if j:
                                dve.wait_ge(*SC.is_used(s + (0,)))
                                v.tensor_scalar(nmx[slot][:, 0:1], mx[slot][:, 0:1], mx[slot][:, 1:2], -1.0, ALU.max,
                                                ALU.mult).then_inc(*maxed.inc(u))
                            else:
                                v.tensor_scalar(nmx[slot][:, 0:1], mx[slot][:, 0:1], -1.0, None, ALU.mult)\
                                    .then_inc(*maxed.inc(u))
                        else:
                            key = s + (0,)
                            dve.wait_ge(*SC.is_full(key))
                            for z in range(2):
                                last = v.tensor_scalar(prob[:, slot, z * nk:(z + 1) * nk],
                                                       sc(key)[:, z * nk:(z + 1) * nk], 0.0, -3e38, ALU.add, ALU.max,
                                                       accum_out=mx[slot][:, z:z + 1])
                            last.then_inc(*SC.release(key))
                            dve.wait_ge(*SC.is_used(key))
                            v.tensor_scalar(wneg[qt][:, h:h + 1], mx[slot][:, 0:1], -1.0, 0.0, ALU.mult, ALU.min)
                            v.tensor_scalar(nmx[slot][:, 0:1], mx[slot][:, 1:2], -1.0, None, ALU.mult)\
                                .then_inc(*maxed.inc(u))
                    elif k == "out":
                        _, br, qt = s
                        d8 = [P, HEADS, HD]
                        nden = 8 if br == "A" else 16
                        dve.wait_ge(*O.is_full(("o", "A" if br == "A" else "S", qt)))
                        dve.wait_ge(late_in, 16 * len(LATE))
                        if br == "C":
                            dve.wait_ge(*pad_exp.at(qt))
                            link(v.scalar_tensor_tensor(den[br, qt][:, 0:8], wneg[qt], n_pads[:, qt:qt + 1],
                                                        den[br, qt][:, 0:8], ALU.mult, ALU.add))
                        link(v.reciprocal(rec[:, 0:nden], den[br, qt]))
                        view = o_sb[:, qt, :].rearrange("p (h d) -> p h d", h=HEADS)
                        if br == "A":
                            dve.wait_ge(*O.is_full(("o", "A", qt)))
                            v.tensor_tensor(view, ob(("o", "A", qt))[:, :].rearrange("p (h d) -> p h d", h=HEADS),
                                            rec[:, 0:8].unsqueeze(2).to_broadcast(d8), ALU.mult)\
                                .then_inc(*O.release(("o", "A", qt)))
                        else:
                            dve.wait_ge(*TR.is_used(("gct",)))
                            link(v.tensor_scalar(rec[:, 0:16], rec[:, 0:16], 0.5, None, ALU.mult))
                            for z, b3 in ((0, 2), (1, 1)):
                                last = v.scalar_tensor_tensor(rec[:, 8 * z:8 * z + 8], gct[:, qt, 8 * b3:8 * b3 + 8],
                                                              1.0, rec[:, 8 * z:8 * z + 8], ALU.add, ALU.mult)
                            link(last)
                            tmp = o_tmp[:, :].rearrange("p (h d) -> p h d", h=HEADS)
                            dve.wait_ge(*TR.is_full(("gateA", qt)))
                            for z, key in ((0, ("o", "W", qt)), (1, ("o", "S", qt))):
                                dve.wait_ge(*O.is_full(key))
                                v.tensor_tensor(view if z == 0 else tmp,
                                                ob(key)[:, :].rearrange("p (h d) -> p h d", h=HEADS),
                                                rec[:, 8 * z:8 * z + 8].unsqueeze(2).to_broadcast(d8), ALU.mult)\
                                    .then_inc(*O.release(key))
                                dve.wait_ge(*O.is_used(key))
                            v.tensor_tensor(o_sb[:, qt, :], o_sb[:, qt, :], o_tmp[:, :], ALU.add)\
                                .then_inc(*c_normed.inc(("W", qt)))
                    elif k in ("gateA", "gateC"):
                        qt = s[1]
                        o_t = oT[0] if k == "gateA" else oT[2]
                        dve.wait_ge(*TR.is_full(s))
                        part = o_t[:, :, qt * P:(qt + 1) * P]
                        dve.wait_ge(*PJ.is_used(("feat", "za" if k == "gateA" else "zc", WT - 1)))
                        v.tensor_tensor(part, tr(s)[:, :].rearrange("p (c n) -> p c n", c=WT), part, ALU.mult)\
                            .then_inc(*TR.release(s))
                    elif k == "ghid":
                        if s[1] == 0:
                            dve.wait_ge(*TR.is_full(("pturn", UNITS[-1], n_turns(UNITS[-1]) - 1)))
                            v.memset(vcz, 0.0).then_inc(*zeroed.inc("all"))
                    elif k == "ghidt":
                        kind = s[1]
                        dve.wait_ge(*TR.is_full(s))
                        n = KV * NCP
                        link(v.tensor_copy(pe_b[:, kind:kind + 1], tr(s)[:, POS_ROW:POS_ROW + 1]))
                        if kind == 0:
                            dve.wait_ge(*O.is_full(("o", "S", 1)))
                            dve.wait_ge(stored, 16 * PROMPT_STORES)
                            v.memset(hidb[:, 512:516], 0.0)
                        else:
                            dve.wait_ge(*hid_done.at(("ghidt", 0)))
                        v.tensor_scalar(hidp[:, 0:n].rearrange("p (g n) -> p g n", g=KV),
                                        tr(s)[:, 0:KV * NROW].rearrange("p (g n) -> p g n", g=KV)[:, :, 0:NCP],
                                        pe_b[:, kind:kind + 1], None, ALU.add).then_inc(*TR.release(s))
                        dve.wait_ge(*hid_tanh.at(s))
                        v.scalar_tensor_tensor(hid[kind][:, 0:n], hidt[:, 0:n], 1.0, hidp[:, 0:n], ALU.add, ALU.mult)\
                            .then_inc(*hid_done.inc(s))
                    elif k == "hid":
                        _, hb, kind = s
                        ka, kb = s + (0,), s + (1,)
                        sv = lambda key: pj(key)[:, :].rearrange("p (m g i) -> p m g i", g=KV, i=8)
                        dve.wait_ge(*PJ.is_full(kb))
                        before = of("ghidt", "hid")
                        dve.wait_ge(*hid_done.at(before[before.index(s) - 1]))
                        for g in range(KV):
                            last = v.tensor_copy(hidb[:, 256 * g:256 * (g + 1)].rearrange("p (m i) -> p m i", i=8),
                                                 sv(kb)[:, :, g, :])
                        last.then_inc(*PJ.release(kb))
                        dve.wait_ge(*PJ.is_used(kb))
                        dve.wait_ge(*PJ.is_full(ka))
                        for g in range(KV):
                            last = v.scalar_tensor_tensor(
                                hidp[:, 256 * g:256 * (g + 1)].rearrange("p (m i) -> p m i", i=8),
                                sv(ka)[:, :, g, :], pe_b[:, kind:kind + 1],
                                hidb[:, 256 * g + 1:256 * (g + 1) + 1].rearrange("p (m i) -> p m i", i=8),
                                ALU.add, ALU.add)
                        last.then_inc(*PJ.release(ka))
                        dve.wait_ge(*hid_tanh.at(s))
                        last = ("vc" if kind else "kc", 0) if hb else ("gvc",) if kind else ("gkc",)
                        dve.wait_ge(*PJ.is_full(last))
                        v.scalar_tensor_tensor(hid[kind], hidt, 1.0, hidp, ALU.add, ALU.mult)\
                            .then_inc(*hid_done.inc(s))
                    elif k in ("gkc", "kc"):
                        who = "p" if k == "gkc" else s[1]
                        dve.wait_ge(*PJ.is_used(s))
                        dve.wait_ge(*(roped.at((G_TOK - 1, 2)) if who == "p" else kc_done.at("p" if who == 0 else 0)))
                        if k == "gkc":
                            view = kcp[:, :].rearrange("p (h d) -> p h d", h=KV)
                            last = rope(NCP, view, view, blk_c[0:NCP, :], blk_s[0:NCP, :], [KV])
                        else:
                            view = kcs[:, :].rearrange("p (h d) -> p h d", h=8)
                            last = rope(64, view, view, blk_c[:, :], blk_s[:, :], [8])
                        last.then_inc(*kc_done.inc(who))
                    elif k in ("gkt", "kct"):
                        dve.wait_ge(*TR.is_full(s))
                        if k == "gkt":
                            for g in range(KV):
                                rows = slice(HD * g, HD * (g + 1))
                                last = v.tensor_copy(kcz[rows, g, 0:NCP], tr(s)[rows, 0:NCP])
                        else:
                            last = v.tensor_copy(kcT[s[1]], tr(s)[:, 0:256].rearrange("p (b n) -> p b n", b=RB))
                        last.then_inc(*TR.release(s))
                    elif k == "gates":
                        for hb in range(HB):
                            key = ("gates", hb)
                            dve.wait_ge(*PJ.is_full(key))
                            v.tensor_tensor(sgt.rearrange("p (b h) -> p b h", b=3),
                                            pj(key)[:, 0:24].rearrange("p (b h) -> p b h", b=3),
                                            row_head[:, :].unsqueeze(1).to_broadcast([P, 3, HEADS]), ALU.mult)\
                                .then_inc(*PJ.release(key))
                            dve.wait_ge(*PJ.is_used(key))
                            link(v.reduce_sum(sg[hb], sgt.rearrange("p (b h) -> p b h", b=3), AX.X))
                            link(v.tensor_scalar(sg[hb], sg[hb], 1.0, 0.5, ALU.add, ALU.mult))
                    elif k == "cscore":
                        qt = s[1]
                        dve.wait_ge(*SC.is_full(s))
                        sv = sc(s)[:, 0:256].rearrange("p (h n) -> p h n", h=HEADS)
                        pv = prob[:, 0, 0:256].rearrange("p (h n) -> p h n", h=HEADS)
                        link(v.reduce_max(cmx, sv, AX.X))
                        if qt == 1:
                            dve.wait_ge(*TR.is_full(("cturn", 0)))
                        v.tensor_tensor(pv, sv, cmx.unsqueeze(2).to_broadcast([P, HEADS, 32]), ALU.subtract)\
                            .then_inc(*SC.release(s))
                        dve.wait_ge(*cexpd.at(qt))
                        link(v.reduce_sum(cden, pv, AX.X))
                        link(v.reciprocal(crec, cden))
                        if qt == 0:
                            link(v.tensor_scalar(crec, crec, row_some[:, 0:1], None, ALU.mult))
                        link(v.tensor_scalar(crec, crec, 0.5, None, ALU.mult))
                        link(v.scalar_tensor_tensor(crec, gct[:, qt, 0:8], 1.0, crec, ALU.add, ALU.mult))
                    elif k == "cpv":
                        qt = s[1]
                        key = ("o", "c", qt)
                        dve.wait_ge(*O.is_full(key))
                        v.tensor_tensor(o_tmp[:, :].rearrange("p (h d) -> p h d", h=HEADS),
                                        ob(key)[:, :].rearrange("p (h d) -> p h d", h=HEADS),
                                        crec.unsqueeze(2).to_broadcast([P, HEADS, HD]), ALU.mult)\
                            .then_inc(*O.release(key))
                        dve.wait_ge(*O.is_used(key))
                        v.tensor_tensor(o_sb[:, qt, :], o_sb[:, qt, :], o_tmp[:, :], ALU.add)\
                            .then_inc(*c_normed.inc(("c", qt)))
                    elif k == "sexp":
                        _, hb, what = s
                        i, c0, n, scores = SOFT[what]
                        dve.wait_ge(*SC.is_used(("sscore", hb, scores)))
                        v.tensor_reduce(smx[:, i:i + 1], srow[:, c0:c0 + n], AX.X, ALU.max, negate=True)\
                            .then_inc(*smaxed.inc((hb, what)))
                        dve.wait_ge(*sexpd.at((hb, what)))
                        link(v.reciprocal(srec[:, i:i + 1], sden[:, i:i + 1]))
                        if what == "cmp":
                            v.tensor_scalar(srow[:, c0:c0 + n], srow[:, c0:c0 + n], srec[:, i:i + 1], None, ALU.mult)\
                                .then_inc(*cnormed.inc(hb))
                    elif k == "imp":
                        hb = s[1]
                        dve.wait_ge(*PJ.is_full(s))
                        v.tensor_copy(impt, pj(s)[:, 0:NBLK + 1]).then_inc(*PJ.release(s))
                    elif k == "impsum":
                        hb = s[1]
                        dve.wait_ge(*PJ.is_full(s))
                        v.tensor_copy(impv, pj(s)[:, 0:NBLK]).then_inc(*PJ.release(s))
                        dve.wait_ge(*PJ.is_used(s))
                        link(v.tensor_reduce(least, impv[:, 1:NBLK], AX.X, ALU.min))
                        link(v.tensor_scalar(hitv, impv, least, None, ALU.is_equal))
                        link(v.tensor_tensor(hitv, hitv, number[:, :], ALU.mult))
                        link(v.tensor_reduce(which, hitv[:, 1:NBLK], AX.X, ALU.max))
                        link(v.tensor_scalar(dropv, number[:, :], which, NEG, ALU.is_equal, ALU.mult))
                    elif k == "drop":
                        hb = s[1]
                        dve.wait_ge(*SC.is_used(("sscore", hb, "slc1")))
                        part = srow[:, S_SLC:S_SLC + PAST].rearrange("p (m n) -> p m n", m=NBLK)
                        link(v.tensor_tensor(part, part, dropv.unsqueeze(2).to_broadcast([P, NBLK, SLC]), ALU.add))
                    elif k in ("soA", "soC"):
                        hb = s[1]
                        okey = ("o", "s" + k[-1], hb)
                        dve.wait_ge(*O.is_full(okey))
                        if k == "soA":
                            link(v.tensor_scalar(scoef[:, 0:2], row_kv[:, :], srec[:, 0:1], None, ALU.mult))
                            terms = [(0, scoef[:, 0:1]), (HD, scoef[:, 1:2])]
                            if hb == 0:
                                dve.wait_ge(*TR.is_full(("gateC", 0)))
                            else:
                                dve.wait_ge(*TR.is_full(("sgateC", hb - 1)))
                        else:
                            terms = []
                            for j, (i, b3, c) in enumerate(((2, 2, 0), (3, 1, P), (1, 0, 2 * P))):
                                cc = scoef[:, 2 * j:2 * j + 2]
                                link(v.tensor_scalar(cc, row_kv[:, :], sg[hb][:, b3:b3 + 1],
                                                     srec[:, i:i + 1] if i != 1 else 1.0, ALU.mult, ALU.mult))
                                terms += [(c, cc[:, 0:1]), (c + HD, cc[:, 1:2])]
                            dve.wait_ge(*TR.is_full(("sgateA", hb)))
                        acc = o_sb[:, 0, 0:HD]
                        for j, (c, coef) in enumerate(terms):
                            src = ob(okey)[:, c:c + HD]
                            if j == 0:
                                link(v.tensor_scalar(acc, src, coef, None, ALU.mult))
                            elif j < len(terms) - 1:
                                link(v.scalar_tensor_tensor(acc, src, coef, acc, ALU.mult, ALU.add))
                            else:
                                v.scalar_tensor_tensor(acc, src, coef, acc, ALU.mult, ALU.add)\
                                    .then_inc(*O.release(okey))
                        dve.wait_ge(*O.is_used(okey))
                        v.tensor_copy(o_sb[:, 0, HD:2 * HD], acc).then_inc(*so_done.inc(s))
                    elif k in ("sgateA", "sgateC"):
                        hb = s[1]
                        o_t = oT[0] if k == "sgateA" else oT[2]
                        dve.wait_ge(*TR.is_full(s))
                        for par in range(2):
                            rows = slice(HD * par, HD * (par + 1))
                            src = tr(s)[rows, 0:P].rearrange("p (b c z t) -> p c z b t", b=RB, z=2, t=NEW)[:, :, par, :, :]
                            part = o_t[rows, :, SEQ + 16 * hb:SEQ + 16 * (hb + 1)]
                            part = part.rearrange("p c (b t) -> p c b t", t=NEW)
                            last = v.tensor_tensor(part, src, part, ALU.mult)
                        last.then_inc(*TR.release(s))
                    elif k == "up":
                        _, fh, i, q4 = s
                        gkey = ("gate", fh, i, q4)
                        dve.wait_ge(*PJ.is_used(gkey))
                        dve.wait_ge(*PJ.is_full(s))
                        tn = tanh[:, tanh_slot[gkey], :]
                        ft = 4 * fh + q4
                        dst = mT[:, ft, :] if i == 0 else prod[:, :]
                        v.scalar_tensor_tensor(dst, tn, 1.0, pj(s)[:, 0:T], ALU.add, ALU.mult)\
                            .then_inc(*PJ.release(s))
                        dve.wait_ge(*PJ.is_used(s))
                        if i:
                            last = v.tensor_tensor(mT[:, ft, :], mT[:, ft, :], prod[:, :], ALU.add)
                            if i == 2:
                                link(last)
                                last = split(m_high[ft], m_low[ft], mT[:, ft, :])
                            last.then_inc(*merged.inc(s[1:]))
                            dve.wait_ge(*merged.at(s[1:]))
                    elif k == "down":
                        _, nh, tt = s
                        n = PARTS[tt]
                        if (nh, tt) == (0, 0):
                            dve.wait_ge(*x_back.at("all"))
                        dve.wait_ge(*PJ.is_full(s))
                        part = x[0:n, tt, 512 * nh:512 * (nh + 1)]
                        v.scalar_tensor_tensor(part, pj(s)[0:n, :], 0.25, part, ALU.mult, ALU.add)\
                            .then_inc(*PJ.release(s))


        with nc.Block() as block:
            @block.gpsimd
            def _(pool):
                pool.dma_reset(per_layer)
                pool.sem_clear(per_layer)

    y = paged[0][:, 0:3 * D_MODEL].rearrange("p (t n) -> p t n", t=3)
    last_g = paged[1][:, 0:D_MODEL]
    with nc.Block() as block:
        @block.sync
        def _(sp):
            sp.dma_start(last_g, a["final_g"]).then_inc(y_out, 16)
            for tt in range(3):
                n = PARTS[tt]
                sp.wait_ge(y_ready, tt + 1)
                sp.dma_start(o["y"][TOK0[tt]:TOK0[tt] + n, :], y[0:n, tt, :]).then_inc(y_out, 16)
            sp.wait_ge(y_out, 16 * 4)

        @block.scalar
        def _(act):
            for tt in range(3):
                n = PARTS[tt]
                nc.scalar.activation(y[0:n, tt, :], x[0:n, tt, :], ACT.Square, accum_out=ss[0:n, tt:tt + 1])\
                    .then_inc(y_squares, 1)
                act.wait_ge(y_mean, tt + 1)
                nc.scalar.activation(rn[0:n, tt:tt + 1], ss[0:n, tt:tt + 1], ACT.Sqrt).then_inc(y_root, 1)

        @block.vector
        def _(dve):
            for tt in range(3):
                n = PARTS[tt]
                dve.wait_ge(y_squares, tt + 1)
                nc.vector.tensor_scalar(ss[0:n, tt:tt + 1], ss[0:n, tt:tt + 1], 1.0 / D_MODEL, EPS, ALU.mult, ALU.add)\
                    .then_inc(y_mean, 1)
                dve.wait_ge(y_root, tt + 1)
                nc.vector.reciprocal(rn[0:n, tt:tt + 1], rn[0:n, tt:tt + 1]).then_inc(y_link, 1)
                dve.wait_ge(y_link, 2 * tt + 1)
                nc.vector.tensor_scalar(y[0:n, tt, :], x[0:n, tt, :], rn[0:n, tt:tt + 1], None, ALU.mult)\
                    .then_inc(y_link, 1)
                dve.wait_ge(y_link, 2 * tt + 2)
                if tt == 0:
                    dve.wait_ge(y_out, 16)
                nc.vector.tensor_tensor(y[0:n, tt, :], y[0:n, tt, :], last_g[0:n, :], ALU.mult).then_inc(y_ready, 1)



def constants():
    f = np.float32
    c = {}
    c["ident"] = np.eye(P, dtype=f)
    inv = (np.float32(THETA) ** (-(2.0 / 16) * np.arange(HALF_ROT, dtype=f))).astype(f)

    def rot(pos):
        ang = pos.astype(f)[:, None] * inv[None, :]
        cos, sin = np.cos(ang).astype(f), np.sin(ang).astype(f)
        return np.concatenate([cos, cos], 1), np.concatenate([-sin, sin], 1)

    pos = np.zeros((3, P))
    pos[0], pos[1] = np.arange(P), P + np.arange(P)
    pos[2, 0:NS] = PAST + np.arange(NS) % NEW
    rc, rs = rot(pos.reshape(-1))
    c["rot_c"] = np.ascontiguousarray(rc.reshape(3, P, 16).transpose(1, 0, 2))
    c["rot_s"] = np.ascontiguousarray(rs.reshape(3, P, 16).transpose(1, 0, 2))
    c["blk_c"], c["blk_s"] = rot(CMP_STRIDE * np.arange(64) + CMP_LEN - 1.0)
    cs, ss = CMP_STRIDE * np.arange(64)[:, None], SLC * np.arange(NBLK + 1)[None, :]
    ov = np.clip(np.minimum(cs + CMP_LEN, ss + SLC) - np.maximum(cs, ss), 0, None) / CMP_STRIDE
    ov[NCS:] = 0
    c["overlap"] = ov.astype(f)
    row = np.arange(P)
    rb, rg, rr, rt = row // 32, row // 16 % 2, row // 4 % 4, row % 4
    key = rb * 1000 + rg * 100 + rt
    c["same_q"] = (key[:, None] == key[None, :]).astype(f)
    pick = np.zeros((NS, HB, P), f)
    for hb in range(HB):
        pick[NEW * (RB * hb + rb) + rt, hb, row] = 1
    c["pick"] = pick
    c["row_head"] = (REP * rg + rr == np.arange(HEADS)[:, None]).T.astype(f)
    c["row_kv"] = (rg == np.arange(KV)[:, None]).T.astype(f)
    c["row_some"] = (row >= CMP_LEN - 1).astype(f)[:, None]
    c["n_pads"] = (WIN - row[:, None] - P * np.arange(2)).astype(f)
    c["number"] = np.broadcast_to(np.arange(NBLK, dtype=f), (P, NBLK))
    m = {}
    q, k = row[:, None] + P, np.arange(SEQ)[None, :]
    dist = q - k
    m["a"] = np.concatenate([(dist >= 0) & (dist <= 128), (dist >= 0) & (dist % 4 == 0),
                             (dist >= 0) & (dist % 16 == 0)], 1)
    m["c"] = dist >= 0
    n = np.arange(32)
    for qt in range(2):
        ok = (CMP_STRIDE * n + CMP_LEN - 1 <= row[:, None] + P * qt) & (n < NCP)
        m["cmp%d" % qt] = np.tile(ok, (1, HEADS))
    t = rt[:, None]
    j = np.arange(512)[None, :]
    m["sd4"] = (j % 4 == t)
    m["swin"] = j >= t
    jn = np.arange(NS)[None, :]
    for hb in range(HB):
        mine = jn // NEW == RB * hb + rb[:, None]
        upto, same = mine & (jn % NEW <= t), mine & (jn % NEW == t)
        m["smix%d" % hb] = np.concatenate([np.arange(P)[None, :] >= t, np.arange(K16)[None, :] % 4 == t,
                                           upto, same, same], 1)
        m["smisc%d" % hb] = np.concatenate([upto, upto, np.broadcast_to(np.arange(64) < NCS, (P, 64))], 1)
    at, total = mask_at()
    masks = np.zeros((P, total), f)
    for name, (m0, m1) in at.items():
        masks[:, m0:m1] = np.where(m[name], 0.0, NEG)
    bf = mybir.dt.np(BF16)
    c["masks"], c["identb"] = masks.astype(bf), np.eye(P, dtype=f).astype(bf)
    return {k2: np.ascontiguousarray(v2) for k2, v2 in c.items()}


SPLITS = dict(q_a=3 * WIDTH, k_a=384, v_a=384, z_a=WIDTH, h_b=WIDTH, b_b=WIDTH, c_b=WIDTH, z_b=WIDTH, q_c=WIDTH,
              kv_c=768, g_c=24, z_c=WIDTH, g_merge=3 * D_MODEL)


def tiles(w, n):
    d, kk, cols = w.shape
    return np.ascontiguousarray(w.reshape(d, kk // P, P, cols // n, n).transpose(0, 3, 2, 1, 4)
                                .reshape(d, cols // n, P, kk // P * n))


def layouts(x_prompt, x_sample, cache_dil1_kv, cache_dil4_kv, cache_dil16_kv, cache_win_kv, state_conv, cache_nsa_kv,
            page_table, norm_g, w_in, conv_w, cmp_pe_k, cmp_pe_v, cmp_wk1, cmp_wk2, cmp_wv1, cmp_wv2, w_up_a, w_up_b,
            w_up_c, w_out, final_norm_g):
    A = {}
    D = DEPTH
    A["x"] = np.concatenate([x_prompt.reshape(SEQ, D_MODEL), x_sample.reshape(NS, D_MODEL)])
    at, cols = 0, {}
    for name, n in SPLITS.items():
        cols[name] = w_in[:, :, at:at + n]
        at += n

    def by_rep(w):
        return w.reshape(D, D_MODEL, KV, REP, HD).transpose(0, 1, 3, 2, 4).reshape(D, D_MODEL, WIDTH)

    ka, va = (cols[n].reshape(D, D_MODEL, 3, P) for n in ("k_a", "v_a"))
    kvc = cols["kv_c"].reshape(D, D_MODEL, 6, P)
    pairs = [z[:, :, i] for i in range(3) for z in (ka, va)] + [kvc[:, :, i] for i in (4, 5, 0, 1, 2, 3)]
    tok = [by_rep(cols["q_a"][:, :, WIDTH * i:WIDTH * (i + 1)]) for i in range(3)] + [by_rep(cols["q_c"])] + pairs
    A["w_tok"] = tiles(np.concatenate(tok, 2), 512)
    col = {"h": "h_b", "c": "c_b", "b": "b_b", "zb": "z_b", "za": "z_a", "zc": "z_c"}
    A["w_first"] = np.concatenate([A["w_tok"][:, 0], A["w_tok"][0:1, 0]])
    A["w_feat"] = tiles(np.concatenate([cols[col[k]][:, :, P * t:P * (t + 1)] for k, t in FEATS], 2), 512)
    A["w_gc"] = tiles(cols["g_c"], 24)[:, 0].reshape(D, P, KT, 24)
    g = tiles(cols["g_merge"], 512).reshape(D, 3, 2, P, KT * 512)
    A["w_gate"] = np.ascontiguousarray(g.transpose(0, 2, 1, 3, 4))
    up = np.stack([tiles(w, 512) for w in (w_up_a, w_up_b, w_up_c)], 1)
    A["w_up"] = np.ascontiguousarray(up.transpose(0, 2, 1, 3, 4))
    A["w_out"] = tiles(w_out, 512)
    A["norm_g"] = np.ascontiguousarray(norm_g.reshape(D, KT, P).transpose(0, 2, 1))
    A["final_g"] = np.broadcast_to(final_norm_g, (P, D_MODEL))
    A["conv_w"] = conv_w.reshape(D, 3, WT, P).transpose(0, 3, 2, 1)
    A["conv_state"] = state_conv.reshape(D, REQ, 2, WT, P).transpose(0, 4, 3, 1, 2)
    A["cmp_pe"] = np.stack([p.reshape(D, 16, P).transpose(0, 2, 1) for p in (cmp_pe_k, cmp_pe_v)], 2)
    A["w1"] = np.stack([w.reshape(D, 16, P, P).transpose(0, 2, 1, 3) for w in (cmp_wk1, cmp_wv1)], 2)\
        .reshape(D, P, 4096)
    A["w2"] = np.stack([cmp_wk2, cmp_wv2], 2)
    k4, v4 = cache_dil4_kv[:, :, :, 0], cache_dil4_kv[:, :, :, 1]
    k1, v1 = cache_dil1_kv[:, :, :, 0], cache_dil1_kv[:, :, :, 1]
    near = cache_dil16_kv.reshape(D, REQ, D16 // 16, 16, 2, KV, HD)[:, :, :, 0:NEW].reshape(D, REQ, K16, 2, KV, HD)
    k16, v16 = near[:, :, :, 0], near[:, :, :, 1]
    kw, vw = cache_win_kv[:, :, :, 0], cache_win_kv[:, :, :, 1]

    def keys(*ks):
        z = np.concatenate(ks, 2).reshape(D, HB, RB, -1, P)
        return z.transpose(0, 1, 4, 2, 3)

    def values(*vs):
        z = np.concatenate(vs, 2).reshape(D, HB, RB, -1, P, P)
        return z.transpose(0, 1, 4, 2, 3, 5).reshape(D, HB, P, RB, -1)

    A["k_a"] = keys(k4, k1, k16).reshape(D, HB, P, -1)
    A["v_a"] = values(v4, v1, v16).reshape(D, HB, P, -1)
    A["kv_win"] = np.concatenate([keys(kw), values(vw)], 4).reshape(D, HB, P, -1)
    nph = cache_nsa_kv.shape[1]
    raw = cache_nsa_kv[:, :, :, 0:2].reshape(D, nph, 8, 8, 2, 2, KV, HD).transpose(0, 1, 4, 7, 5, 3, 6, 2)
    raw = raw.reshape(D, nph, P, 2, P)
    ks = cache_nsa_kv[:, :, :, 2].reshape(D, nph, PAGE, P).transpose(0, 1, 3, 2)[:, :, :, None]
    vs = cache_nsa_kv[:, :, :, 3].reshape(D, nph, PAGE, P)[:, :, :, None]
    A["pool"] = np.concatenate([raw, ks, vs], 3)
    A["page_table"] = page_table.reshape(1, REQ * PAGES)
    for n, z in (("dil1", cache_dil1_kv), ("dil4", cache_dil4_kv), ("dil16", cache_dil16_kv), ("win", cache_win_kv)):
        A["cache_" + n] = z.reshape(D, REQ, z.shape[2], 2 * P)
    return A


OUTS = {"y": (T, D_MODEL), "conv_state_out": (DEPTH, P, WT, 2 + 2 * REQ)}
for _n, _w in (("dil1", D1), ("dil4", D4), ("dil16", D16), ("win", WIN)):
    OUTS[f"new_{_n}_prompt"] = (DEPTH, min(_w, SEQ), 2 * P)
    OUTS[f"new_{_n}_sample"] = (DEPTH, REQ, _w, 2 * P)
OUTS["new_nsa_rows_prompt"] = (DEPTH, SEQ, 4 * P)
OUTS["new_nsa_rows_sample"] = (DEPTH, NS, 4 * P)


def kernel(**inputs):
    import concourse.bacc as bacc
    from concourse.bass_utils import run_bass_kernel_spmd

    arrays = layouts(**{k: np.asarray(v) for k, v in inputs.items()})
    arrays.update(constants())
    arrays = {"in_" + k: np.ascontiguousarray(v) for k, v in arrays.items()}
    nc = bacc.Bacc("TRN2", target_bir_lowering=False, num_devices=1)
    a = {k[3:]: nc.dram_tensor(k, v.shape, mybir.dt.from_np(v.dtype), kind="ExternalInput").ap()
         for k, v in arrays.items()}
    o = {k: nc.dram_tensor("out_" + k, shape, FP32, kind="ExternalOutput").ap() for k, shape in OUTS.items()}
    trunk_program(nc, a, o)
    res = run_bass_kernel_spmd(nc, [arrays], core_ids=[0]).results[0]
    r = {k: res["out_" + k] for k in OUTS}
    y = r["y"]
    state = r["conv_state_out"].transpose(0, 3, 2, 1).reshape(DEPTH, 2 + 2 * REQ, WIDTH)
    outs = [y[0:SEQ].reshape(1, SEQ, D_MODEL), y[SEQ:].reshape(REQ, NEW, D_MODEL)]
    for n in ("dil1", "dil4", "dil16", "win"):
        z = r[f"new_{n}_prompt"]
        outs.append(z.reshape(DEPTH, 1, z.shape[1], 2, KV, HD))
        z = r[f"new_{n}_sample"]
        outs.append(z.reshape(DEPTH, REQ, z.shape[2], 2, KV, HD))
    outs.append(np.ascontiguousarray(state[:, 0:2]).reshape(DEPTH, 1, 2, WIDTH))
    outs.append(np.ascontiguousarray(state[:, 2:]).reshape(DEPTH, REQ, 2, WIDTH))
    outs.append(r["new_nsa_rows_prompt"].reshape(DEPTH, 1, SEQ, 4, KV, HD))
    outs.append(r["new_nsa_rows_sample"].reshape(DEPTH, REQ, NEW, 4, KV, HD))
    return tuple(outs)
```
